# Optimizing a Trainium2 kernel written in Bass

```python
import jax, jax.numpy as jnp
from jax import lax
import numpy as np

D_MODEL = 1024
BATCH = 1
SEQ = 128
DEPTH = 2
DEC_BATCH = 1
DEC_SEQ = 512
PAST_LEN = 128

GRID_W = 64
N_HEADS = 8
QK_NOPE = 64
QK_ROPE = 32
V_HEAD = 64
Q_LORA = 384
KV_LORA = 256
C_CONV = 512
CONV_K = 31
CONV_PAD = CONV_K // 2
D_IN = Q_LORA + KV_LORA + QK_ROPE + 2 * C_CONV
D_MIX = N_HEADS * V_HEAD + C_CONV
N_EXPERTS = 16
N_GROUPS = 4
EXPERTS_PER_GROUP = N_EXPERTS // N_GROUPS
TOP_K = 2
D_EXPERT = 256
ROPE_BASE = 10000.0
ROPE_PAIRS = QK_ROPE // 4
Q_BLOCK = 128
EPS = 1e-6
ATTN_SCALE = (QK_NOPE + QK_ROPE) ** -0.5

kernel_name = "hybrid_mla_conformer_moe_diffusion_step"

def rmsnorm(x, g):
    xf = x.astype(jnp.float32)
    y = xf * lax.rsqrt(jnp.mean(xf * xf, axis=-1, keepdims=True) + EPS) * g
    return y.astype(x.dtype)

def layernorm(x, g, b):
    xf = x.astype(jnp.float32)
    mu = jnp.mean(xf, axis=-1, keepdims=True)
    var = jnp.mean(jnp.square(xf - mu), axis=-1, keepdims=True)
    return ((xf - mu) * lax.rsqrt(var + EPS) * g + b).astype(x.dtype)

def ada_params(cvec, w_ada, b_ada):
    m = jax.nn.silu(cvec) @ w_ada + b_ada
    return jnp.split(m[:, None, :], 6, axis=-1)

def axial_rope_tables(n_tokens):
    rows = n_tokens // GRID_W
    row = jnp.repeat(jnp.arange(rows), GRID_W).astype(jnp.float32)
    col = jnp.tile(jnp.arange(GRID_W), rows).astype(jnp.float32)
    freqs = ROPE_BASE ** (-jnp.arange(ROPE_PAIRS, dtype=jnp.float32) / ROPE_PAIRS)
    ang = jnp.stack([row[:, None] * freqs, col[:, None] * freqs], axis=1)
    return jnp.cos(ang), jnp.sin(ang)

def apply_axial_rope(x, cos, sin):
    xr = x.reshape(x.shape[:-1] + (2, 2, ROPE_PAIRS))
    x1, x2 = xr[..., 0, :], xr[..., 1, :]
    cos = cos.astype(x.dtype)
    sin = sin.astype(x.dtype)
    out = jnp.stack([x1 * cos - x2 * sin, x2 * cos + x1 * sin], axis=-2)
    return out.reshape(x.shape)

def expand_kv(ckv, w_ukv):
    b, s, _ = ckv.shape
    kv = (ckv @ w_ukv).reshape(b, s, N_HEADS, QK_NOPE + V_HEAD)
    return kv[..., :QK_NOPE], kv[..., QK_NOPE:]

def mla_attend(q_nope, q_rope, k_nope, k_rope, v):
    b, t, h, _ = q_nope.shape
    nb = t // Q_BLOCK

    def blocks(a):
        return jnp.moveaxis(a.reshape((b, nb, Q_BLOCK) + a.shape[2:]), 1, 0)

    def attend_block(qs):
        qn, qr = qs
        s = jnp.einsum("bqhd,bkhd->bhqk", qn, k_nope) + jnp.einsum("bqhr,bkr->bhqk", qr, k_rope)
        p = jax.nn.softmax(s.astype(jnp.float32) * ATTN_SCALE, axis=-1).astype(v.dtype)
        return jnp.einsum("bhqk,bkhd->bqhd", p, v)

    o = lax.map(attend_block, (blocks(q_nope), blocks(q_rope)))
    return jnp.moveaxis(o, 0, 1).reshape(b, t, h * V_HEAD)

def conv_module(u, conv_w, conv_b, ln_g, ln_b):
    a, gate = jnp.split(u, 2, axis=-1)
    z = a * jax.nn.sigmoid(gate)
    z = lax.conv_general_dilated(z, conv_w[:, None, :], (1,), [(CONV_PAD, CONV_PAD)],
                                 dimension_numbers=("NWC", "WIO", "NWC"),
                                 feature_group_count=C_CONV) + conv_b
    return jax.nn.silu(layernorm(z, ln_g, ln_b))

def grouped_moe(h, router_w, router_b, w_gate, w_up, w_down):
    b, t, d = h.shape
    xt = h.reshape(b * t, d)
    aff = jax.nn.sigmoid((xt @ router_w).astype(jnp.float32))
    sel = aff + router_b.astype(jnp.float32)
    grp_score = lax.top_k(sel.reshape(-1, N_GROUPS, EXPERTS_PER_GROUP), TOP_K)[0].sum(-1)
    g_idx = jnp.argmax(grp_score, axis=-1)
    in_group = (jnp.arange(N_EXPERTS) // EXPERTS_PER_GROUP)[None, :] == g_idx[:, None]
    _, top_idx = lax.top_k(jnp.where(in_group, sel, -jnp.inf), TOP_K)
    top_aff = jnp.take_along_axis(aff, top_idx, axis=-1)
    wts = top_aff / jnp.sum(top_aff, axis=-1, keepdims=True)
    gates = jnp.sum(jax.nn.one_hot(top_idx, N_EXPERTS, dtype=jnp.float32) * wts[..., None], axis=1).astype(h.dtype)
    hid = jax.nn.silu(jnp.einsum("nd,edf->nef", xt, w_gate)) * jnp.einsum("nd,edf->nef", xt, w_up)
    out = jnp.einsum("nef,efd->nd", hid * gates[..., None], w_down)
    return out.reshape(b, t, d)

def trunk_layer(x, cvec, p, router_w, router_b, rope=None, ctx_ckv=None, ctx_krope=None):
    b, t, _ = x.shape
    sh1, sc1, g1, sh2, sc2, g2 = ada_params(cvec, p["w_ada"], p["b_ada"])
    h = rmsnorm(x, p["norm1_g"]) * (1 + sc1) + sh1
    proj = h @ p["w_in"]
    q_c, kv_c, k_rope, conv_in = jnp.split(proj, [Q_LORA, Q_LORA + KV_LORA, Q_LORA + KV_LORA + QK_ROPE], axis=-1)
    q = (rmsnorm(q_c, p["q_norm_g"]) @ p["w_uq"]).reshape(b, t, N_HEADS, QK_NOPE + QK_ROPE)
    q_nope, q_rope = q[..., :QK_NOPE], q[..., QK_NOPE:]
    ckv = rmsnorm(kv_c, p["kv_norm_g"])
    k_nope, v = expand_kv(ckv, p["w_ukv"])
    if ctx_ckv is None:
        attn = mla_attend(q_nope, q_rope, k_nope, k_rope, v)
    else:
        cos, sin = rope
        q_rope = apply_axial_rope(q_rope, cos[:, None], sin[:, None])
        k_rope_lat = apply_axial_rope(k_rope, cos, sin)
        ck_nope, cv = expand_kv(ctx_ckv, p["w_ukv"])
        attn = mla_attend(q_nope, q_rope,
                          jnp.concatenate([k_nope, ck_nope], axis=1),
                          jnp.concatenate([k_rope_lat, ctx_krope], axis=1),
                          jnp.concatenate([v, cv], axis=1))
    conv = conv_module(conv_in, p["conv_w"], p["conv_b"], p["conv_ln_g"], p["conv_ln_b"])
    x = x + g1 * (jnp.concatenate([attn, conv], axis=-1) @ p["w_out"])
    h2 = rmsnorm(x, p["norm2_g"]) * (1 + sc2) + sh2
    x = x + g2 * grouped_moe(h2, router_w, router_b, p["w_gate"], p["w_up"], p["w_down"])
    return x, ckv, k_rope

def setup_inputs(seed: int = 0) -> dict:
    key = jax.random.key(seed)
    ks = jax.random.split(key, 28)

    def nrm(k, shape, s):
        return jax.random.normal(k, shape, jnp.float32) * s

    return {
        "x_prompt": nrm(ks[0], (BATCH, SEQ, D_MODEL), 1.0),
        "x_sample": nrm(ks[1], (DEC_BATCH, DEC_SEQ, D_MODEL), 1.0),
        "cache_ckv": nrm(ks[2], (DEC_BATCH, DEPTH, PAST_LEN, KV_LORA), 1.0),
        "cache_krope": nrm(ks[3], (DEC_BATCH, DEPTH, PAST_LEN, QK_ROPE), 1.0),
        "c": nrm(ks[4], (DEC_BATCH, D_MODEL), 1.0),
        "c_ctx": nrm(ks[5], (D_MODEL,), 1.0),
        "w_ada": nrm(ks[6], (DEPTH, D_MODEL, 6 * D_MODEL), 0.5 * D_MODEL ** -0.5),
        "b_ada": nrm(ks[7], (DEPTH, 6 * D_MODEL), 0.01),
        "norm1_g": 1.0 + nrm(ks[8], (DEPTH, D_MODEL), 0.05),
        "w_in": nrm(ks[9], (DEPTH, D_MODEL, D_IN), D_MODEL ** -0.5),
        "q_norm_g": 1.0 + nrm(ks[10], (DEPTH, Q_LORA), 0.05),
        "w_uq": nrm(ks[11], (DEPTH, Q_LORA, N_HEADS * (QK_NOPE + QK_ROPE)), Q_LORA ** -0.5),
        "kv_norm_g": 1.0 + nrm(ks[12], (DEPTH, KV_LORA), 0.05),
        "w_ukv": nrm(ks[13], (DEPTH, KV_LORA, N_HEADS * (QK_NOPE + V_HEAD)), KV_LORA ** -0.5),
        "conv_w": nrm(ks[14], (DEPTH, CONV_K, C_CONV), CONV_K ** -0.5),
        "conv_b": nrm(ks[15], (DEPTH, C_CONV), 0.01),
        "conv_ln_g": 1.0 + nrm(ks[16], (DEPTH, C_CONV), 0.05),
        "conv_ln_b": nrm(ks[17], (DEPTH, C_CONV), 0.01),
        "w_out": nrm(ks[18], (DEPTH, D_MIX, D_MODEL), D_MIX ** -0.5),
        "norm2_g": 1.0 + nrm(ks[19], (DEPTH, D_MODEL), 0.05),
        "router_w": nrm(ks[20], (D_MODEL, N_EXPERTS), D_MODEL ** -0.5),
        "router_b": nrm(ks[21], (N_EXPERTS,), 0.01),
        "w_gate": nrm(ks[22], (DEPTH, N_EXPERTS, D_MODEL, D_EXPERT), D_MODEL ** -0.5),
        "w_up": nrm(ks[23], (DEPTH, N_EXPERTS, D_MODEL, D_EXPERT), D_MODEL ** -0.5),
        "w_down": nrm(ks[24], (DEPTH, N_EXPERTS, D_EXPERT, D_MODEL), D_EXPERT ** -0.5),
        "final_g": 1.0 + nrm(ks[25], (D_MODEL,), 0.05),
    }

def reference(x_prompt, x_sample, cache_ckv, cache_krope, c, c_ctx, w_ada, b_ada, norm1_g, w_in,
              q_norm_g, w_uq, kv_norm_g, w_ukv, conv_w, conv_b, conv_ln_g, conv_ln_b, w_out,
              norm2_g, router_w, router_b, w_gate, w_up, w_down, final_g):
    def layer(l):
        return {"w_ada": w_ada[l], "b_ada": b_ada[l], "norm1_g": norm1_g[l], "w_in": w_in[l],
                "q_norm_g": q_norm_g[l], "w_uq": w_uq[l], "kv_norm_g": kv_norm_g[l], "w_ukv": w_ukv[l],
                "conv_w": conv_w[l], "conv_b": conv_b[l], "conv_ln_g": conv_ln_g[l], "conv_ln_b": conv_ln_b[l],
                "w_out": w_out[l], "norm2_g": norm2_g[l], "w_gate": w_gate[l], "w_up": w_up[l],
                "w_down": w_down[l]}

    xp = x_prompt
    cctx = c_ctx[None, :]
    ckv_list, krope_list = [], []
    for l in range(DEPTH):
        xp, ckv, krope = trunk_layer(xp, cctx, layer(l), router_w, router_b)
        ckv_list.append(ckv)
        krope_list.append(krope)
    y_prompt = rmsnorm(xp, final_g)
    new_ckv = jnp.stack(ckv_list, axis=1)
    new_krope = jnp.stack(krope_list, axis=1)

    rope = axial_rope_tables(x_sample.shape[1])
    xs = x_sample
    for l in range(DEPTH):
        xs, _, _ = trunk_layer(xs, c, layer(l), router_w, router_b, rope, cache_ckv[:, l], cache_krope[:, l])
    y_sample = rmsnorm(xs, final_g)
    return (y_prompt, y_sample, new_ckv, new_krope)


_drawn_inputs = setup_inputs


def setup_inputs(seed=0):
    import zlib

    import numpy as np

    out = dict(_drawn_inputs(seed))
    spreads = {}
    factors = {'cache_ckv': 2.904,
     'cache_krope': 3.402,
     'q_norm_g': 8.0,
     'conv_b': 4.835,
     'conv_ln_b': 7.557}
    for name, (base, spread) in spreads.items():
        noise = np.random.default_rng([zlib.crc32(name.encode()), seed]).standard_normal(out[name].shape)
        drawn = base * np.exp(spread * noise) if base else spread * noise
        out[name] = __import__('jax').numpy.asarray(drawn.astype(out[name].dtype))
    for name, factor in factors.items():
        out[name] = (out[name] * factor).astype(out[name].dtype)
    return out
```

```python
from contextlib import ExitStack

import numpy as np

import concourse.bass as bass
from concourse import mybir

FP32 = mybir.dt.float32
INT32 = mybir.dt.int32
ALU = mybir.AluOpType
ACT = mybir.ActivationFunctionType
AXIS_X = mybir.AxisListType.X

P = 128
D = 1024
DK = D // P
DEPTH = 2
SEQ, DEC_SEQ, PAST = 128, 512, 128
GRID_W = 64
TILES = (DEC_SEQ + SEQ) // P
LAT = DEC_SEQ // P
TOK = TILES * P
HEADS, NOPE, ROPE, VH = 8, 64, 32, 64
Q_LORA, KV_LORA, CONV_C, CONV_K = 384, 256, 512, 31
QC, KC, CC = Q_LORA // P, KV_LORA // P, CONV_C // P
PAD = CONV_K // 2
QKV = Q_LORA + KV_LORA + ROPE
D_IN = QKV + 2 * CONV_C
KEYS = TOK + PAST
LAT_KEYS = DEC_SEQ + PAST
EXPERTS, GROUPS, PER_GROUP, FF = 16, 4, 4, 256
PAIRS = ROPE // 4
EPS = 1e-6
SCALE = (NOPE + ROPE) ** -0.5
MAX_BLOCKS = 2 * TOK // P + EXPERTS - 1
NO_ROW = 1 << 20
BIG = 1e30
ADA_CHUNKS = 6 * D // 512
ZPAD = 3 * PAD + TOK
CONV_OUT = TOK + PAD
UNITS = HEADS * TILES
VEC_ROWS = 48 + 8 + 8 + QC + 3 * CC
(V_BADA, V_G1, V_G2, V_QG, V_CB, V_LG, V_LB) = (0, 48, 56, 64, 64 + QC, 64 + QC + CC, 64 + QC + 2 * CC)

C_ID, C_TRI, C_ONE, C_TAB = 0, 128, 256, 384
C_KC = C_TAB + TOK
C_KS = C_KC + LAT * ROPE
C_W16 = C_KS + LAT * ROPE
C_W4 = C_W16 + EXPERTS
C_TOKID = C_W4 + GROUPS
N_CONST = C_TOKID + TILES


def shape_constants():
    c = np.zeros((P, N_CONST), np.float32)
    p = np.arange(P)
    c[:, C_ID:C_ID + P] = np.eye(P)
    c[:, C_TRI:C_TRI + P] = p[:, None] < p[None, :]
    c[:, C_ONE:C_ONE + P] = 1.0
    tok = np.arange(DEC_SEQ)
    freqs = (np.float32(10000.0) ** (-np.arange(PAIRS, dtype=np.float32) / PAIRS)).astype(np.float32)
    pos = np.stack([tok // GRID_W, tok % GRID_W], 1).astype(np.float32)
    ang = pos[:, :, None] * freqs
    cos, sin = np.cos(ang).astype(np.float32), np.sin(ang).astype(np.float32)
    cos_r = np.stack([cos, cos], 2).reshape(DEC_SEQ, ROPE)
    sin_r = np.stack([-sin, sin], 2).reshape(DEC_SEQ, ROPE)
    tab = c[:, C_TAB:C_TAB + TOK]
    tab[0:NOPE + ROPE] = 1.0
    tab[NOPE:NOPE + ROPE, 0:DEC_SEQ] = cos_r.T
    tab[NOPE + ROPE:P, 0:DEC_SEQ] = sin_r.T
    c[:, C_KC:C_KC + LAT * ROPE] = cos_r.reshape(LAT, P, ROPE).transpose(1, 0, 2).reshape(P, -1)
    c[:, C_KS:C_KS + LAT * ROPE] = sin_r.reshape(LAT, P, ROPE).transpose(1, 0, 2).reshape(P, -1)
    c[:, C_W16:C_W16 + EXPERTS] = EXPERTS - np.arange(EXPERTS)
    c[:, C_W4:C_W4 + GROUPS] = GROUPS - np.arange(GROUPS)
    c[:, C_TOKID:C_TOKID + TILES] = p[:, None] + P * np.arange(TILES)
    return c


class Ring:

    def __init__(self, banks, full, empty):
        self.banks, self.full, self.empty, self.number, self.order = banks, full, empty, {}, []

    def plan(self, *keys):
        for key in keys:
            self.number[key] = len(self.order)
            self.order.append(key)

    def bank(self, key):
        return self.banks[self.number[key] % len(self.banks)]

    def open(self, pe, key):
        before = self.number[key] - len(self.banks)
        if before >= 0:
            pe.wait_ge(self.empty, before + 1)
        return self.bank(key)

    def take(self, eng, key):
        eng.wait_ge(self.full, self.number[key] + 1)
        return self.bank(key)

    def wait_full(self, eng, key):
        eng.wait_ge(self.full, self.number[key] + 1)

    def wait_empty(self, eng, key):
        eng.wait_ge(self.empty, self.number[key] + 1)


def hybrid_step_kernel(nc, x_prompt, x_sample, cache_ckv, cache_krope, c, c_ctx, w_ada, b_ada, norm1_g, w_in,
                       q_norm_g, w_uq, kv_norm_g, w_ukv, conv_w, conv_b, conv_ln_g, conv_ln_b, w_out,
                       norm2_g, router_w, router_b, w_gate, w_up, w_down, final_g, consts,
                       y_prompt, y_sample, new_ckv, new_krope):
    ctx = ExitStack()
    with ctx:
        def sb(name, cols, dt=FP32, parts=P):
            return ctx.enter_context(nc.sbuf_tensor(name, [parts, cols], dt))

        def sem(name):
            return ctx.enter_context(nc.semaphore(name))

        h2_dram = nc.dram_tensor("h2_rows", [TOK, D], FP32, kind="Internal").ap()
        y_dram = nc.dram_tensor("expert_rows", [2 * TOK, D], FP32, kind="Internal").ap()
        tables = [nc.dram_tensor(f"slot_table{l}", [(MAX_BLOCKS + 1) * P, 3], INT32, kind="Internal").ap() for l in range(DEPTH)]

        con = sb("con", N_CONST)
        ident, tri, ones = con[:, C_ID:C_ID + P], con[:, C_TRI:C_TRI + P], con[:, C_ONE:C_ONE + P]
        vec_rows = sb("vec_rows", 2 * P)
        vecs = sb("vecs", 2 * P)
        cond = sb("cond", 2 * DK)
        cond_raw = sb("cond_raw", 2 * DK)
        adat = sb("adat", 96)
        mod = sb("mod", 32)
        kvg = sb("kvg", KV_LORA)
        rw = sb("rw", DK * EXPERTS)
        rb = sb("rb", EXPERTS)
        eps_t = sb("eps_t", 1)
        stat = sb("stat", 64)
        idx = sb("idx", 2 * TILES, INT32)
        slot_src = sb("slot_src", 6 * TILES, INT32)
        slot_tab = sb("slot_tab", 3, INT32)
        gate_col = sb("gate_col", 1)
        row_next, row_work, row_out = sb("row_next", 1, INT32), sb("row_work", 1, INT32), sb("row_out", 1, INT32)
        no_rows = sb("no_rows", 3 * (MAX_BLOCKS + 1), INT32)
        blocks = [sb(f"blocks{l}", 2 * EXPERTS + 1, INT32) for l in range(DEPTH)]
        nbf = sb("nbf", 5 * 24)
        block_total = sb("block_total", 1)
        att_stat = sb("att_stat", 4 * UNITS)

        x = sb("x", TILES * D)[:, :].rearrange("p (t d) -> p t d", t=TILES)
        W1 = sb("region_weights", DK * D_IN)
        H = sb("region_h", TILES * D)
        Q = sb("region_q", TILES * D)
        O = sb("region_o", 8576)
        BC = sb("region_bc", 6 * D)
        PR = sb("region_proj", TILES * QKV)
        CV = sb("region_conv", 3 * D)

        hT = H[:, 0:DK * TOK].rearrange("p (k t) -> p k t", k=DK)
        mixT = hT
        xn = Q[:, :].rearrange("p (t d) -> p t d", t=TILES)
        qT = Q[:, :].rearrange("p (h t) -> p h t", h=HEADS)
        h2T = Q[:, :].rearrange("p (k t) -> p k t", k=DK)
        win = W1[:, :].rearrange("p (k n) -> p k n", k=DK)
        kT = W1[:, 0:HEADS * KEYS].rearrange("p (h t) -> p h t", h=HEADS)
        base = HEADS * KEYS
        v_sb = W1[:, base:base + 6 * 512].rearrange("p (t n) -> p t n", t=6)
        base += 6 * 512
        prob = W1[:, base:base + 2 * LAT_KEYS].rearrange("p (b n) -> p b n", b=2)
        base += 2 * LAT_KEYS
        probT = W1[:, base:base + 2 * LAT_KEYS].rearrange("p (b n) -> p b n", b=2)
        base += 2 * LAT_KEYS
        kr = W1[:, base:base + 6 * P].rearrange("p (t n) -> p t n", t=6)
        base += 6 * P
        cache_sb = W1[:, base:base + KV_LORA + ROPE]
        assert base + KV_LORA + ROPE <= DK * D_IN
        EW = DK * 512 + 2 * D
        wgu = [W1[:, s * EW:s * EW + DK * 512].rearrange("p (k n) -> p k n", k=DK) for s in range(2)]
        wdn = [W1[:, s * EW + DK * 512:(s + 1) * EW].rearrange("p (k n) -> p k n", k=2) for s in range(2)]
        ada_w = [O[:, s * 4096:(s + 1) * 4096].rearrange("p (k n) -> p k n", k=DK) for s in range(2)]
        wuq = O[:, 0:3072].rearrange("p (k h n) -> p k h n", k=QC, h=HEADS)
        wk = O[:, 3072:4096].rearrange("p (k n) -> p k n", k=KC)
        wv = O[:, 4096:5120].rearrange("p (k n) -> p k n", k=KC)
        qcT = O[:, 5120:5120 + QC * TOK].rearrange("p (k t) -> p k t", k=QC)
        ckvT = O[:, 7040:7040 + KC * KEYS].rearrange("p (k t) -> p k t", k=KC)
        wout = O[:, 0:8192].rearrange("p (k n) -> p k n", k=DK)
        proj = PR[:, :].rearrange("p (t n) -> p t n", t=TILES)
        o_tok = PR[:, 0:TILES * 512].rearrange("p (t n) -> p t n", t=TILES)
        y_sb, hid = PR[:, 0:1024], PR[:, 1024:1280]
        hidT = PR[:, 1280:1536].rearrange("p (k n) -> p k n", k=2)
        silu_g = PR[:, 1536:1792]
        zpad = CV[:, 0:CC * ZPAD].rearrange("p (k n) -> p k n", k=CC)
        diag = CV[:, 0:1024].rearrange("p (b n) -> p b n", b=2)
        h2s = CV[:, 0:2048].rearrange("p (b n) -> p b n", b=2)
        res_tmp = CV[:, 2048:3072]
        xg = CV[:, 0:1024]
        xgT = CV[:, 1024:2048].rearrange("p (k n) -> p k n", k=DK)
        acc = BC[:, 0:CC * CONV_OUT].rearrange("p (k n) -> p k n", k=CC)
        sig = BC[:, 2 * D + 1024:2 * D + 1024 + 2 * TOK].rearrange("p (b n) -> p b n", b=2)
        junk = BC[:, 5 * D:6 * D]
        junk2 = PR[:, 2048:3072]
        ada_row = H[:, 4096:5120]
        bc = BC[:, :].rearrange("p (i n) -> p i n", i=6)
        g1_bc, a2_bc, sh2_bc = (lambda v: bc[:, v]), (lambda v: bc[:, 2 + v]), (lambda v: bc[:, 4 + v])
        g2_bc = g1_bc
        zsq = Q[:, 0:CC * CONV_OUT].rearrange("p (k n) -> p k n", k=CC)
        ln_rstd = Q[:, CC * CONV_OUT:CC * CONV_OUT + CONV_OUT]
        comb = [H[:, n * D:(n + 1) * D] for n in range(4)] + [CV[:, n * D:(n + 1) * D] for n in range(3)] \
            + [PR[:, n * D:(n + 1) * D] for n in range(3)]
        r_tmp = H[:, 4096:5120]
        final_bc = bc[:, 2]

        ps = ctx.enter_context(nc.psum_tensor("ps", [P, 8, 512], FP32))
        flat = ps[:, :, :].rearrange("p b n -> p (b n)")

        ring_a = Ring([ps[:, b] for b in range(4)], sem("act_bank_full"), sem("act_bank_empty"))
        ring_v = Ring([ps[:, b] for b in range(4, 8)], sem("dve_bank_full"), sem("dve_bank_empty"))
        x_loaded, const_loaded, rows_loaded = sem("x_loaded"), sem("const_loaded"), sem("rows_loaded")
        cond_loaded = sem("cond_loaded")
        kvg_loaded, final_loaded = sem("kvg_loaded"), sem("final_loaded")
        ada_loaded = [sem(f"ada_loaded{s}") for s in range(2)]
        win_conv_loaded, win_qkv_loaded = sem("win_conv_loaded"), sem("win_qkv_loaded")
        wuq_loaded, wukv_loaded, cache_loaded = sem("wuq_loaded"), sem("wukv_loaded"), sem("cache_loaded")
        wout_loaded = sem("wout_loaded")
        expert_loaded = [sem(f"expert_loaded{s}") for s in range(2)]
        act_step, dve_step, pool_step = sem("act_step"), sem("dve_step"), sem("pool_step")
        cond_ready, mod_ready = sem("cond_ready"), sem("mod_ready")
        rms_stat, xn_ready, zero_ready = sem("rms_stat"), sem("xn_ready"), sem("pad_zeroed")
        sig_ready, qkv_stat, qkv_normed = sem("sig_ready"), sem("qkv_stat"), sem("qkv_normed")
        krope_ready, wuq_swapped, k_spread = sem("krope_ready"), sem("wuq_swapped"), sem("k_spread")
        scores, att_max, att_exp = sem("scores"), sem("att_max"), sem("att_exp")
        prob_turned, probT_ready, att_out, att_out_empty = (
            sem("prob_turned"), sem("probT_ready"), sem("att_out"), sem("att_out_empty"))
        conv_step, ln_centred, ln_squared, ln_sqrt, ln_done, conv_silu = (
            sem("conv_step"), sem("ln_centred"), sem("ln_squared"), sem("ln_sqrt"), sem("ln_done"),
            sem("conv_silu"))
        diag_ready = sem("diag_ready")
        x_updated, h2_stat, h2_ready, h2_stored = sem("x_updated"), sem("h2_stat"), sem("h2_ready"), [sem("h2_stored0"), sem("h2_stored1")]
        masks_ready, slots_ready, plan_ready = sem("masks_ready"), sem("slots_ready"), sem("plan_ready")
        table_cleared, table_written = sem("table_cleared"), sem("table_written")
        tab_loaded, gathered, gate_copied, row_moved = sem("tab_loaded"), sem("gathered"), sem("gate_copied"), sem("row_moved")
        xT_full, xT_act, xT_dve = sem("xT_full"), sem("xT_act"), sem("xT_dve")
        gu_full, silu_ready, hid_ready = sem("gu_full"), sem("silu_ready"), sem("hid_ready")
        hidT_full, hidT_ready = sem("hidT_full"), sem("hidT_ready")
        y_full, y_act, y_dve, y_stored = sem("y_full"), sem("y_act"), sem("y_dve"), sem("y_stored")
        comb_loaded, comb_added = [sem(f"comb_loaded{t}") for t in range(TILES)], sem("comb_added")
        pool_passed, pe_passed, act_passed = sem("pool_passed"), sem("pe_passed"), sem("act_passed")
        outputs_done, final_ready = sem("outputs_done"), sem("final_ready")
        ckv_out = sem("ckv_out")

        for l in range(DEPTH):
            if l == 0:
                ring_v.plan("cond")
            ring_v.plan((l, "vec"))
            for ch in range(ADA_CHUNKS):
                ring_a.plan((l, "ada", ch))
                ring_v.plan((l, "adaT", ch))
            for k in range(DK):
                (ring_v if k % 2 else ring_a).plan((l, "xnT", k))
            ring_a.plan((l, "xpT", 0))
            ring_v.plan((l, "xpT", 1))
            for ct in range(CC):
                ring_a.plan((l, "gate_lat", ct), (l, "gate_ctx", ct))
                ring_v.plan((l, "a_lat", ct), (l, "a_ctx", ct))
            for t in range(TILES):
                ring_a.plan((l, "qkv0", t))
                ring_v.plan((l, "qkv1", t))
            ring_a.plan(*[(l, "qcT", k) for k in range(QC)], (l, "qcT_ctx"))
            ring_v.plan(*[(l, "ckvT", k) for k in range(KC)], *[(l, "ckvT_rest", k) for k in range(KC)],
                        (l, "krT", 0), (l, "krT", 1))
            ring_v.plan(*[(l, "q", h) for h in range(HEADS)], (l, "q_ctx", 0), (l, "q_ctx", 1))
            for pr in range(HEADS // 2):
                ring_a.plan((l, "k0", pr), (l, "k1", pr))
            ring_a.plan(*[(l, "v", t) for t in range(6)])
            ring_a.plan(*[(l, "oT", k) for k in range(4)], (l, "oT_ctx"))
            ring_v.plan(*[(l, "ln", s, j) for s in range(2) for j in range(2)])
            ring_v.plan(*[(l, "bc", i, j) for i in range(6) for j in range(2)])
            for t in range(TILES):
                ring_v.plan((l, "wo", t, 0), (l, "wo", t, 1))
                ring_a.plan((l, "h2T", t, 0), (l, "h2T", t, 1))
            ring_a.plan((l, "logits"))
            ring_v.plan((l, "g2", 0, 0), (l, "g2", 0, 1), (l, "g2", 1, 0), (l, "g2", 1, 1))
            ring_v.plan((l, "slots"))

        def sb_v(v):
            return vecs[:, v:v + 1]

        def stores_of(l, t, parity):
            return l * ((TILES + 1 - parity) // 2) + (t + 1 - parity) // 2

        def slot_of_diag(l, n):
            if n < 0:
                return (l - 1, "g2", (n + 4) // 2, n % 2)
            return (l, "bc", n // 2, n % 2) if n < 12 else (l, "g2", (n - 12) // 2, n % 2)

        block = ctx.enter_context(nc.Block())

        @block.sync
        def _(sp):
            sp.dma_start(con[:, :], consts).then_inc(const_loaded, 16)
            sp.dma_start(vec_rows[0:DK, P:2 * P], c[0, :].rearrange("(k q) -> k q", q=P)).then_inc(cond_loaded, 16)
            sp.dma_start(vec_rows[DK:2 * DK, P:2 * P], c_ctx.rearrange("(k q) -> k q", q=P)).then_inc(cond_loaded, 16)
            wgu_dram = [w.rearrange("l e (k p) n -> l e p k n", p=P) for w in (w_gate, w_up)]
            wdn_dram = w_down.rearrange("l e (k p) n -> l e p k n", p=P)

            def load_expert(l, e, s):
                for j, w in enumerate(wgu_dram):
                    sp.dma_start(wgu[s][:, :, j * FF:(j + 1) * FF], w[l, e]).then_inc(expert_loaded[s], 16)
                sp.dma_start(wdn[s], wdn_dram[l, e]).then_inc(expert_loaded[s], 16)

            for l in range(DEPTH):
                if l == 0:
                    ring_v.wait_full(sp, "cond")
                else:
                    ring_v.wait_full(sp, (l - 1, "vec"))
                at = 0
                for vec in (b_ada, norm1_g, norm2_g, q_norm_g, conv_b, conv_ln_g, conv_ln_b):
                    n = vec.shape[1] // P
                    sp.dma_start(vec_rows[at:at + n, 0:P], vec[l].rearrange("(k q) -> k q", q=P)).then_inc(rows_loaded, 16)
                    at += n
                sp.dma_start(vec_rows[0:CONV_K * CC, P:2 * P], conv_w[l].rearrange("j (k q) -> (j k) q", q=P)).then_inc(rows_loaded, 16)
                if l >= 1:
                    sp.wait_ge(qkv_normed, TILES * l)
                sp.dma_start(kvg[:, :], kv_norm_g[l:l + 1, :].broadcast_to([P, KV_LORA])).then_inc(kvg_loaded, 16)
                if l >= 1:
                    ring_v.wait_full(sp, (l - 1, "wo", TILES - 1, 1))
                for ch in range(ADA_CHUNKS):
                    if ch >= 2:
                        ring_a.wait_full(sp, (l, "ada", ch - 2))
                    sp.dma_start(ada_w[ch % 2], w_ada[l].rearrange("(k p) n -> p k n", p=P)[:, :, ch * 512:(ch + 1) * 512]).then_inc(ada_loaded[ch % 2], 16)
                    if l == 0 and ch == 1:
                        sp.dma_start(x[:, 0:LAT, :], x_sample[0].rearrange("(t p) d -> p t d", p=P)).then_inc(x_loaded, 16)
                        sp.dma_start(x[:, LAT, :], x_prompt[0]).then_inc(x_loaded, 16)
                        sp.dma_start(rw[:, :].rearrange("p (k n) -> p k n", k=DK), router_w.rearrange("(k p) n -> p k n", p=P)).then_inc(x_loaded, 16)
                        sp.dma_start(rb[:, :], router_b.rearrange("(a n) -> a n", a=1).broadcast_to([P, EXPERTS])).then_inc(x_loaded, 16)
                if l >= 1:
                    last = sp.value_load(blocks[l - 1][0:1, 2 * EXPERTS - 1:2 * EXPERTS], min_val=0, max_val=100)
                    n_last = sp.value_load(blocks[l - 1][0:1, EXPERTS - 1:EXPERTS], min_val=1, max_val=5)
                    sp.wait_ge(y_full, last + n_last)
                win_dram = w_in[l].rearrange("(k p) n -> p k n", p=P)
                sp.dma_start(win[:, :, QKV:D_IN], win_dram[:, :, QKV:D_IN]).then_inc(win_conv_loaded, 16)
                sp.dma_start(win[:, :, 0:QKV], win_dram[:, :, 0:QKV]).then_inc(win_qkv_loaded, 16)
                ring_a.wait_full(sp, (l, "ada", ADA_CHUNKS - 1))
                for k in range(QC):
                    sp.dma_start(wuq[:, k, :, 0:NOPE + ROPE], w_uq[l, k * P:(k + 1) * P, :].rearrange("p (h n) -> p h n", h=HEADS)).then_inc(wuq_loaded, 16)
                for k in range(KC):
                    src = w_ukv[l, k * P:(k + 1) * P, :].rearrange("p (h n) -> p h n", h=HEADS)
                    sp.dma_start(wk[:, k, :].rearrange("p (h n) -> p h n", h=HEADS), src[:, :, 0:NOPE]).then_inc(wukv_loaded, 16)
                    sp.dma_start(wv[:, k, :].rearrange("p (h n) -> p h n", h=HEADS), src[:, :, NOPE:NOPE + VH]).then_inc(wukv_loaded, 16)
                ring_v.wait_full(sp, (l, "qkv1", TILES - 1))
                sp.dma_start(cache_sb[:, 0:KV_LORA], cache_ckv[0, l]).then_inc(cache_loaded, 16)
                sp.dma_start(cache_sb[:, KV_LORA:KV_LORA + ROPE], cache_krope[0, l]).then_inc(cache_loaded, 16)
                ring_a.wait_full(sp, (l, "v", 5))
                ring_v.wait_full(sp, (l, "q_ctx", 1))
                sp.dma_start(wout, w_out[l].rearrange("(k p) n -> p k n", p=P)).then_inc(wout_loaded, 16)
                sp.wait_ge(att_out, UNITS * (l + 1))
                for s in range(2):
                    load_expert(l, s, s)
                sp.wait_ge(plan_ready, l + 1)
                with sp.Fori(0, EXPERTS // 2 - 1) as i:
                    for s in range(2):
                        done = sp.value_load(blocks[l][0:1, bass.ds(EXPERTS + 2 * i + s, 1)], min_val=0, max_val=100)
                        n = sp.value_load(blocks[l][0:1, bass.ds(2 * i + s, 1)], min_val=1, max_val=5)
                        sp.wait_ge(y_full, done + n)
                        load_expert(l, 2 * i + s + 2, s)
            sp.wait_ge(ckv_out, 16 * 2 * DEPTH)
            sp.wait_ge(outputs_done, 16 * TILES)

        @block.gpsimd
        def _(pool):
            steps = [0]

            def step(ins):
                steps[0] += 1
                ins.then_inc(pool_step, 1)
                pool.wait_ge(pool_step, steps[0])

            step(nc.gpsimd.memset(no_rows[:, :], NO_ROW))
            for l in range(DEPTH):
                done = y_stored if l == DEPTH - 1 else table_cleared
                pool.dma_start(tables[l].rearrange("(p r) j -> p (r j)", p=P), no_rows[:, :]).then_inc(done, 16)
            pool.wait_ge(table_cleared, 16 * (DEPTH - 1))
            pool.wait_ge(y_stored, 16)
            for l in range(DEPTH):
                if l >= 1:
                    pool.wait_ge(comb_added, l * TILES)
                for a, b in ((0, PAD), (PAD + DEC_SEQ, 2 * PAD + DEC_SEQ), (2 * PAD + TOK, ZPAD)):
                    nc.gpsimd.memset(zpad[:, :, a:b], 0.0).then_inc(zero_ready, 1)
                pool.wait_ge(wuq_loaded, 16 * QC * (l + 1))
                for half in range(2):
                    dst = wuq[:, :, :, NOPE + ROPE:P].rearrange("p k h (a s r) -> p (k h) a s r", a=2, s=2)
                    src = wuq[:, :, :, NOPE:NOPE + ROPE].rearrange("p k h (a s r) -> p (k h) a s r", a=2, s=2)
                    nc.gpsimd.tensor_copy(dst[:, :, :, half, :], src[:, :, :, 1 - half, :]).then_inc(wuq_swapped, 1)
                ring_v.wait_empty(pool, (l, "krT", 1))
                pool.wait_ge(wuq_swapped, 2 * (l + 1))
                for h in range(1, HEADS):
                    nc.gpsimd.tensor_copy(kT[NOPE:P, h, :], kT[NOPE:P, 0, :]).then_inc(k_spread, 1)
                pool.wait_ge(k_spread, (HEADS - 1) * (l + 1))
                for k in range(CC):
                    pool.wait_ge(ln_centred, CC * l + k + 1)
                    nc.gpsimd.tensor_tensor(zsq[:, k, :], acc[:, k, :], acc[:, k, :], ALU.mult).then_inc(ln_squared, 1)
                ring_v.wait_full(pool, (l, "ln", 1, 1))
                n = 0
                for i in range(8):
                    part = (2, 6, 3, 5)[i // 2]
                    for j in range(2):
                        d = 16 * l + n
                        if d >= 2:
                            key = slot_of_diag(l, n - 2)
                            ring_v.wait_full(pool, key)
                        if i == 6 and j == 0:
                            for s in range(2):
                                pool.wait_ge(h2_stored[s], 16 * stores_of(l, TILES - s, s))
                            ring_a.wait_full(pool, (l, "h2T", TILES - 1, 1))
                        v = i % 2
                        if part == 6:
                            col = mod[:, 16:32].rearrange("p (k v) -> p k v", v=2)[:, 4 * j:4 * j + 4, v]
                        else:
                            col = adat[:, :].rearrange("p (k v) -> p k v", v=2)[:, 8 * part + 4 * j:8 * part + 4 * j + 4, v]
                        nc.gpsimd.tensor_tensor(diag[:, n % 2].rearrange("p (a n) -> p a n", a=4),
                                                ident.unsqueeze(1).broadcast_to([P, 4, P]),
                                                col.unsqueeze(2).broadcast_to([P, 4, P]), ALU.mult).then_inc(diag_ready, 1)
                        n += 1
                pool.wait_ge(slots_ready, l + 1)
                for t in range(TILES):
                    for r in range(2):
                        at = 3 * (2 * t + r)
                        pool.indirect_dma_start(tables[l], bass.IndirectOffsetOnAxis(ap=idx[:, 2 * t + r:2 * t + r + 1], axis=0),
                                                slot_src[:, at:at + 3], None).then_inc(table_written, 16)
                pool.wait_ge(table_written, 16 * 2 * TILES * (l + 1))
                for s in range(2):
                    pool.wait_ge(h2_stored[s], 16 * stores_of(l, TILES - s, s))
                ring_v.wait_full(pool, (l, "g2", 1, 1))
                step(nc.gpsimd.memset(xg, 0.0))
                pool.wait_ge(plan_ready, l + 1)
                start = pool.value_load(blocks[l][0:1, EXPERTS:EXPERTS + 1], min_val=0, max_val=100)
                count = pool.value_load(blocks[l][0:1, 2 * EXPERTS:2 * EXPERTS + 1], min_val=1, max_val=MAX_BLOCKS)

                def gather(i, n):
                    pool.wait_ge(gate_copied, n + 1)
                    pool.sem_inc(pool_passed, 1)
                    pool.dma_start(slot_tab[:, :], tables[l][bass.ds(i * P, P), :]).then_inc(tab_loaded, 16)
                    pool.wait_ge(tab_loaded, 16 * n + 16)
                    pool.sem_inc(pool_passed, 1)
                    pool.indirect_dma_start(xg, None, h2_dram, bass.IndirectOffsetOnAxis(ap=slot_tab[:, 0:1], axis=0),
                                            bounds_check=TOK - 1, oob_is_err=False).then_inc(gathered, 16)
                    pool.wait_ge(gathered, 16 * n + 16)
                    pool.sem_inc(pool_passed, 1)

                gather(0, start + l)
                with pool.Fori(0, count) as i:
                    gather(i + 1, start + i + (l + 1))
                    pool.wait_ge(y_act, start + i + 2)
                    pool.wait_ge(y_dve, start + i + 2)
                    pool.sem_inc(pool_passed, 1)
                    pool.indirect_dma_start(y_dram, bass.IndirectOffsetOnAxis(ap=row_out[:, 0:1], axis=0), y_sb, None,
                                            bounds_check=2 * TOK - 1, oob_is_err=False).then_inc(y_stored, 16)

        @block.scalar
        def _(act):
            steps = [0]

            def step(ins):
                steps[0] += 1
                ins.then_inc(act_step, 1)
                act.wait_ge(act_step, steps[0])

            def row_stats(l, source):
                for t in range(TILES):
                    step(nc.scalar.activation(junk, source(t), ACT.Square, accum_out=stat[:, t:t + 1]))
                nc.scalar.activation(stat[:, 8:8 + TILES], stat[:, 0:TILES], ACT.Sqrt, scale=1.0 / D,
                                     bias=eps_t[:, 0:1]).then_inc(rms_stat, 1)

            ring_v.wait_empty(act, "cond")
            nc.scalar.activation(cond[:, :].rearrange("p (k v) -> p v k", v=2),
                                 cond_raw[:, :].rearrange("p (v k) -> p v k", v=2),
                                 ACT.Silu).then_inc(cond_ready, 1)
            act.sem_inc(y_act, 1)
            act.wait_ge(x_loaded, 64)

            for l in range(DEPTH):
                for ch in range(ADA_CHUNKS):
                    bank = ring_a.take(act, (l, "ada", ch))
                    if ch >= 2:
                        ring_v.wait_full(act, (l, "adaT", ch - 2))
                    nc.scalar.activation(ada_row[0:2, (ch % 2) * 512:(ch % 2 + 1) * 512], bank[0:2, :], ACT.Copy).then_inc(ring_a.empty, 1)
                if l >= 1:
                    act.wait_ge(comb_added, TILES * l)
                row_stats(l, lambda t: x[:, t, :])
                act.wait_ge(mod_ready, l + 1)

                def modulate(k, v, dst, src):
                    return nc.scalar.activation(dst, src, ACT.Identity, scale=mod[:, 2 * k + v:2 * k + v + 1],
                                                bias=adat[:, 2 * k + v:2 * k + v + 1])

                for k in range(0, DK, 2):
                    bank = ring_a.take(act, (l, "xnT", k))
                    modulate(k, 0, hT[:, k, 0:DEC_SEQ], bank).then_inc(ring_a.empty, 1)
                bank = ring_a.take(act, (l, "xpT", 0))
                for k in range(4):
                    ins = modulate(k, 1, hT[:, k, DEC_SEQ:TOK], bank[:, k * P:(k + 1) * P])
                ins.then_inc(ring_a.empty, 1)
                for ct in range(CC):
                    if ct >= 2 or l >= 1:
                        ring_v.wait_empty(act, (l, "a_ctx", ct - 2) if ct >= 2 else (l - 1, "a_ctx", ct + 2))
                    for name, a, b in (("gate_lat", 0, DEC_SEQ), ("gate_ctx", DEC_SEQ, TOK)):
                        bank = ring_a.take(act, (l, name, ct))
                        nc.scalar.activation(sig[:, ct % 2, a:b], bank[:, 0:b - a], ACT.Sigmoid).then_inc(ring_a.empty, 1)
                for t in range(TILES):
                    bank = ring_a.take(act, (l, "qkv0", t))
                    nc.scalar.activation(proj[:, t, 0:512], bank, ACT.Copy).then_inc(ring_a.empty, 1)
                for t in range(TILES):
                    ring_a.wait_empty(act, (l, "qkv0", t))
                    ring_v.wait_empty(act, (l, "qkv1", t))
                    step(nc.scalar.activation(junk[:, 0:Q_LORA], proj[:, t, 0:Q_LORA], ACT.Square, accum_out=stat[:, 16 + t:17 + t]))
                    step(nc.scalar.activation(junk[:, 0:KV_LORA], proj[:, t, Q_LORA:Q_LORA + KV_LORA], ACT.Square, accum_out=stat[:, 24 + t:25 + t]))
                nc.scalar.activation(stat[:, 32:32 + TILES], stat[:, 16:16 + TILES], ACT.Sqrt, scale=1.0 / Q_LORA,
                                     bias=eps_t[:, 0:1]).then_inc(qkv_stat, 1)
                nc.scalar.activation(stat[:, 40:40 + TILES], stat[:, 24:24 + TILES], ACT.Sqrt, scale=1.0 / KV_LORA,
                                     bias=eps_t[:, 0:1]).then_inc(qkv_stat, 1)
                act.wait_ge(qkv_normed, TILES * (l + 1))
                act.dma_start(new_ckv[0, l], proj[:, LAT, Q_LORA:Q_LORA + KV_LORA]).then_inc(ckv_out, 16)
                act.dma_start(new_krope[0, l], proj[:, LAT, Q_LORA + KV_LORA:QKV]).then_inc(ckv_out, 16)
                for k in range(QC):
                    bank = ring_a.take(act, (l, "qcT", k))
                    nc.scalar.activation(qcT[:, k, 0:DEC_SEQ], bank, ACT.Copy, scale=sb_v(V_QG + k)).then_inc(ring_a.empty, 1)
                bank = ring_a.take(act, (l, "qcT_ctx"))
                for k in range(QC):
                    ins = nc.scalar.activation(qcT[:, k, DEC_SEQ:TOK], bank[:, k * P:(k + 1) * P], ACT.Copy, scale=sb_v(V_QG + k))
                ins.then_inc(ring_a.empty, 1)
                for pr in range(HEADS // 2):
                    for name, a, b in (("k0", 0, 512), ("k1", 512, KEYS)):
                        bank = ring_a.take(act, (l, name, pr))
                        nc.scalar.activation(kT[0:NOPE, 2 * pr, a:b], bank[0:NOPE, 0:b - a], ACT.Copy)
                        nc.scalar.activation(kT[0:NOPE, 2 * pr + 1, a:b], bank[NOPE:P, 0:b - a], ACT.Copy).then_inc(ring_a.empty, 1)
                for t in range(6):
                    bank = ring_a.take(act, (l, "v", t))
                    nc.scalar.activation(v_sb[:, t, :], bank, ACT.Copy).then_inc(ring_a.empty, 1)

                def exponential(i):
                    n = LAT_KEYS if i % TILES < LAT else SEQ
                    u = UNITS * l + i
                    act.wait_ge(att_max, u + 1)
                    if i >= 2:
                        act.wait_ge(prob_turned, u - 1)
                    nc.scalar.activation(prob[:, i % 2, 0:n], flat[:, 1024 * (i % 2):1024 * (i % 2) + n], ACT.Exp,
                                         bias=att_stat[:, UNITS + i:UNITS + i + 1], scale=SCALE,
                                         accum_out=att_stat[:, 2 * UNITS + i:2 * UNITS + i + 1]).then_inc(att_exp, 1)

                def turned(i):
                    n = LAT_KEYS if i % TILES < LAT else SEQ
                    u = UNITS * l + i
                    act.wait_ge(prob_turned, u + 1)
                    if i >= 2:
                        act.wait_ge(att_out, u - 1)
                    nc.scalar.activation(probT[:, i % 2, 0:n], flat[:, 2048:2048 + n], ACT.Copy).then_inc(probT_ready, 1)

                exponential(0)
                for i in range(UNITS):
                    if i + 1 < UNITS:
                        exponential(i + 1)
                    turned(i)
                for k in range(4):
                    bank = ring_a.take(act, (l, "oT", k))
                    nc.scalar.activation(mixT[:, k, 0:DEC_SEQ], bank, ACT.Copy).then_inc(ring_a.empty, 1)
                bank = ring_a.take(act, (l, "oT_ctx"))
                nc.scalar.activation(mixT[:, 0:4, DEC_SEQ:TOK], bank.rearrange("p (k n) -> p k n", k=4), ACT.Copy).then_inc(ring_a.empty, 1)
                for j, (a, b) in enumerate(((0, 512), (512, CONV_OUT))):
                    ring_v.wait_full(act, (l, "ln", 1, j))
                    nc.scalar.activation(ln_rstd[:, a:b], ring_v.bank((l, "ln", 1, j))[:, 0:b - a], ACT.Sqrt,
                                         scale=1.0 / CONV_C, bias=eps_t[:, 0:1]).then_inc(ln_sqrt, 1)
                for k in range(CC):
                    act.wait_ge(ln_done, CC * l + k + 1)
                    for src, dst in (((0, 512), (0, 512)), ((512 + PAD, CONV_OUT), (512, TOK))):
                        nc.scalar.activation(mixT[:, 4 + k, dst[0]:dst[1]], acc[:, k, src[0]:src[1]], ACT.Silu,
                                             scale=sb_v(V_LG + k), bias=sb_v(V_LB + k)).then_inc(conv_silu, 1)

                def turned_h2(t):
                    for j in range(2):
                        bank = ring_a.take(act, (l, "h2T", t, j))
                        nc.scalar.activation(h2T[:, 4 * j:4 * j + 4, t * P:(t + 1) * P],
                                             bank.rearrange("p (k n) -> p k n", k=4), ACT.Copy).then_inc(ring_a.empty, 1)

                for t in range(TILES):
                    act.wait_ge(x_updated, 2 * (TILES * l + t + 1))
                    step(nc.scalar.activation(junk2, x[:, t, :], ACT.Square, accum_out=stat[:, 48 + t:49 + t]))
                    nc.scalar.activation(stat[:, 56 + t:57 + t], stat[:, 48 + t:49 + t], ACT.Sqrt, scale=1.0 / D,
                                         bias=eps_t[:, 0:1]).then_inc(h2_stat, 1)
                    act.wait_ge(h2_ready, TILES * l + t + 1)
                    act.dma_start(h2_dram[t * P:(t + 1) * P, :], h2s[:, t % 2]).then_inc(h2_stored[t % 2], 16)
                    if t >= 1:
                        turned_h2(t - 1)
                turned_h2(TILES - 1)
                bank = ring_a.take(act, (l, "logits"))
                nc.scalar.activation(r_tmp[:, 0:80], bank[:, 0:80], ACT.Sigmoid).then_inc(ring_a.empty, 1)

                act.wait_ge(plan_ready, l + 1)
                start = act.value_load(blocks[l][0:1, EXPERTS:EXPERTS + 1], min_val=0, max_val=100)
                count = act.value_load(blocks[l][0:1, 2 * EXPERTS:2 * EXPERTS + 1], min_val=1, max_val=MAX_BLOCKS)

                def turn(n):
                    act.wait_ge(xT_full, n + 1)
                    nc.scalar.activation(xgT[:, 0:4, :], ps[:, 0].rearrange("p (k n) -> p k n", k=4), ACT.Copy).then_inc(xT_act, 1)

                turn(start + l)
                with act.Fori(0, count) as i:
                    g = start + i
                    act.wait_ge(gu_full, g + 1)
                    nc.scalar.activation(silu_g, ps[:, 2, 0:FF], ACT.Silu).then_inc(silu_ready, 1)
                    turn(g + l + 1)
                    act.wait_ge(y_full, g + 1)
                    act.wait_ge(y_stored, 16 * g + 16)
                    nc.scalar.activation(y_sb[:, 0:512], ps[:, 4], ACT.Copy).then_inc(y_act, 1)
                act.wait_ge(y_stored, (start + count) * 16 + 16)
                act.sem_inc(act_passed, 1)
                for t in range(TILES):
                    for r in range(2):
                        act.dma_start(comb[2 * t + r], y_dram[r * TOK + t * P:r * TOK + (t + 1) * P, :]).then_inc(comb_loaded[t], 16)
            act.wait_ge(comb_added, TILES * DEPTH)
            act.dma_start(final_bc, final_g.rearrange("(a n) -> a n", a=1).broadcast_to([P, D])).then_inc(final_loaded, 16)
            row_stats(DEPTH, lambda t: x[:, t, :])
            for t in range(TILES):
                act.wait_ge(final_ready, t + 1)
                act.dma_start(y_sample[0, t * P:(t + 1) * P, :] if t < LAT else y_prompt[0], xn[:, t, :]).then_inc(outputs_done, 16)

        @block.vector
        def _(dve):
            steps = [0]

            def step(ins):
                steps[0] += 1
                ins.then_inc(dve_step, 1)
                dve.wait_ge(dve_step, steps[0])

            def tt(out, a, b, op):
                return nc.vector.tensor_tensor(out, a, b, op)

            step(nc.vector.memset(eps_t[:, :], EPS))
            step(nc.vector.memset(block_total[:, :], 0.0))
            step(nc.vector.memset(nbf[:, :], 0.0))
            bank = ring_v.take(dve, "cond")
            nc.vector.tensor_copy(cond_raw[:, :], bank[:, 0:2 * DK]).then_inc(ring_v.empty, 1)
            dve.sem_inc(gate_copied, 1)
            dve.sem_inc(y_dve, 1)
            adat3 = adat[:, :].rearrange("p (k v) -> p k v", v=2)
            mod3 = mod[:, :].rearrange("p (k v) -> p k v", v=2)

            for l in range(DEPTH):
                bank = ring_v.take(dve, (l, "vec"))
                step(nc.vector.tensor_copy(vecs[:, 0:VEC_ROWS], bank[:, 0:VEC_ROWS]))
                nc.vector.tensor_copy(vecs[:, P:P + CONV_K * CC], bank[:, P:P + CONV_K * CC]).then_inc(ring_v.empty, 1)
                for ch in range(ADA_CHUNKS):
                    bank = ring_v.take(dve, (l, "adaT", ch))
                    tt(adat3[:, 4 * ch:4 * ch + 4, :], bank[:, 0:8].rearrange("p (k v) -> p k v", v=2),
                       vecs[:, V_BADA + 4 * ch:V_BADA + 4 * ch + 4].unsqueeze(2).broadcast_to([P, 4, 2]),
                       ALU.add).then_inc(ring_v.empty, 1)
                ring_v.wait_empty(dve, (l, "adaT", ADA_CHUNKS - 1))
                for i, (part, gains) in enumerate(((1, V_G1), (4, V_G2))):
                    step(nc.vector.tensor_scalar(mod3[:, 8 * i:8 * i + 8, :], adat3[:, 8 * part:8 * part + 8, :], 1.0, None, ALU.add))
                    ins = tt(mod3[:, 8 * i:8 * i + 8, :], mod3[:, 8 * i:8 * i + 8, :],
                             vecs[:, gains:gains + 8].unsqueeze(2).broadcast_to([P, 8, 2]), ALU.mult)
                    if i == 0:
                        step(ins)
                ins.then_inc(mod_ready, 1)
                dve.wait_ge(mod_ready, l + 1)
                dve.wait_ge(rms_stat, l + 1)
                step(nc.vector.reciprocal(stat[:, 8:8 + TILES], stat[:, 8:8 + TILES]))
                for t in range(TILES):
                    nc.vector.tensor_scalar(xn[:, t, :], x[:, t, :], stat[:, 8 + t:9 + t], None, ALU.mult).then_inc(xn_ready, 1)

                def modulate(k, v, dst, src):
                    return nc.vector.tensor_scalar(dst, src, mod[:, 2 * k + v:2 * k + v + 1],
                                                   adat[:, 2 * k + v:2 * k + v + 1], ALU.mult, ALU.add)

                for k in range(1, DK, 2):
                    bank = ring_v.take(dve, (l, "xnT", k))
                    modulate(k, 0, hT[:, k, 0:DEC_SEQ], bank).then_inc(ring_v.empty, 1)
                bank = ring_v.take(dve, (l, "xpT", 1))
                for k in range(4):
                    ins = modulate(4 + k, 1, hT[:, 4 + k, DEC_SEQ:TOK], bank[:, k * P:(k + 1) * P])
                ins.then_inc(ring_v.empty, 1)
                dve.wait_ge(zero_ready, 3 * (l + 1))
                for ct in range(CC):
                    for name, gate, a, b, at in (("a_lat", "gate_lat", 0, DEC_SEQ, PAD), ("a_ctx", "gate_ctx", DEC_SEQ, TOK, 2 * PAD)):
                        bank = ring_v.take(dve, (l, name, ct))
                        ring_a.wait_empty(dve, (l, gate, ct))
                        tt(zpad[:, ct, a + at:b + at], bank[:, 0:b - a], sig[:, ct % 2, a:b], ALU.mult).then_inc(ring_v.empty, 1)

                conv_list = [(ct, j) for pair in range(CC // 2) for j in range(CONV_K) for ct in (2 * pair, 2 * pair + 1)]
                conv_at = [0]

                def conv(n):
                    for ct, j in conv_list[conv_at[0]:conv_at[0] + n]:
                        m = conv_at[0]
                        w = vecs[:, P + j * CC + ct:P + j * CC + ct + 1]
                        if j == 0:
                            ring_v.wait_empty(dve, (l, "a_ctx", ct))
                            ins = nc.vector.tensor_scalar(acc[:, ct, :], zpad[:, ct, 0:CONV_OUT], w, sb_v(V_CB + ct), ALU.mult, ALU.add)
                        else:
                            dve.wait_ge(conv_step, l * len(conv_list) + m - 1)
                            ins = nc.vector.scalar_tensor_tensor(acc[:, ct, :], zpad[:, ct, j:j + CONV_OUT], w, acc[:, ct, :], ALU.mult, ALU.add)
                        ins.then_inc(conv_step, 1)
                        conv_at[0] += 1

                for t in range(TILES):
                    bank = ring_v.take(dve, (l, "qkv1", t))
                    nc.vector.tensor_copy(proj[:, t, 512:QKV], bank[:, 0:QKV - 512]).then_inc(ring_v.empty, 1)
                    conv(3)
                dve.wait_ge(qkv_stat, 2 * (l + 1))
                step(nc.vector.reciprocal(stat[:, 32:32 + TILES], stat[:, 32:32 + TILES]))
                step(nc.vector.reciprocal(stat[:, 40:40 + TILES], stat[:, 40:40 + TILES]))
                dve.wait_ge(kvg_loaded, 16 * (l + 1))
                for t in range(TILES):
                    nc.vector.tensor_scalar(proj[:, t, 0:Q_LORA], proj[:, t, 0:Q_LORA], stat[:, 32 + t:33 + t], None, ALU.mult)
                    nc.vector.scalar_tensor_tensor(proj[:, t, Q_LORA:Q_LORA + KV_LORA], proj[:, t, Q_LORA:Q_LORA + KV_LORA],
                                                   stat[:, 40 + t:41 + t], kvg[:, :], ALU.mult, ALU.mult).then_inc(qkv_normed, 1)
                step(nc.vector.memset(kr[:, :, 0:NOPE], 0.0))
                kin = proj[:, 0:LAT, Q_LORA + KV_LORA:QKV]
                kcos = con[:, C_KC:C_KC + LAT * ROPE].rearrange("p (t n) -> p t n", t=LAT)
                ksin = con[:, C_KS:C_KS + LAT * ROPE].rearrange("p (t n) -> p t n", t=LAT)
                half = lambda ap, s: ap.rearrange("p t (a s r) -> p t a s r", a=2, s=2)[:, :, :, s, :]
                k1, k2 = kr[:, 0:LAT, NOPE:NOPE + ROPE], kr[:, 0:LAT, NOPE + ROPE:P]
                step(tt(k1, kin, kcos, ALU.mult))
                step(tt(half(k2, 0), half(kin, 1), half(ksin, 0), ALU.mult))
                step(tt(half(k2, 1), half(kin, 0), half(ksin, 1), ALU.mult))
                step(tt(k1, k1, k2, ALU.add))
                step(nc.vector.tensor_copy(k2, k1))
                dve.wait_ge(cache_loaded, 32 * (l + 1))
                for s in range(2):
                    a = NOPE + s * ROPE
                    step(nc.vector.tensor_copy(kr[:, 4, a:a + ROPE], cache_sb[:, KV_LORA:KV_LORA + ROPE]))
                    ins = nc.vector.tensor_copy(kr[:, 5, a:a + ROPE], proj[:, LAT, Q_LORA + KV_LORA:QKV])
                    if s == 0:
                        step(ins)
                ins.then_inc(krope_ready, 1)
                for k in range(KC):
                    bank = ring_v.take(dve, (l, "ckvT", k))
                    nc.vector.tensor_copy(ckvT[:, k, 0:DEC_SEQ], bank).then_inc(ring_v.empty, 1)
                for k in range(KC):
                    bank = ring_v.take(dve, (l, "ckvT_rest", k))
                    nc.vector.tensor_copy(ckvT[:, k, DEC_SEQ:KEYS], bank[:, 0:256]).then_inc(ring_v.empty, 1)
                bank = ring_v.take(dve, (l, "krT", 0))
                nc.vector.tensor_copy(kT[NOPE:P, 0, 0:512], bank[NOPE:P, :]).then_inc(ring_v.empty, 1)
                bank = ring_v.take(dve, (l, "krT", 1))
                nc.vector.tensor_copy(kT[NOPE:P, 0, 512:KEYS], bank[NOPE:P, 0:256]).then_inc(ring_v.empty, 1)
                tab = con[:, C_TAB:C_TAB + TOK]
                for h in range(HEADS):
                    bank = ring_v.take(dve, (l, "q", h))
                    tt(qT[:, h, 0:DEC_SEQ], bank, tab[:, 0:DEC_SEQ], ALU.mult).then_inc(ring_v.empty, 1)
                    conv(1)
                for j in range(2):
                    bank = ring_v.take(dve, (l, "q_ctx", j))
                    tt(qT[:, 4 * j:4 * j + 4, DEC_SEQ:TOK], bank.rearrange("p (h n) -> p h n", h=4),
                       tab[:, DEC_SEQ:TOK].unsqueeze(1).broadcast_to([P, 4, P]), ALU.mult).then_inc(ring_v.empty, 1)
                conv(8)

                def maximum(i):
                    n = LAT_KEYS if i % TILES < LAT else SEQ
                    dve.wait_ge(scores, UNITS * l + i + 1)
                    step(nc.vector.reduce_max(att_stat[:, i:i + 1], flat[:, 1024 * (i % 2):1024 * (i % 2) + n], AXIS_X))
                    nc.vector.tensor_scalar(att_stat[:, UNITS + i:UNITS + i + 1], att_stat[:, i:i + 1], -SCALE, None, ALU.mult).then_inc(att_max, 1)

                def output(i):
                    h, t = divmod(i, TILES)
                    dve.wait_ge(att_out, UNITS * l + i + 1)
                    step(nc.vector.reciprocal(att_stat[:, 3 * UNITS + i:3 * UNITS + i + 1], att_stat[:, 2 * UNITS + i:2 * UNITS + i + 1]))
                    nc.vector.tensor_scalar(o_tok[:, t, h * VH:(h + 1) * VH], ps[:, 6 + i % 2, 0:VH],
                                            att_stat[:, 3 * UNITS + i:3 * UNITS + i + 1], None, ALU.mult).then_inc(att_out_empty, 1)

                dve.wait_ge(ckv_out, 32 * (l + 1))
                for i in range(UNITS):
                    maximum(i)
                    if i >= 2:
                        output(i - 2)
                    conv(3)
                output(UNITS - 2)
                output(UNITS - 1)
                conv(len(conv_list))
                dve.wait_ge(conv_step, (l + 1) * len(conv_list))
                halves = ((0, 512), (512, CONV_OUT))
                for j, (a, b) in enumerate(halves):
                    bank = ring_v.take(dve, (l, "ln", 0, j))
                    for k in range(CC):
                        ins = nc.vector.scalar_tensor_tensor(acc[:, k, a:b], bank[:, 0:b - a], -1.0 / CONV_C, acc[:, k, a:b], ALU.mult, ALU.add)
                        if j == 0:
                            if k == CC - 1:
                                ins.then_inc(ring_v.empty, 1)
                        elif k < CC - 1:
                            ins.then_inc(ln_centred, 1)
                        else:
                            step(ins)
                dve.sem_inc(ln_centred, 1)
                dve.sem_inc(ring_v.empty, 1)
                for j, (a, b) in enumerate(halves):
                    dve.wait_ge(ln_sqrt, 2 * l + j + 1)
                    step(nc.vector.reciprocal(ln_rstd[:, a:b], ln_rstd[:, a:b]))
                    dve.sem_inc(ring_v.empty, 1)
                for k in range(CC):
                    tt(acc[:, k, :], acc[:, k, :], ln_rstd, ALU.mult).then_inc(ln_done, 1)
                dve.wait_ge(conv_silu, 2 * CC * (l + 1))
                for i in range(6):
                    for j in range(2):
                        bank = ring_v.take(dve, (l, "bc", i, j))
                        nc.vector.tensor_copy(bc[:, i, j * 512:(j + 1) * 512], bank).then_inc(ring_v.empty, 1)
                ring_v.wait_empty(dve, (l, "bc", 5, 1))
                for t in range(TILES):
                    v = 0 if t < LAT else 1
                    for j in range(2):
                        cols = slice(j * 512, (j + 1) * 512)
                        bank = ring_v.take(dve, (l, "wo", t, j))
                        tt(res_tmp[:, cols], bank, g1_bc(v)[:, cols], ALU.mult).then_inc(ring_v.empty, 1)
                        ring_v.wait_empty(dve, (l, "wo", t, j))
                        tt(x[:, t, cols], x[:, t, cols], res_tmp[:, cols], ALU.add).then_inc(x_updated, 1)
                    dve.wait_ge(h2_stat, TILES * l + t + 1)
                    step(nc.vector.reciprocal(stat[:, 56 + t:57 + t], stat[:, 56 + t:57 + t]))
                    if t >= 2:
                        dve.wait_ge(h2_stored[t % 2], 16 * stores_of(l, t, t % 2))
                        ring_a.wait_full(dve, (l, "h2T", t - 2, 1))
                    step(nc.vector.scalar_tensor_tensor(h2s[:, t % 2], x[:, t, :], stat[:, 56 + t:57 + t], a2_bc(v), ALU.mult, ALU.mult))
                    tt(h2s[:, t % 2], h2s[:, t % 2], sh2_bc(v), ALU.add).then_inc(h2_ready, 1)

                cur = [80]

                def temp(n):
                    a = cur[0]
                    cur[0] += n
                    return r_tmp[:, a:a + n]

                t16 = lambda ap: ap.rearrange("p (t e) -> p t e", t=TILES)
                over16 = lambda ap, n=EXPERTS: ap.unsqueeze(2).broadcast_to([P, TILES, n])
                aff = t16(r_tmp[:, 0:80])
                w16 = con[:, C_W16:C_W16 + EXPERTS].unsqueeze(1).broadcast_to([P, TILES, EXPERTS])
                w4 = con[:, C_W4:C_W4 + GROUPS].unsqueeze(1).broadcast_to([P, TILES, GROUPS])
                ring_a.wait_empty(dve, (l, "logits"))
                sel = temp(80)
                step(tt(t16(sel), aff, rb[:, :].unsqueeze(1).broadcast_to([P, TILES, EXPERTS]), ALU.add))
                TG = TILES * GROUPS
                s4 = sel.rearrange("p (g m) -> p g m", m=PER_GROUP)
                sums = temp(TG * 6).rearrange("p (g m) -> p g m", m=6)
                for n, m, at in ((3, 3, 0), (2, 2, 3), (1, 1, 5)):
                    step(tt(sums[:, :, at:at + n], s4[:, :, 0:n], s4[:, :, m:m + 1].broadcast_to([P, TG, n]), ALU.add))
                score = temp(TG)
                step(nc.vector.reduce_max(score, sums, AXIS_X))

                def first_max(values, weights, out, width):
                    top = temp(TILES)
                    v3 = values.rearrange("p (t e) -> p t e", t=TILES)
                    o3 = out.rearrange("p (t e) -> p t e", t=TILES)
                    step(nc.vector.reduce_max(top, v3, AXIS_X))
                    step(tt(o3, v3, over16(top, width), ALU.is_equal))
                    step(tt(o3, o3, weights, ALU.mult))
                    step(nc.vector.reduce_max(top, o3, AXIS_X))
                    step(tt(o3, o3, over16(top, width), ALU.is_equal))

                in_group = temp(TG)
                first_max(score, w4, in_group, GROUPS)
                outside = temp(TG)
                step(nc.vector.tensor_scalar(outside, in_group, 1.0, BIG, ALU.subtract, ALU.mult))
                step(tt(s4, s4, in_group.unsqueeze(2).broadcast_to([P, TG, PER_GROUP]), ALU.mult))
                step(tt(s4, s4, outside.unsqueeze(2).broadcast_to([P, TG, PER_GROUP]), ALU.add))
                hot = [temp(80), temp(80)]
                first_max(sel, w16, hot[0], EXPERTS)
                step(nc.vector.scalar_tensor_tensor(sel, hot[0], -2 * BIG, sel, ALU.mult, ALU.add))
                first_max(sel, w16, hot[1], EXPERTS)
                both = temp(80)
                tt(both, hot[0], hot[1], ALU.add).then_inc(masks_ready, 1)
                dve.wait_ge(masks_ready, l + 1)
                top_aff, total, prod = temp(2 * TILES), temp(TILES), temp(80)
                for r in range(2):
                    step(tt(t16(prod), aff, t16(hot[r]), ALU.mult))
                    step(nc.vector.reduce_sum(top_aff[:, r * TILES:(r + 1) * TILES], t16(prod), AXIS_X))
                step(tt(total, top_aff[:, 0:TILES], top_aff[:, TILES:2 * TILES], ALU.add))
                step(nc.vector.reciprocal(total, total))
                src4 = slot_src[:, :].rearrange("p (t r j) -> p t r j", r=2, j=3)
                for r in range(2):
                    step(nc.vector.tensor_scalar(src4[:, :, r, 2], con[:, C_TOKID:C_TOKID + TILES], float(r * TOK), None, ALU.add))
                    step(tt(src4[:, :, r, 1].bitcast(FP32), top_aff[:, r * TILES:(r + 1) * TILES], total, ALU.mult))
                    step(nc.vector.tensor_copy(src4[:, :, r, 0], con[:, C_TOKID:C_TOKID + TILES]))
                for v in range(2):
                    for j in range(2):
                        bank = ring_v.take(dve, (l, "g2", v, j))
                        nc.vector.tensor_copy(g2_bc(v)[:, j * 512:(j + 1) * 512], bank).then_inc(ring_v.empty, 1)
                bank = ring_v.take(dve, (l, "slots"))
                counts = bank[:, 80:96]
                row = lambda i: nbf[:, 24 * i + 8:24 * i + 24]
                row_shift = lambda i, s: nbf[:, 24 * i + 8 - s:24 * i + 24 - s]
                step(nc.vector.tensor_scalar(row(0), counts, float(P) + 0.5, 1.0, ALU.is_gt, ALU.add))
                for m in range(2, TOK // P):
                    step(nc.vector.scalar_tensor_tensor(row(0), counts, float(m * P) + 0.5, row(0), ALU.is_gt, ALU.add))
                step(tt(row(1), row(0), row_shift(0, 1), ALU.add))
                step(tt(row(2), row(1), row_shift(1, 2), ALU.add))
                step(tt(row(1), row(2), row_shift(2, 4), ALU.add))
                step(tt(row(2), row(1), row_shift(1, 8), ALU.add))
                step(tt(row(3), row(2), row(0), ALU.subtract))
                place = temp(80)
                step(nc.vector.tensor_scalar(row(1), row(3), float(P), None, ALU.mult))
                step(tt(t16(place), t16(bank[:, 0:80]), row(1).unsqueeze(1).broadcast_to([P, TILES, EXPERTS]), ALU.add))
                found = temp(TILES)
                idx3 = idx[:, :].rearrange("p (t r) -> p t r", r=2)
                for r in range(2):
                    step(tt(t16(prod), t16(place), t16(hot[r]), ALU.mult))
                    step(nc.vector.reduce_sum(found, t16(prod), AXIS_X))
                    ins = nc.vector.tensor_copy(idx3[:, :, r], found)
                    if r == 0:
                        step(ins)
                ins.then_inc(slots_ready, 1)
                step(nc.vector.tensor_copy(blocks[l][0:1, 0:EXPERTS], row(0)[0:1]))
                step(nc.vector.tensor_scalar(blocks[l][0:1, EXPERTS:2 * EXPERTS], row(3)[0:1], block_total[0:1, 0:1], None, ALU.add))
                step(nc.vector.tensor_copy(blocks[l][0:1, 2 * EXPERTS:2 * EXPERTS + 1], row(2)[0:1, EXPERTS - 1:EXPERTS]))
                step(tt(block_total[0:1, 0:1], block_total[0:1, 0:1], row(2)[0:1, EXPERTS - 1:EXPERTS], ALU.add))
                dve.sem_inc(plan_ready, 1)
                dve.sem_inc(ring_v.empty, 1)

                start = dve.value_load(blocks[l][0:1, EXPERTS:EXPERTS + 1], min_val=0, max_val=100)
                count = dve.value_load(blocks[l][0:1, 2 * EXPERTS:2 * EXPERTS + 1], min_val=1, max_val=MAX_BLOCKS)

                def turn(n):
                    dve.wait_ge(xT_full, n + 1)
                    nc.vector.tensor_copy(xgT[:, 4:8, :], ps[:, 1].rearrange("p (k n) -> p k n", k=4)).then_inc(xT_dve, 1)
                    dve.wait_ge(gathered, 16 * n + 16)
                    nc.vector.tensor_copy(row_next[:, :], slot_tab[:, 2:3])
                    nc.vector.tensor_copy(gate_col[:, :], slot_tab[:, 1:2].bitcast(FP32)).then_inc(gate_copied, 1)

                turn(start + l)
                with dve.Fori(0, count) as i:
                    g = start + i
                    dve.wait_ge(silu_ready, g + 1)
                    dve.wait_ge(gate_copied, g + (l + 2))
                    nc.vector.scalar_tensor_tensor(hid, ps[:, 2, FF:2 * FF], gate_col[:, 0:1], silu_g, ALU.mult, ALU.mult).then_inc(hid_ready, 1)
                    dve.wait_ge(y_dve, g + 1)
                    nc.vector.tensor_copy(row_work[:, :], row_next[:, :]).then_inc(row_moved, 1)
                    dve.wait_ge(hidT_full, g + 1)
                    nc.vector.tensor_copy(hidT, ps[:, 3, 0:256].rearrange("p (k n) -> p k n", k=2)).then_inc(hidT_ready, 1)
                    dve.wait_ge(row_moved, g + 1)
                    dve.wait_ge(hid_ready, g + 1)
                    turn(g + (l + 1))
                    dve.wait_ge(y_stored, 16 * g + 16)
                    nc.vector.tensor_copy(row_out[:, :], row_work[:, :])
                    dve.wait_ge(y_full, g + 1)
                    nc.vector.tensor_copy(y_sb[:, 512:1024], ps[:, 5]).then_inc(y_dve, 1)
                for t in range(TILES):
                    v = 0 if t < LAT else 1
                    a, b2 = comb[2 * t], comb[2 * t + 1]
                    dve.wait_ge(comb_loaded[t], 32 * (l + 1))
                    step(tt(a, a, b2, ALU.add))
                    step(tt(a, a, g2_bc(v), ALU.mult))
                    tt(x[:, t, :], x[:, t, :], a, ALU.add).then_inc(comb_added, 1)
            dve.wait_ge(rms_stat, DEPTH + 1)
            step(nc.vector.reciprocal(stat[:, 8:8 + TILES], stat[:, 8:8 + TILES]))
            dve.wait_ge(final_loaded, 16)
            for t in range(TILES):
                nc.vector.scalar_tensor_tensor(xn[:, t, :], x[:, t, :], stat[:, 8 + t:9 + t], final_bc, ALU.mult, ALU.mult).then_inc(final_ready, 1)

        @block.tensor
        def _(pe):
            def product(out, lhs, rhs, n):
                for k in range(n):
                    ins = nc.tensor.matmul(out, lhs(k), rhs(k), start=(k == 0), stop=(k == n - 1))
                return ins

            pe.wait_ge(const_loaded, 16)
            pe.wait_ge(cond_loaded, 32)
            bank = ring_v.open(pe, "cond")
            nc.tensor.transpose(bank[:, 0:2 * DK], vec_rows[0:2 * DK, P:2 * P], ident[0:2 * DK, 0:2 * DK]).then_inc(ring_v.full, 1)

            for l in range(DEPTH):
                if l >= 1:
                    end = pe.value_load(blocks[l - 1][0:1, 2 * EXPERTS - 1:2 * EXPERTS], min_val=0, max_val=100)
                    n_last = pe.value_load(blocks[l - 1][0:1, EXPERTS - 1:EXPERTS], min_val=1, max_val=5)
                    for s in (y_act, y_dve):
                        pe.wait_ge(s, end + n_last + 1)
                    for s in (xT_act, xT_dve):
                        pe.wait_ge(s, end + n_last + l)
                    pe.sem_inc(pe_passed, 1)
                pe.wait_ge(rows_loaded, 128 * (l + 1))
                bank = ring_v.open(pe, (l, "vec"))
                nc.tensor.transpose(bank[:, 0:VEC_ROWS], vec_rows[0:VEC_ROWS, 0:P], ident[0:VEC_ROWS, 0:VEC_ROWS])
                nc.tensor.transpose(bank[:, P:P + CONV_K * CC], vec_rows[0:CONV_K * CC, P:2 * P],
                                    ident[0:CONV_K * CC, 0:CONV_K * CC]).then_inc(ring_v.full, 1)
                if l == 0:
                    pe.wait_ge(cond_ready, 1)

                def ada_turn(ch):
                    ring_a.wait_empty(pe, (l, "ada", ch))
                    bank = ring_v.open(pe, (l, "adaT", ch))
                    for j in range(4):
                        at = (ch % 2) * 512 + j * P
                        ins = nc.tensor.transpose(bank[:, 2 * j:2 * j + 2], ada_row[0:2, at:at + P], ident[0:2, 0:2])
                    ins.then_inc(ring_v.full, 1)

                for ch in range(ADA_CHUNKS):
                    pe.wait_ge(ada_loaded[ch % 2], 16 * (ADA_CHUNKS // 2 * l + ch // 2 + 1))
                    bank = ring_a.open(pe, (l, "ada", ch))
                    product(bank[0:2, :], lambda k: cond[:, 2 * k:2 * k + 2], lambda k: ada_w[ch % 2][:, k, :], DK).then_inc(ring_a.full, 1)
                    if ch >= 1:
                        ada_turn(ch - 1)
                ada_turn(ADA_CHUNKS - 1)
                pe.wait_ge(xn_ready, TILES * (l + 1))
                for k in range(DK):
                    ring = ring_v if k % 2 else ring_a
                    bank = ring.open(pe, (l, "xnT", k))
                    for t in range(LAT):
                        ins = nc.tensor.transpose(bank[:, t * P:(t + 1) * P], xn[:, t, k * P:(k + 1) * P], ident)
                    ins.then_inc(ring.full, 1)
                for j, ring in enumerate((ring_a, ring_v)):
                    bank = ring.open(pe, (l, "xpT", j))
                    for k in range(4):
                        ins = nc.tensor.transpose(bank[:, k * P:(k + 1) * P], xn[:, LAT, (4 * j + k) * P:(4 * j + k + 1) * P], ident)
                    ins.then_inc(ring.full, 1)
                ring_a.wait_empty(pe, (l, "xpT", 0))
                ring_v.wait_empty(pe, (l, "xpT", 1))
                pe.wait_ge(win_conv_loaded, 16 * (l + 1))
                for ct in range(CC):
                    for ring, name, col in ((ring_a, "gate", QKV + CONV_C + ct * P), (ring_v, "a", QKV + ct * P)):
                        for part, a, b in (("_lat", 0, DEC_SEQ), ("_ctx", DEC_SEQ, TOK)):
                            bank = ring.open(pe, (l, name + part, ct))
                            product(bank[:, 0:b - a], lambda k: win[:, k, col:col + P], lambda k: hT[:, k, a:b], DK).then_inc(ring.full, 1)
                pe.wait_ge(win_qkv_loaded, 16 * (l + 1))
                for t in range(TILES):
                    for ring, name, a, b in ((ring_a, "qkv0", 0, 512), (ring_v, "qkv1", 512, QKV)):
                        bank = ring.open(pe, (l, name, t))
                        product(bank[:, 0:b - a], lambda k: hT[:, k, t * P:(t + 1) * P], lambda k: win[:, k, a:b], DK).then_inc(ring.full, 1)
                pe.wait_ge(qkv_normed, TILES * (l + 1))
                for k in range(QC):
                    bank = ring_a.open(pe, (l, "qcT", k))
                    for t in range(LAT):
                        ins = nc.tensor.transpose(bank[:, t * P:(t + 1) * P], proj[:, t, k * P:(k + 1) * P], ident)
                    ins.then_inc(ring_a.full, 1)
                bank = ring_a.open(pe, (l, "qcT_ctx"))
                for k in range(QC):
                    ins = nc.tensor.transpose(bank[:, k * P:(k + 1) * P], proj[:, LAT, k * P:(k + 1) * P], ident)
                ins.then_inc(ring_a.full, 1)
                for k in range(KC):
                    bank = ring_v.open(pe, (l, "ckvT", k))
                    for t in range(LAT):
                        ins = nc.tensor.transpose(bank[:, t * P:(t + 1) * P], proj[:, t, Q_LORA + k * P:Q_LORA + (k + 1) * P], ident)
                    ins.then_inc(ring_v.full, 1)
                pe.wait_ge(cache_loaded, 32 * (l + 1))
                for k in range(KC):
                    bank = ring_v.open(pe, (l, "ckvT_rest", k))
                    nc.tensor.transpose(bank[:, 0:P], cache_sb[:, k * P:(k + 1) * P], ident)
                    nc.tensor.transpose(bank[:, P:2 * P], proj[:, LAT, Q_LORA + k * P:Q_LORA + (k + 1) * P], ident).then_inc(ring_v.full, 1)
                pe.wait_ge(krope_ready, l + 1)
                for j, tiles in enumerate(((0, 1, 2, 3), (4, 5))):
                    bank = ring_v.open(pe, (l, "krT", j))
                    for n, t in enumerate(tiles):
                        ins = nc.tensor.transpose(bank[:, n * P:(n + 1) * P], kr[:, t, :], ident)
                    ins.then_inc(ring_v.full, 1)
                pe.wait_ge(wuq_swapped, 2 * (l + 1))
                ring_a.wait_empty(pe, (l, "qcT_ctx"))
                for h in range(HEADS):
                    bank = ring_v.open(pe, (l, "q", h))
                    product(bank, lambda k: wuq[:, k, h, :], lambda k: qcT[:, k, 0:DEC_SEQ], QC).then_inc(ring_v.full, 1)
                for j in range(2):
                    bank = ring_v.open(pe, (l, "q_ctx", j))
                    for h in range(4):
                        ins = product(bank[:, h * P:(h + 1) * P], lambda k: wuq[:, k, 4 * j + h, :], lambda k: qcT[:, k, DEC_SEQ:TOK], QC)
                    ins.then_inc(ring_v.full, 1)
                pe.wait_ge(wukv_loaded, 16 * 2 * KC * (l + 1))
                ring_v.wait_empty(pe, (l, "ckvT_rest", KC - 1))
                for pr in range(HEADS // 2):
                    for name, a, b in (("k0", 0, 512), ("k1", 512, KEYS)):
                        bank = ring_a.open(pe, (l, name, pr))
                        product(bank[:, 0:b - a], lambda k: wk[:, k, pr * P:(pr + 1) * P], lambda k: ckvT[:, k, a:b], KC).then_inc(ring_a.full, 1)
                for t in range(6):
                    bank = ring_a.open(pe, (l, "v", t))
                    product(bank, lambda k: ckvT[:, k, t * P:(t + 1) * P], lambda k: wv[:, k, :], KC).then_inc(ring_a.full, 1)

                pe.wait_ge(k_spread, (HEADS - 1) * (l + 1))
                ring_a.wait_empty(pe, (l, "v", 5))
                ring_v.wait_empty(pe, (l, "q_ctx", 1))

                def score(i):
                    h, t = divmod(i, TILES)
                    b = 2 * (i % 2)
                    if i >= 2:
                        pe.wait_ge(att_exp, UNITS * l + i - 1)
                    q = qT[:, h, t * P:(t + 1) * P]
                    if t < LAT:
                        nc.tensor.matmul(ps[:, b], q, kT[:, h, 0:512], start=True, stop=True)
                        nc.tensor.matmul(ps[:, b + 1, 0:P], q, kT[:, h, 512:LAT_KEYS], start=True, stop=True).then_inc(scores, 1)
                    else:
                        nc.tensor.matmul(ps[:, b, 0:P], q, kT[:, h, LAT_KEYS:KEYS], start=True, stop=True).then_inc(scores, 1)

                score(0)
                score(1)
                for i in range(UNITS):
                    h, t = divmod(i, TILES)
                    u = UNITS * l + i
                    key_tiles = range(LAT + 1) if t < LAT else range(5, 6)
                    pe.wait_ge(att_exp, u + 1)
                    if i >= 1:
                        pe.wait_ge(probT_ready, u)
                    for n, kt in enumerate(key_tiles):
                        ins = nc.tensor.transpose(flat[:, 2048 + n * P:2048 + (n + 1) * P], prob[:, i % 2, n * P:(n + 1) * P], ident)
                    ins.then_inc(prob_turned, 1)
                    if i + 2 < UNITS:
                        score(i + 2)
                    pe.wait_ge(probT_ready, u + 1)
                    if i >= 2:
                        pe.wait_ge(att_out_empty, u - 1)
                    for n, kt in enumerate(key_tiles):
                        ins = nc.tensor.matmul(ps[:, 6 + i % 2, 0:VH], probT[:, i % 2, n * P:(n + 1) * P],
                                               v_sb[:, kt, h * VH:(h + 1) * VH], start=(n == 0), stop=(n == len(key_tiles) - 1))
                    ins.then_inc(att_out, 1)
                pe.wait_ge(att_out_empty, UNITS * (l + 1))
                pe.wait_ge(probT_ready, UNITS * (l + 1))
                for k in range(4):
                    bank = ring_a.open(pe, (l, "oT", k))
                    for t in range(LAT):
                        ins = nc.tensor.transpose(bank[:, t * P:(t + 1) * P], o_tok[:, t, k * P:(k + 1) * P], ident)
                    ins.then_inc(ring_a.full, 1)
                bank = ring_a.open(pe, (l, "oT_ctx"))
                for k in range(4):
                    ins = nc.tensor.transpose(bank[:, k * P:(k + 1) * P], o_tok[:, LAT, k * P:(k + 1) * P], ident)
                ins.then_inc(ring_a.full, 1)
                pe.wait_ge(conv_step, (l + 1) * CONV_K * CC)
                for s in range(2):
                    if s == 1:
                        pe.wait_ge(ln_squared, CC * (l + 1))
                    src = zsq if s else acc
                    for j, (a, b) in enumerate(((0, 512), (512, CONV_OUT))):
                        bank = ring_v.open(pe, (l, "ln", s, j))
                        product(bank[:, 0:b - a], lambda k: ones, lambda k: src[:, k, a:b], CC).then_inc(ring_v.full, 1)

                def spread(key, d):
                    pe.wait_ge(diag_ready, d + 1)
                    bank = ring_v.open(pe, key)
                    nc.tensor.matmul(bank, ones, diag[:, d % 2], start=True, stop=True).then_inc(ring_v.full, 1)

                for n in range(12):
                    spread((l, "bc", n // 2, n % 2), 16 * l + n)
                pe.wait_ge(wout_loaded, 16 * (l + 1))
                pe.wait_ge(conv_silu, 2 * CC * (l + 1))
                ring_a.wait_empty(pe, (l, "oT_ctx"))

                def h2_turn(t):
                    pe.wait_ge(h2_ready, TILES * l + t + 1)
                    for j in range(2):
                        bank = ring_a.open(pe, (l, "h2T", t, j))
                        for k in range(4):
                            ins = nc.tensor.transpose(bank[:, k * P:(k + 1) * P], h2s[:, t % 2, (4 * j + k) * P:(4 * j + k + 1) * P], ident)
                        ins.then_inc(ring_a.full, 1)

                for t in range(TILES):
                    for j in range(2):
                        bank = ring_v.open(pe, (l, "wo", t, j))
                        product(bank, lambda k: mixT[:, k, t * P:(t + 1) * P], lambda k: wout[:, k, j * 512:(j + 1) * 512], DK).then_inc(ring_v.full, 1)
                    if t >= 1:
                        h2_turn(t - 1)
                h2_turn(TILES - 1)
                ring_a.wait_empty(pe, (l, "h2T", TILES - 1, 1))
                bank = ring_a.open(pe, (l, "logits"))
                for t in range(TILES):
                    ins = product(bank[:, t * EXPERTS:(t + 1) * EXPERTS], lambda k: h2T[:, k, t * P:(t + 1) * P],
                                  lambda k: rw[:, k * EXPERTS:(k + 1) * EXPERTS], DK)
                ins.then_inc(ring_a.full, 1)
                for n in range(4):
                    spread((l, "g2", n // 2, n % 2), 16 * l + 12 + n)
                pe.wait_ge(masks_ready, l + 1)
                both = r_tmp[:, BOTH_AT:BOTH_AT + 80]
                bank = ring_v.open(pe, (l, "slots"))
                for t in range(TILES):
                    for s in range(t + 1):
                        nc.tensor.matmul(bank[:, t * EXPERTS:(t + 1) * EXPERTS], tri if s == t else ones,
                                         both[:, s * EXPERTS:(s + 1) * EXPERTS], start=(s == 0), stop=(s == t))
                for s in range(TILES):
                    ins = nc.tensor.matmul(bank[:, 80:96], ones, both[:, s * EXPERTS:(s + 1) * EXPERTS], start=(s == 0), stop=(s == TILES - 1))
                ins.then_inc(ring_v.full, 1)

                pe.wait_ge(plan_ready, l + 1)
                start = pe.value_load(blocks[l][0:1, EXPERTS:EXPERTS + 1], min_val=0, max_val=100)

                def turn(n):
                    pe.wait_ge(gathered, 16 * n + 16)
                    for k in range(DK):
                        ins = nc.tensor.transpose(ps[:, k // 4, (k % 4) * P:(k % 4 + 1) * P], xg[:, k * P:(k + 1) * P], ident)
                    ins.then_inc(xT_full, 1)

                turn(start + l)
                with pe.Fori(0, EXPERTS // 2) as i:
                    for s in range(2):
                        first = pe.value_load(blocks[l][0:1, bass.ds(EXPERTS + 2 * i + s, 1)], min_val=0, max_val=100)
                        count = pe.value_load(blocks[l][0:1, bass.ds(2 * i + s, 1)], min_val=1, max_val=5)
                        pe.wait_ge(expert_loaded[s], (i + (EXPERTS // 2 * l + 1)) * 48)
                        pe.sem_inc(pe_passed, 1)
                        with pe.Fori(0, count) as b:
                            g = first + b
                            pe.wait_ge(xT_act, g + l + 1)
                            pe.wait_ge(xT_dve, g + l + 1)
                            product(ps[:, 2], lambda k: xgT[:, k, :], lambda k: wgu[s][:, k, :], DK).then_inc(gu_full, 1)
                            turn(g + l + 1)
                            pe.wait_ge(hid_ready, g + 1)
                            for k in range(2):
                                ins = nc.tensor.transpose(ps[:, 3, k * P:(k + 1) * P], hid[:, k * P:(k + 1) * P], ident)
                            ins.then_inc(hidT_full, 1)
                            pe.wait_ge(hidT_ready, g + 1)
                            pe.wait_ge(y_act, g + 1)
                            pe.wait_ge(y_dve, g + 1)
                            product(ps[:, 4], lambda k: hidT[:, k, :], lambda k: wdn[s][:, k, 0:512], 2)
                            product(ps[:, 5], lambda k: hidT[:, k, :], lambda k: wdn[s][:, k, 512:1024], 2).then_inc(y_full, 1)


BOTH_AT = 80 + 80 + 120 + 20 + 20 + 5 + 20 + 80 + 80 + 5 + 5
_INS = ['x_prompt', 'x_sample', 'cache_ckv', 'cache_krope', 'c', 'c_ctx', 'w_ada', 'b_ada', 'norm1_g', 'w_in',
        'q_norm_g', 'w_uq', 'kv_norm_g', 'w_ukv', 'conv_w', 'conv_b', 'conv_ln_g', 'conv_ln_b', 'w_out',
        'norm2_g', 'router_w', 'router_b', 'w_gate', 'w_up', 'w_down', 'final_g']
_OUTS = [("y_prompt", (1, SEQ, D)), ("y_sample", (1, DEC_SEQ, D)),
         ("new_ckv", (1, DEPTH, SEQ, KV_LORA)), ("new_krope", (1, DEPTH, SEQ, ROPE))]


def kernel(**inputs):
    import concourse.bacc as _bacc
    from concourse.bass_utils import run_bass_kernel_spmd as _run

    nc = _bacc.Bacc("TRN2", target_bir_lowering=False, num_devices=1)
    arrays, args = {}, []
    for name in _INS:
        a = np.ascontiguousarray(inputs[name])
        arrays[f"in_{name}"] = a
        args.append(nc.dram_tensor(f"in_{name}", a.shape, mybir.dt.from_np(a.dtype), kind="ExternalInput").ap())
    a = shape_constants()
    arrays["in_consts"] = a
    args.append(nc.dram_tensor("in_consts", a.shape, FP32, kind="ExternalInput").ap())
    for name, shape in _OUTS:
        args.append(nc.dram_tensor(f"out_{name}", shape, FP32, kind="ExternalOutput").ap())
    hybrid_step_kernel(nc, *args)
    r = _run(nc, [arrays], core_ids=[0])
    return tuple(r.results[0][f"out_{name}"] for name, _ in _OUTS)
```

```python
from contextlib import ExitStack

import numpy as np

import concourse.bass as bass
from concourse import mybir

FP32 = mybir.dt.float32
INT32 = mybir.dt.int32
ALU = mybir.AluOpType
ACT = mybir.ActivationFunctionType
AXIS_X = mybir.AxisListType.X

P = 128
D = 1024
DK = D // P
DEPTH = 2
SEQ, DEC_SEQ, PAST = 128, 512, 128
GRID_W = 64
TILES = (DEC_SEQ + SEQ) // P
LAT = DEC_SEQ // P
TOK = TILES * P
HEADS, NOPE, ROPE, VH = 8, 64, 32, 64
Q_LORA, KV_LORA, CONV_C, CONV_K = 384, 256, 512, 31
QC, KC, CC = Q_LORA // P, KV_LORA // P, CONV_C // P
PAD = CONV_K // 2
QKV = Q_LORA + KV_LORA + ROPE
D_IN = QKV + 2 * CONV_C
KEYS = TOK + PAST
LAT_KEYS = DEC_SEQ + PAST
EXPERTS, GROUPS, PER_GROUP, FF = 16, 4, 4, 256
PAIRS = ROPE // 4
EPS = 1e-6
SCALE = (NOPE + ROPE) ** -0.5
MAX_BLOCKS = 2 * TOK // P + EXPERTS - 1
TABLE_BLOCKS = MAX_BLOCKS + 2
NO_ROW = 1 << 20
BIG = 1e30
ADA_CHUNKS = 6 * D // 512
CONV_EARLY = (0, 16, 16, 12)
ADA_FIRST = 4
ZPAD = 3 * PAD + TOK
CONV_OUT = TOK + PAD
UNITS = HEADS * TILES
VEC_ROWS = 48 + 8 + 8 + QC + 3 * CC
(V_BADA, V_G1, V_G2, V_QG, V_CB, V_LG, V_LB) = (0, 48, 56, 64, 64 + QC, 64 + QC + CC, 64 + QC + 2 * CC)

C_ID, C_TRI, C_ONE, C_TAB = 0, 128, 256, 384
C_KC = C_TAB + TOK
C_KS = C_KC + LAT * ROPE
C_W16 = C_KS + LAT * ROPE
C_W4 = C_W16 + EXPERTS
C_TOKID = C_W4 + GROUPS
C_SEL = C_TOKID + TILES
N_CONST = C_SEL + 2
ADA_W = 512
ADA_NEXT_W = 256
ADA_NEXT_CHUNKS = 6 * D // ADA_NEXT_W


def shape_constants():
    c = np.zeros((P, N_CONST), np.float32)
    p = np.arange(P)
    c[:, C_ID:C_ID + P] = np.eye(P)
    c[:, C_TRI:C_TRI + P] = p[:, None] < p[None, :]
    c[:, C_ONE:C_ONE + P] = 1.0
    tok = np.arange(DEC_SEQ)
    freqs = (np.float32(10000.0) ** (-np.arange(PAIRS, dtype=np.float32) / PAIRS)).astype(np.float32)
    pos = np.stack([tok // GRID_W, tok % GRID_W], 1).astype(np.float32)
    ang = pos[:, :, None] * freqs
    cos, sin = np.cos(ang).astype(np.float32), np.sin(ang).astype(np.float32)
    cos_r = np.stack([cos, cos], 2).reshape(DEC_SEQ, ROPE)
    sin_r = np.stack([-sin, sin], 2).reshape(DEC_SEQ, ROPE)
    tab = c[:, C_TAB:C_TAB + TOK]
    tab[0:NOPE + ROPE] = 1.0
    tab[NOPE:NOPE + ROPE, 0:DEC_SEQ] = cos_r.T
    tab[NOPE + ROPE:P, 0:DEC_SEQ] = sin_r.T
    c[:, C_KC:C_KC + LAT * ROPE] = cos_r.reshape(LAT, P, ROPE).transpose(1, 0, 2).reshape(P, -1)
    c[:, C_KS:C_KS + LAT * ROPE] = sin_r.reshape(LAT, P, ROPE).transpose(1, 0, 2).reshape(P, -1)
    c[:, C_W16:C_W16 + EXPERTS] = EXPERTS - np.arange(EXPERTS)
    c[:, C_W4:C_W4 + GROUPS] = GROUPS - np.arange(GROUPS)
    c[:, C_SEL:C_SEL + 2] = p[:, None] % 32 == np.arange(2)
    c[:, C_TOKID:C_TOKID + TILES] = p[:, None] + P * np.arange(TILES)
    return c


class Ring:

    def __init__(self, banks, full, empty):
        self.banks, self.full, self.empty, self.number, self.order = banks, full, empty, {}, []

    def plan(self, *keys):
        for key in keys:
            self.number[key] = len(self.order)
            self.order.append(key)

    def bank(self, key):
        return self.banks[self.number[key] % len(self.banks)]

    def open(self, pe, key):
        before = self.number[key] - len(self.banks)
        if before >= 0:
            pe.wait_ge(self.empty, before + 1)
        return self.bank(key)

    def take(self, eng, key):
        eng.wait_ge(self.full, self.number[key] + 1)
        return self.bank(key)

    def wait_full(self, eng, key):
        eng.wait_ge(self.full, self.number[key] + 1)

    def wait_empty(self, eng, key):
        eng.wait_ge(self.empty, self.number[key] + 1)


def hybrid_step_kernel(nc, x_prompt, x_sample, cache_ckv, cache_krope, c, c_ctx, w_ada, b_ada, norm1_g, w_in,
                       q_norm_g, w_uq, kv_norm_g, w_ukv, conv_w, conv_b, conv_ln_g, conv_ln_b, w_out,
                       norm2_g, router_w, router_b, w_gate, w_up, w_down, final_g, consts,
                       y_prompt, y_sample, new_ckv, new_krope):
    ctx = ExitStack()
    with ctx:
        def sb(name, cols, dt=FP32, parts=P):
            return ctx.enter_context(nc.sbuf_tensor(name, [parts, cols], dt))

        def sem(name):
            return ctx.enter_context(nc.semaphore(name))

        h2_dram = nc.dram_tensor("h2_rows", [TOK, D], FP32, kind="Internal").ap()
        y_dram = nc.dram_tensor("expert_rows", [2 * TOK, D], FP32, kind="Internal").ap()
        tables = [nc.dram_tensor(f"slot_table{l}", [TABLE_BLOCKS * P, 3], INT32, kind="Internal").ap() for l in range(DEPTH)]

        con = sb("con", N_CONST)
        ident, tri, ones = con[:, C_ID:C_ID + P], con[:, C_TRI:C_TRI + P], con[:, C_ONE:C_ONE + P]
        vec_cols = [sb(f"vecs{l}", 2 * P) for l in range(DEPTH)]
        cond = sb("cond", 32 * DK)
        cond_raw = sb("cond_raw", 2 * DK)
        ada_cols = [sb(f"adat{l}", 96) for l in range(DEPTH)]
        mod = sb("mod", 32)
        rw = sb("rw", DK * EXPERTS)
        rb = sb("rb", EXPERTS)
        eps_t = sb("eps_t", 1)
        stat = sb("stat", 64)
        idx = sb("idx", 2 * TILES, INT32)
        slot_src = sb("slot_src", 6 * TILES, INT32)
        slot_tab = sb("slot_tab", 3 * TABLE_BLOCKS, INT32)
        token_col, row_out = sb("token_col", 1, INT32), sb("row_out", 1, INT32)
        no_rows = slot_tab
        blocks = [sb(f"blocks{l}", 2 * EXPERTS + 1, INT32) for l in range(DEPTH)]
        nbf = sb("nbf", 5 * 24)
        block_total = sb("block_total", 1)
        att_stat = sb("att_stat", 4 * UNITS)

        x = sb("x", TILES * D)[:, :].rearrange("p (t d) -> p t d", t=TILES)
        W1 = sb("region_weights", DK * D_IN)
        H = sb("region_h", TILES * D)
        Q = sb("region_q", TILES * D)
        O = sb("region_o", 8576)
        BC = sb("region_bc", 6 * D)
        PR = sb("region_proj", TILES * QKV)
        CV = sb("region_conv", 3 * D)

        hT = H[:, 0:DK * TOK].rearrange("p (k t) -> p k t", k=DK)
        mixT = hT
        xn = Q[:, :].rearrange("p (t d) -> p t d", t=TILES)
        qT = Q[:, :].rearrange("p (h t) -> p h t", h=HEADS)
        h2T = Q[:, :].rearrange("p (k t) -> p k t", k=DK)
        win = W1[:, :].rearrange("p (k n) -> p k n", k=DK)
        kvg = Q[:, 0:KV_LORA]
        vec_rows = [PR[:, 1024 + 2 * P * l:1024 + 2 * P * (l + 1)] for l in range(DEPTH)]
        cond_rows = PR[:, 2048:2048 + P]
        kT = W1[:, 0:HEADS * KEYS].rearrange("p (h t) -> p h t", h=HEADS)
        base = HEADS * KEYS
        v_sb = W1[:, base:base + 6 * 512].rearrange("p (t n) -> p t n", t=6)
        base += 6 * 512
        prob = W1[:, base:base + 2 * LAT_KEYS].rearrange("p (b n) -> p b n", b=2)
        base += 2 * LAT_KEYS
        probT = W1[:, base:base + 2 * LAT_KEYS].rearrange("p (b n) -> p b n", b=2)
        base += 2 * LAT_KEYS
        kr = W1[:, base:base + 6 * P].rearrange("p (t n) -> p t n", t=6)
        base += 6 * P
        cache_sb = W1[:, base:base + KV_LORA + ROPE]
        assert base + KV_LORA + ROPE <= DK * D_IN
        EW = DK * 512 + 2 * D
        wgu = [W1[:, s * EW:s * EW + DK * 512].rearrange("p (k n) -> p k n", k=DK) for s in range(2)]
        wdn = [W1[:, s * EW + DK * 512:(s + 1) * EW].rearrange("p (k n) -> p k n", k=2) for s in range(2)]
        ada_w = [O[:, s * 4096:(s + 1) * 4096].rearrange("p (k n) -> p k n", k=DK) for s in range(2)]
        wuq = O[:, 0:3072].rearrange("p (k h n) -> p k h n", k=QC, h=HEADS)
        wk = O[:, 3072:4096].rearrange("p (k n) -> p k n", k=KC)
        wv = O[:, 4096:5120].rearrange("p (k n) -> p k n", k=KC)
        qcT = O[:, 5120:5120 + QC * TOK].rearrange("p (k t) -> p k t", k=QC)
        ckvT = O[:, 7040:7040 + KC * KEYS].rearrange("p (k t) -> p k t", k=KC)
        wout = O[:, 0:8192].rearrange("p (k n) -> p k n", k=DK)
        proj = PR[:, :].rearrange("p (t n) -> p t n", t=TILES)
        o_tok = PR[:, 0:TILES * 512].rearrange("p (t n) -> p t n", t=TILES)
        y_sb, hid = PR[:, 0:1024], PR[:, 1024:1280]
        hidT = PR[:, 1280:1536].rearrange("p (k n) -> p k n", k=2)
        silu_g = PR[:, 1536:1792]
        zpad = CV[:, 0:CC * ZPAD].rearrange("p (k n) -> p k n", k=CC)
        diag = CV[:, 0:1024].rearrange("p (b n) -> p b n", b=2)
        h2s = CV[:, 0:2048].rearrange("p (b n) -> p b n", b=2)
        res_tmp = CV[:, 2048:3072]
        xg = CV[:, 0:1024]
        xgT = CV[:, 1024:2048].rearrange("p (k n) -> p k n", k=DK)
        acc = BC[:, 0:CC * CONV_OUT].rearrange("p (k n) -> p k n", k=CC)
        sig = BC[:, 2 * D + 1024:2 * D + 1024 + 2 * TOK].rearrange("p (b n) -> p b n", b=2)
        junk = BC[:, 5 * D:6 * D]
        junk2 = PR[:, 2048:3072]
        ada_row = PR[:, 0:1024]
        ada_next = [H[:, s * 2048:(s + 1) * 2048].rearrange("p (k n) -> p k n", k=DK) for s in range(2)]
        ada_next_row = H[:, 4096:4096 + ADA_NEXT_W]
        bc = BC[:, :].rearrange("p (i n) -> p i n", i=6)
        g1_bc, a2_bc, sh2_bc = (lambda v: bc[:, v]), (lambda v: bc[:, 2 + v]), (lambda v: bc[:, 4 + v])
        g2_bc = g1_bc
        zsq = Q[:, 0:CC * CONV_OUT].rearrange("p (k n) -> p k n", k=CC)
        ln_rstd = Q[:, CC * CONV_OUT:CC * CONV_OUT + CONV_OUT]
        comb = [H[:, n * D:(n + 1) * D] for n in range(4)] + [CV[:, n * D:(n + 1) * D] for n in range(3)] \
            + [PR[:, n * D:(n + 1) * D] for n in range(3)]
        r_tmp = H[:, 4096:5120]
        final_bc = bc[:, 2]

        ps = ctx.enter_context(nc.psum_tensor("ps", [P, 8, 512], FP32))
        flat = ps[:, :, :].rearrange("p b n -> p (b n)")

        ring_a = Ring([ps[:, b] for b in range(4)], sem("act_bank_full"), sem("act_bank_empty"))
        ring_v = Ring([ps[:, b] for b in range(4, 8)], sem("dve_bank_full"), sem("dve_bank_empty"))
        x_loaded, const_loaded, rows_loaded = sem("x_loaded"), sem("const_loaded"), sem("rows_loaded")
        cond_loaded = sem("cond_loaded")
        kvg_loaded, final_loaded = sem("kvg_loaded"), sem("final_loaded")
        ada_loaded = [sem(f"ada_loaded{s}") for s in range(2)]
        win_conv_loaded, win_qkv_loaded = sem("win_conv_loaded"), sem("win_qkv_loaded")
        wuq_loaded, wukv_loaded, cache_loaded = sem("wuq_loaded"), sem("wukv_loaded"), sem("cache_loaded")
        wout_loaded = sem("wout_loaded")
        expert_loaded = [sem(f"expert_loaded{s}") for s in range(2)]
        act_step, dve_step, pool_step = sem("act_step"), sem("dve_step"), sem("pool_step")
        cond_ready, mod_ready, mod2_ready = sem("cond_ready"), sem("mod_ready"), sem("mod2_ready")
        ada_next_loaded = [sem(f"ada_next_loaded{s}") for s in range(2)]
        ada_next_full, ada_next_taken = sem("ada_next_full"), sem("ada_next_taken")
        rms_stat, xn_ready, zero_ready = sem("rms_stat"), sem("xn_ready"), sem("pad_zeroed")
        sig_ready, qkv_stat, qkv_normed = sem("sig_ready"), sem("qkv_stat"), sem("qkv_normed")
        krope_ready, wuq_swapped, k_spread = sem("krope_ready"), sem("wuq_swapped"), sem("k_spread")
        scores, att_max, att_exp = sem("scores"), sem("att_max"), sem("att_exp")
        prob_turned, probT_ready, att_out, att_out_empty = (
            sem("prob_turned"), sem("probT_ready"), sem("att_out"), sem("att_out_empty"))
        conv_step, ln_centred, ln_squared, ln_sqrt, ln_done, conv_silu = (
            sem("conv_step"), sem("ln_centred"), sem("ln_squared"), sem("ln_sqrt"), sem("ln_done"),
            sem("conv_silu"))
        diag_ready = sem("diag_ready")
        x_updated, h2_stat, h2_ready, h2_stored = sem("x_updated"), sem("h2_stat"), sem("h2_ready"), [sem("h2_stored0"), sem("h2_stored1")]
        masks_ready, slots_ready, plan_ready = sem("masks_ready"), sem("slots_ready"), sem("plan_ready")
        table_cleared, table_written = sem("table_cleared"), sem("table_written")
        tab_loaded, gathered, tokens_given = sem("tab_loaded"), sem("gathered"), sem("tokens_given")
        xT_full, xT_act, xT_dve = sem("xT_full"), sem("xT_act"), sem("xT_dve")
        gu_full, silu_ready, hid_ready = sem("gu_full"), sem("silu_ready"), sem("hid_ready")
        hidT_full, hidT_ready = sem("hidT_full"), sem("hidT_ready")
        y_full, y_act, y_dve, y_stored = sem("y_full"), sem("y_act"), sem("y_dve"), sem("y_stored")
        comb_loaded, comb_added = [sem(f"comb_loaded{t}") for t in range(TILES)], sem("comb_added")
        pool_passed, pe_passed, act_passed = sem("pool_passed"), sem("pe_passed"), sem("act_passed")
        outputs_done, final_ready = sem("outputs_done"), sem("final_ready")
        ckv_out = sem("ckv_out")

        def plan_ada(a, b):
            for ch in range(a, b):
                ring_a.plan(("ada", ch))
                ring_v.plan(("adaT", ch))

        for l in range(DEPTH):
            if l == 0:
                ring_v.plan("cond", *[(m, "vec") for m in range(DEPTH)])
                plan_ada(0, ADA_FIRST)
            for k in range(DK):
                (ring_v if k % 2 else ring_a).plan((l, "xnT", k))
            ring_a.plan((l, "xpT", 0))
            ring_v.plan((l, "xpT", 1))
            for ct in range(CC):
                ring_a.plan((l, "gate_lat", ct), (l, "gate_ctx", ct))
                ring_v.plan((l, "a_lat", ct), (l, "a_ctx", ct))
                if l == 0:
                    plan_ada(ADA_FIRST + 2 * ct, ADA_FIRST + 2 * ct + 2)
            for t in range(TILES):
                ring_a.plan((l, "qkv0", t))
                ring_v.plan((l, "qkv1", t))
            ring_a.plan(*[(l, "qcT", k) for k in range(QC)], (l, "qcT_ctx"))
            ring_v.plan(*[(l, "ckvT", k) for k in range(KC)], *[(l, "ckvT_rest", k) for k in range(KC)],
                        (l, "krT", 0), (l, "krT", 1))
            ring_v.plan(*[(l, "q", h) for h in range(HEADS)], (l, "q_ctx", 0), (l, "q_ctx", 1))
            for pr in range(HEADS // 2):
                ring_a.plan((l, "k0", pr), (l, "k1", pr))
            ring_a.plan(*[(l, "v", t) for t in range(6)])
            ring_a.plan(*[(l, "oT", k) for k in range(4)], (l, "oT_ctx"))
            ring_v.plan(*[(l, "ln", s, j) for s in range(2) for j in range(2)])
            ring_v.plan(*[(l, "bc", i, j) for i in range(6) for j in range(2)])
            for t in range(TILES):
                ring_v.plan((l, "wo", t, 0), (l, "wo", t, 1))
                ring_a.plan((l, "h2T", t, 0), (l, "h2T", t, 1))
            ring_a.plan((l, "logits"))
            ring_v.plan((l, "g2", 0, 0), (l, "g2", 0, 1), (l, "g2", 1, 0), (l, "g2", 1, 1))
            ring_v.plan((l, "slots"))

        def vec_col(l, v):
            return vec_cols[l][:, v:v + 1]

        def stores_of(l, t, parity):
            return l * ((TILES + 1 - parity) // 2) + (t + 1 - parity) // 2

        def slot_of_diag(l, n):
            if n < 0:
                return (l - 1, "g2", (n + 4) // 2, n % 2)
            return (l, "bc", n // 2, n % 2) if n < 12 else (l, "g2", (n - 12) // 2, n % 2)

        block = ctx.enter_context(nc.Block())

        @block.sync
        def _(sp):
            sp.dma_start(con[:, :], consts).then_inc(const_loaded, 16)
            sp.dma_start(cond_rows[0:DK, :], c[0, :].rearrange("(k q) -> k q", q=P)).then_inc(cond_loaded, 16)
            sp.dma_start(cond_rows[DK:2 * DK, :], c_ctx.rearrange("(k q) -> k q", q=P)).then_inc(cond_loaded, 16)
            for l in range(DEPTH):
                at = 0
                for vec in (b_ada, norm1_g, norm2_g, q_norm_g, conv_b, conv_ln_g, conv_ln_b):
                    n = vec.shape[1] // P
                    sp.dma_start(vec_rows[l][at:at + n, 0:P], vec[l].rearrange("(k q) -> k q", q=P)).then_inc(rows_loaded, 16)
                    at += n
                sp.dma_start(vec_rows[l][0:CONV_K * CC, P:2 * P], conv_w[l].rearrange("j (k q) -> (j k) q", q=P)).then_inc(rows_loaded, 16)
            wgu_dram = [w.rearrange("l e (k p) n -> l e p k n", p=P) for w in (w_gate, w_up)]
            wdn_dram = w_down.rearrange("l e (k p) n -> l e p k n", p=P)

            def load_expert(l, e, s):
                for j, w in enumerate(wgu_dram):
                    sp.dma_start(wgu[s][:, :, j * FF:(j + 1) * FF], w[l, e]).then_inc(expert_loaded[s], 16)
                sp.dma_start(wdn[s], wdn_dram[l, e]).then_inc(expert_loaded[s], 16)

            def load_ada(ch):
                if ch >= 2:
                    ring_a.wait_full(sp, ("ada", ch - 2))
                sp.dma_start(ada_w[ch % 2], w_ada[0].rearrange("(k p) n -> p k n", p=P)[:, :, ch * ADA_W:(ch + 1) * ADA_W]).then_inc(ada_loaded[ch % 2], 16)

            def load_ada_next(l, ch):
                m = l * ADA_NEXT_CHUNKS + ch
                if ch >= 2:
                    sp.wait_ge(ada_next_full, m - 1)
                sp.dma_start(ada_next[ch % 2], w_ada[l + 1].rearrange("(k p) n -> p k n", p=P)[:, :, ch * ADA_NEXT_W:(ch + 1) * ADA_NEXT_W]).then_inc(ada_next_loaded[ch % 2], 16)

            def load_attention_weights(l):
                for k in range(QC):
                    sp.dma_start(wuq[:, k, :, 0:NOPE + ROPE], w_uq[l, k * P:(k + 1) * P, :].rearrange("p (h n) -> p h n", h=HEADS)).then_inc(wuq_loaded, 16)
                for k in range(KC):
                    src = w_ukv[l, k * P:(k + 1) * P, :].rearrange("p (h n) -> p h n", h=HEADS)
                    sp.dma_start(wk[:, k, :].rearrange("p (h n) -> p h n", h=HEADS), src[:, :, 0:NOPE]).then_inc(wukv_loaded, 16)
                    sp.dma_start(wv[:, k, :].rearrange("p (h n) -> p h n", h=HEADS), src[:, :, NOPE:NOPE + VH]).then_inc(wukv_loaded, 16)

            for l in range(DEPTH):
                if l == 0:
                    load_ada(0)
                    load_ada(1)
                    sp.dma_start(x[:, 0:LAT, :], x_sample[0].rearrange("(t p) d -> p t d", p=P)).then_inc(x_loaded, 16)
                    sp.dma_start(x[:, LAT, :], x_prompt[0]).then_inc(x_loaded, 16)
                    sp.dma_start(rw[:, :].rearrange("p (k n) -> p k n", k=DK), router_w.rearrange("(k p) n -> p k n", p=P)).then_inc(x_loaded, 16)
                    sp.dma_start(rb[:, :], router_b.rearrange("(a n) -> a n", a=1).broadcast_to([P, EXPERTS])).then_inc(x_loaded, 16)
                    for ch in range(2, ADA_FIRST):
                        load_ada(ch)
                if l >= 1:
                    ring_v.wait_full(sp, (l - 1, "wo", TILES - 1, 1))
                    load_attention_weights(l)
                    last = sp.value_load(blocks[l - 1][0:1, 2 * EXPERTS - 1:2 * EXPERTS], min_val=0, max_val=100)
                    n_last = sp.value_load(blocks[l - 1][0:1, EXPERTS - 1:EXPERTS], min_val=1, max_val=5)
                    sp.wait_ge(y_full, last + n_last)
                win_dram = w_in[l].rearrange("(k p) n -> p k n", p=P)
                sp.dma_start(win[:, :, QKV:D_IN], win_dram[:, :, QKV:D_IN]).then_inc(win_conv_loaded, 16)
                if l == 0:
                    load_ada(ADA_FIRST)
                    load_ada(ADA_FIRST + 1)
                sp.dma_start(win[:, :, 0:QKV], win_dram[:, :, 0:QKV]).then_inc(win_qkv_loaded, 16)
                if l == 0:
                    for ch in range(ADA_FIRST + 2, ADA_CHUNKS):
                        load_ada(ch)
                    ring_a.wait_full(sp, ("ada", ADA_CHUNKS - 1))
                    load_attention_weights(l)
                ring_v.wait_full(sp, (l, "a_ctx", CC - 1))
                sp.dma_start(kvg, kv_norm_g[l:l + 1, :].broadcast_to([P, KV_LORA])).then_inc(kvg_loaded, 16)
                ring_v.wait_full(sp, (l, "qkv1", TILES - 1))
                sp.dma_start(cache_sb[:, 0:KV_LORA], cache_ckv[0, l]).then_inc(cache_loaded, 16)
                sp.dma_start(cache_sb[:, KV_LORA:KV_LORA + ROPE], cache_krope[0, l]).then_inc(cache_loaded, 16)
                if l + 1 < DEPTH:
                    load_ada_next(l, 0)
                    load_ada_next(l, 1)
                ring_a.wait_full(sp, (l, "v", 5))
                ring_v.wait_full(sp, (l, "q_ctx", 1))
                sp.dma_start(wout, w_out[l].rearrange("(k p) n -> p k n", p=P)).then_inc(wout_loaded, 16)
                if l + 1 < DEPTH:
                    for ch in range(2, ADA_NEXT_CHUNKS):
                        load_ada_next(l, ch)
                sp.wait_ge(att_out, UNITS * (l + 1))
                for s in range(2):
                    load_expert(l, s, s)
                sp.wait_ge(plan_ready, l + 1)
                with sp.Fori(0, EXPERTS // 2 - 1) as i:
                    for s in range(2):
                        done = sp.value_load(blocks[l][0:1, bass.ds(EXPERTS + 2 * i + s, 1)], min_val=0, max_val=100)
                        n = sp.value_load(blocks[l][0:1, bass.ds(2 * i + s, 1)], min_val=1, max_val=5)
                        sp.wait_ge(y_full, done + n)
                        load_expert(l, 2 * i + s + 2, s)
            sp.wait_ge(ckv_out, 16 * 2 * DEPTH)
            sp.wait_ge(outputs_done, 16 * TILES)

        @block.gpsimd
        def _(pool):
            steps = [0]

            def step(ins):
                steps[0] += 1
                ins.then_inc(pool_step, 1)
                pool.wait_ge(pool_step, steps[0])

            step(nc.gpsimd.memset(no_rows[:, :], NO_ROW))
            for l in range(DEPTH):
                done = y_stored if l == DEPTH - 1 else table_cleared
                pool.dma_start(tables[l].rearrange("(p r) j -> p (r j)", p=P), no_rows[:, :]).then_inc(done, 16)
            pool.wait_ge(table_cleared, 16 * (DEPTH - 1))
            pool.wait_ge(y_stored, 16)
            for l in range(DEPTH):
                if l >= 1:
                    pool.wait_ge(comb_added, l * TILES)
                for a, b in ((0, PAD), (PAD + DEC_SEQ, 2 * PAD + DEC_SEQ), (2 * PAD + TOK, ZPAD)):
                    nc.gpsimd.memset(zpad[:, :, a:b], 0.0).then_inc(zero_ready, 1)
                pool.wait_ge(wuq_loaded, 16 * QC * (l + 1))
                for half in range(2):
                    dst = wuq[:, :, :, NOPE + ROPE:P].rearrange("p k h (a s r) -> p (k h) a s r", a=2, s=2)
                    src = wuq[:, :, :, NOPE:NOPE + ROPE].rearrange("p k h (a s r) -> p (k h) a s r", a=2, s=2)
                    nc.gpsimd.tensor_copy(dst[:, :, :, half, :], src[:, :, :, 1 - half, :]).then_inc(wuq_swapped, 1)
                ring_v.wait_empty(pool, (l, "krT", 1))
                pool.wait_ge(wuq_swapped, 2 * (l + 1))
                for h in range(1, HEADS):
                    nc.gpsimd.tensor_copy(kT[NOPE:P, h, :], kT[NOPE:P, 0, :]).then_inc(k_spread, 1)
                pool.wait_ge(k_spread, (HEADS - 1) * (l + 1))
                for k in range(CC):
                    pool.wait_ge(ln_centred, CC * l + k + 1)
                    nc.gpsimd.tensor_tensor(zsq[:, k, :], acc[:, k, :], acc[:, k, :], ALU.mult).then_inc(ln_squared, 1)
                pool.wait_ge(mod2_ready, l + 1)
                ring_v.wait_full(pool, (l, "ln", 1, 1))
                n = 0
                for i in range(8):
                    part = (2, 6, 3, 5)[i // 2]
                    for j in range(2):
                        d = 16 * l + n
                        if d >= 2:
                            key = slot_of_diag(l, n - 2)
                            ring_v.wait_full(pool, key)
                        if i == 6 and j == 0:
                            for s in range(2):
                                pool.wait_ge(h2_stored[s], 16 * stores_of(l, TILES - s, s))
                            ring_a.wait_full(pool, (l, "h2T", TILES - 1, 1))
                        v = i % 2
                        if part == 6:
                            col = mod[:, 16:32].rearrange("p (k v) -> p k v", v=2)[:, 4 * j:4 * j + 4, v]
                        else:
                            col = ada_cols[l][:, :].rearrange("p (k v) -> p k v", v=2)[:, 8 * part + 4 * j:8 * part + 4 * j + 4, v]
                        nc.gpsimd.tensor_tensor(diag[:, n % 2].rearrange("p (a n) -> p a n", a=4),
                                                ident.unsqueeze(1).broadcast_to([P, 4, P]),
                                                col.unsqueeze(2).broadcast_to([P, 4, P]), ALU.mult).then_inc(diag_ready, 1)
                        n += 1
                pool.wait_ge(slots_ready, l + 1)
                for t in range(TILES):
                    for r in range(2):
                        at = 3 * (2 * t + r)
                        pool.indirect_dma_start(tables[l], bass.IndirectOffsetOnAxis(ap=idx[:, 2 * t + r:2 * t + r + 1], axis=0),
                                                slot_src[:, at:at + 3], None).then_inc(table_written, 16)
                pool.wait_ge(table_written, 16 * 2 * TILES * (l + 1))
                for s in range(2):
                    pool.wait_ge(h2_stored[s], 16 * stores_of(l, TILES - s, s))
                ring_v.wait_full(pool, (l, "g2", 1, 1))
                step(nc.gpsimd.memset(xg, 0.0))
                pool.dma_start(slot_tab[:, :], tables[l].rearrange("(p r) j -> p (r j)", p=P)).then_inc(tab_loaded, 16)
                pool.wait_ge(plan_ready, l + 1)
                start = pool.value_load(blocks[l][0:1, EXPERTS:EXPERTS + 1], min_val=0, max_val=100)
                count = pool.value_load(blocks[l][0:1, 2 * EXPERTS:2 * EXPERTS + 1], min_val=1, max_val=MAX_BLOCKS)

                def gather(n):
                    pool.wait_ge(tokens_given, n + 1)
                    pool.sem_inc(pool_passed, 1)
                    pool.indirect_dma_start(xg, None, h2_dram, bass.IndirectOffsetOnAxis(ap=token_col[:, 0:1], axis=0),
                                            bounds_check=TOK - 1, oob_is_err=False).then_inc(gathered, 16)

                gather(start + 2 * l)
                gather(start + (2 * l + 1))
                with pool.Fori(0, count) as i:
                    gather(start + i + (2 * l + 2))
                    pool.wait_ge(y_act, start + i + 2)
                    pool.wait_ge(y_dve, start + i + 2)
                    pool.sem_inc(pool_passed, 1)
                    pool.indirect_dma_start(y_dram, bass.IndirectOffsetOnAxis(ap=row_out[:, 0:1], axis=0), y_sb, None,
                                            bounds_check=2 * TOK - 1, oob_is_err=False).then_inc(y_stored, 16)

        @block.scalar
        def _(act):
            steps = [0]

            def step(ins):
                steps[0] += 1
                ins.then_inc(act_step, 1)
                act.wait_ge(act_step, steps[0])

            def row_stats(l, source):
                for t in range(TILES):
                    step(nc.scalar.activation(junk, source(t), ACT.Square, accum_out=stat[:, t:t + 1]))
                nc.scalar.activation(stat[:, 8:8 + TILES], stat[:, 0:TILES], ACT.Sqrt, scale=1.0 / D,
                                     bias=eps_t[:, 0:1]).then_inc(rms_stat, 1)

            ring_v.wait_empty(act, "cond")
            nc.scalar.activation(cond[:, :].rearrange("p (k v) -> p v k", v=32)[:, 0:2, :],
                                 cond_raw[:, :].rearrange("p (v k) -> p v k", v=2),
                                 ACT.Silu).then_inc(cond_ready, 1)
            act.sem_inc(y_act, 1)
            act.wait_ge(x_loaded, 64)

            for l in range(DEPTH):
                def ada_rows(a, b):
                    for ch in range(a, b):
                        bank = ring_a.take(act, ("ada", ch))
                        if ch >= 2:
                            ring_v.wait_full(act, ("adaT", ch - 2))
                        nc.scalar.activation(ada_row[:, (ch % 2) * ADA_W:(ch % 2 + 1) * ADA_W], bank, ACT.Copy).then_inc(ring_a.empty, 1)

                if l == 0:
                    ada_rows(0, ADA_FIRST)
                if l >= 1:
                    act.wait_ge(comb_added, TILES * l)
                row_stats(l, lambda t: x[:, t, :])
                act.wait_ge(mod_ready, l + 1)

                def modulate(k, v, dst, src):
                    return nc.scalar.activation(dst, src, ACT.Identity, scale=mod[:, 2 * k + v:2 * k + v + 1],
                                                bias=ada_cols[l][:, 2 * k + v:2 * k + v + 1])

                for k in range(0, DK, 2):
                    bank = ring_a.take(act, (l, "xnT", k))
                    modulate(k, 0, hT[:, k, 0:DEC_SEQ], bank).then_inc(ring_a.empty, 1)
                bank = ring_a.take(act, (l, "xpT", 0))
                for k in range(4):
                    ins = modulate(k, 1, hT[:, k, DEC_SEQ:TOK], bank[:, k * P:(k + 1) * P])
                ins.then_inc(ring_a.empty, 1)
                for ct in range(CC):
                    if ct >= 2 or l >= 1:
                        ring_v.wait_empty(act, (l, "a_ctx", ct - 2) if ct >= 2 else (l - 1, "a_ctx", ct + 2))
                    for name, a, b in (("gate_lat", 0, DEC_SEQ), ("gate_ctx", DEC_SEQ, TOK)):
                        bank = ring_a.take(act, (l, name, ct))
                        nc.scalar.activation(sig[:, ct % 2, a:b], bank[:, 0:b - a], ACT.Sigmoid).then_inc(ring_a.empty, 1)
                    if l == 0:
                        ada_rows(ADA_FIRST + 2 * ct, ADA_FIRST + 2 * ct + 2)
                for t in range(TILES):
                    bank = ring_a.take(act, (l, "qkv0", t))
                    nc.scalar.activation(proj[:, t, 0:512], bank, ACT.Copy).then_inc(ring_a.empty, 1)
                for t in range(TILES):
                    ring_a.wait_empty(act, (l, "qkv0", t))
                    ring_v.wait_empty(act, (l, "qkv1", t))
                    step(nc.scalar.activation(junk[:, 0:Q_LORA], proj[:, t, 0:Q_LORA], ACT.Square, accum_out=stat[:, 16 + t:17 + t]))
                    step(nc.scalar.activation(junk[:, 0:KV_LORA], proj[:, t, Q_LORA:Q_LORA + KV_LORA], ACT.Square, accum_out=stat[:, 24 + t:25 + t]))
                nc.scalar.activation(stat[:, 32:32 + TILES], stat[:, 16:16 + TILES], ACT.Sqrt, scale=1.0 / Q_LORA,
                                     bias=eps_t[:, 0:1]).then_inc(qkv_stat, 1)
                nc.scalar.activation(stat[:, 40:40 + TILES], stat[:, 24:24 + TILES], ACT.Sqrt, scale=1.0 / KV_LORA,
                                     bias=eps_t[:, 0:1]).then_inc(qkv_stat, 1)
                act.wait_ge(qkv_normed, TILES * (l + 1))
                act.dma_start(new_ckv[0, l], proj[:, LAT, Q_LORA:Q_LORA + KV_LORA]).then_inc(ckv_out, 16)
                act.dma_start(new_krope[0, l], proj[:, LAT, Q_LORA + KV_LORA:QKV]).then_inc(ckv_out, 16)
                for k in range(QC):
                    bank = ring_a.take(act, (l, "qcT", k))
                    nc.scalar.activation(qcT[:, k, 0:DEC_SEQ], bank, ACT.Copy, scale=vec_col(l, V_QG + k)).then_inc(ring_a.empty, 1)
                bank = ring_a.take(act, (l, "qcT_ctx"))
                for k in range(QC):
                    ins = nc.scalar.activation(qcT[:, k, DEC_SEQ:TOK], bank[:, k * P:(k + 1) * P], ACT.Copy, scale=vec_col(l, V_QG + k))
                ins.then_inc(ring_a.empty, 1)
                for pr in range(HEADS // 2):
                    for name, a, b in (("k0", 0, 512), ("k1", 512, KEYS)):
                        bank = ring_a.take(act, (l, name, pr))
                        nc.scalar.activation(kT[0:NOPE, 2 * pr, a:b], bank[0:NOPE, 0:b - a], ACT.Copy)
                        nc.scalar.activation(kT[0:NOPE, 2 * pr + 1, a:b], bank[NOPE:P, 0:b - a], ACT.Copy).then_inc(ring_a.empty, 1)
                for t in range(6):
                    bank = ring_a.take(act, (l, "v", t))
                    nc.scalar.activation(v_sb[:, t, :], bank, ACT.Copy).then_inc(ring_a.empty, 1)

                def exponential(i):
                    n = LAT_KEYS if i % TILES < LAT else SEQ
                    u = UNITS * l + i
                    act.wait_ge(att_max, u + 1)
                    if i >= 2:
                        act.wait_ge(prob_turned, u - 1)
                    nc.scalar.activation(prob[:, i % 2, 0:n], flat[:, 1024 * (i % 2):1024 * (i % 2) + n], ACT.Exp,
                                         bias=att_stat[:, UNITS + i:UNITS + i + 1], scale=SCALE,
                                         accum_out=att_stat[:, 2 * UNITS + i:2 * UNITS + i + 1]).then_inc(att_exp, 1)

                def turned(i):
                    n = LAT_KEYS if i % TILES < LAT else SEQ
                    u = UNITS * l + i
                    act.wait_ge(prob_turned, u + 1)
                    if i >= 2:
                        act.wait_ge(att_out, u - 1)
                    nc.scalar.activation(probT[:, i % 2, 0:n], flat[:, 2048:2048 + n], ACT.Copy).then_inc(probT_ready, 1)

                exponential(0)
                for i in range(UNITS):
                    if i + 1 < UNITS:
                        exponential(i + 1)
                    if l + 1 < DEPTH and 1 <= i <= ADA_NEXT_CHUNKS:
                        act.wait_ge(ada_next_full, ADA_NEXT_CHUNKS * l + i)
                        act.wait_ge(att_out, UNITS * l + i)
                        nc.scalar.activation(ada_next_row, ps[:, 7, 0:ADA_NEXT_W], ACT.Copy).then_inc(ada_next_taken, 1)
                    turned(i)
                for k in range(4):
                    bank = ring_a.take(act, (l, "oT", k))
                    nc.scalar.activation(mixT[:, k, 0:DEC_SEQ], bank, ACT.Copy).then_inc(ring_a.empty, 1)
                bank = ring_a.take(act, (l, "oT_ctx"))
                nc.scalar.activation(mixT[:, 0:4, DEC_SEQ:TOK], bank.rearrange("p (k n) -> p k n", k=4), ACT.Copy).then_inc(ring_a.empty, 1)
                for j, (a, b) in enumerate(((0, 512), (512, CONV_OUT))):
                    ring_v.wait_full(act, (l, "ln", 1, j))
                    nc.scalar.activation(ln_rstd[:, a:b], ring_v.bank((l, "ln", 1, j))[:, 0:b - a], ACT.Sqrt,
                                         scale=1.0 / CONV_C, bias=eps_t[:, 0:1]).then_inc(ln_sqrt, 1)
                for k in range(CC):
                    act.wait_ge(ln_done, CC * l + k + 1)
                    for src, dst in (((0, 512), (0, 512)), ((512 + PAD, CONV_OUT), (512, TOK))):
                        nc.scalar.activation(mixT[:, 4 + k, dst[0]:dst[1]], acc[:, k, src[0]:src[1]], ACT.Silu,
                                             scale=vec_col(l, V_LG + k), bias=vec_col(l, V_LB + k)).then_inc(conv_silu, 1)

                def turned_h2(t):
                    for j in range(2):
                        bank = ring_a.take(act, (l, "h2T", t, j))
                        nc.scalar.activation(h2T[:, 4 * j:4 * j + 4, t * P:(t + 1) * P],
                                             bank.rearrange("p (k n) -> p k n", k=4), ACT.Copy).then_inc(ring_a.empty, 1)

                for t in range(TILES):
                    act.wait_ge(x_updated, 2 * (TILES * l + t + 1))
                    step(nc.scalar.activation(junk2, x[:, t, :], ACT.Square, accum_out=stat[:, 48 + t:49 + t]))
                    nc.scalar.activation(stat[:, 56 + t:57 + t], stat[:, 48 + t:49 + t], ACT.Sqrt, scale=1.0 / D,
                                         bias=eps_t[:, 0:1]).then_inc(h2_stat, 1)
                    act.wait_ge(h2_ready, TILES * l + t + 1)
                    act.dma_start(h2_dram[t * P:(t + 1) * P, :], h2s[:, t % 2]).then_inc(h2_stored[t % 2], 16)
                    if t >= 1:
                        turned_h2(t - 1)
                turned_h2(TILES - 1)
                bank = ring_a.take(act, (l, "logits"))
                nc.scalar.activation(r_tmp[:, 0:80], bank[:, 0:80], ACT.Sigmoid).then_inc(ring_a.empty, 1)

                act.wait_ge(plan_ready, l + 1)
                start = act.value_load(blocks[l][0:1, EXPERTS:EXPERTS + 1], min_val=0, max_val=100)
                count = act.value_load(blocks[l][0:1, 2 * EXPERTS:2 * EXPERTS + 1], min_val=1, max_val=MAX_BLOCKS)

                def turn(n):
                    act.wait_ge(xT_full, n + 1)
                    nc.scalar.activation(xgT[:, 0:4, :], ps[:, 0].rearrange("p (k n) -> p k n", k=4), ACT.Copy).then_inc(xT_act, 1)

                turn(start + l)
                with act.Fori(0, count) as i:
                    g = start + i
                    act.wait_ge(gu_full, g + 1)
                    nc.scalar.activation(silu_g, ps[:, 2, 0:FF], ACT.Silu).then_inc(silu_ready, 1)
                    turn(g + l + 1)
                    act.wait_ge(y_full, g + 1)
                    act.wait_ge(y_stored, 16 * g + 16)
                    nc.scalar.activation(y_sb[:, 0:512], ps[:, 4], ACT.Copy).then_inc(y_act, 1)
                act.wait_ge(y_stored, (start + count) * 16 + 16)
                act.sem_inc(act_passed, 1)
                for t in range(TILES):
                    for r in range(2):
                        act.dma_start(comb[2 * t + r], y_dram[r * TOK + t * P:r * TOK + (t + 1) * P, :]).then_inc(comb_loaded[t], 16)
            act.wait_ge(comb_added, TILES * DEPTH)
            act.dma_start(final_bc, final_g.rearrange("(a n) -> a n", a=1).broadcast_to([P, D])).then_inc(final_loaded, 16)
            row_stats(DEPTH, lambda t: x[:, t, :])
            for t in range(TILES):
                act.wait_ge(final_ready, t + 1)
                act.dma_start(y_sample[0, t * P:(t + 1) * P, :] if t < LAT else y_prompt[0], xn[:, t, :]).then_inc(outputs_done, 16)

        @block.vector
        def _(dve):
            steps = [0]

            def step(ins):
                steps[0] += 1
                ins.then_inc(dve_step, 1)
                dve.wait_ge(dve_step, steps[0])

            def tt(out, a, b, op):
                return nc.vector.tensor_tensor(out, a, b, op)

            step(nc.vector.memset(eps_t[:, :], EPS))
            step(nc.vector.memset(block_total[:, :], 0.0))
            step(nc.vector.memset(nbf[:, :], 0.0))
            step(nc.vector.memset(cond[:, :], 0.0))
            bank = ring_v.take(dve, "cond")
            nc.vector.tensor_copy(cond_raw[:, :], bank[:, 0:2 * DK]).then_inc(ring_v.empty, 1)
            dve.sem_inc(y_dve, 1)
            for l in range(DEPTH):
                bank = ring_v.take(dve, (l, "vec"))
                step(nc.vector.tensor_copy(vec_cols[l][:, 0:VEC_ROWS], bank[:, 0:VEC_ROWS]))
                nc.vector.tensor_copy(vec_cols[l][:, P:P + CONV_K * CC], bank[:, P:P + CONV_K * CC]).then_inc(ring_v.empty, 1)
            ring_v.wait_empty(dve, (DEPTH - 1, "vec"))
            mod3 = mod[:, :].rearrange("p (k v) -> p k v", v=2)

            for l in range(DEPTH):
                vecs = vec_cols[l]
                adat3 = ada_cols[l][:, :].rearrange("p (k v) -> p k v", v=2)

                def ada_columns(a, b):
                    for ch in range(a, b):
                        bank = ring_v.take(dve, ("adaT", ch))
                        tt(adat3[:, 4 * ch:4 * ch + 4, :], bank[:, 0:8].rearrange("p (k v) -> p k v", v=2),
                           vecs[:, V_BADA + 4 * ch:V_BADA + 4 * ch + 4].unsqueeze(2).broadcast_to([P, 4, 2]),
                           ALU.add).then_inc(ring_v.empty, 1)

                def norm_gains(i, done):
                    part, gains = ((1, V_G1), (4, V_G2))[i]
                    step(nc.vector.tensor_scalar(mod3[:, 8 * i:8 * i + 8, :], adat3[:, 8 * part:8 * part + 8, :], 1.0, None, ALU.add))
                    tt(mod3[:, 8 * i:8 * i + 8, :], mod3[:, 8 * i:8 * i + 8, :],
                       vecs[:, gains:gains + 8].unsqueeze(2).broadcast_to([P, 8, 2]), ALU.mult).then_inc(done, 1)

                if l == 0:
                    ada_columns(0, ADA_FIRST)
                    ring_v.wait_empty(dve, ("adaT", ADA_FIRST - 1))
                norm_gains(0, mod_ready)
                dve.wait_ge(mod_ready, l + 1)
                dve.wait_ge(rms_stat, l + 1)
                step(nc.vector.reciprocal(stat[:, 8:8 + TILES], stat[:, 8:8 + TILES]))
                for t in range(TILES):
                    nc.vector.tensor_scalar(xn[:, t, :], x[:, t, :], stat[:, 8 + t:9 + t], None, ALU.mult).then_inc(xn_ready, 1)

                def modulate(k, v, dst, src):
                    return nc.vector.tensor_scalar(dst, src, mod[:, 2 * k + v:2 * k + v + 1],
                                                   ada_cols[l][:, 2 * k + v:2 * k + v + 1], ALU.mult, ALU.add)

                for k in range(1, DK, 2):
                    bank = ring_v.take(dve, (l, "xnT", k))
                    modulate(k, 0, hT[:, k, 0:DEC_SEQ], bank).then_inc(ring_v.empty, 1)
                bank = ring_v.take(dve, (l, "xpT", 1))
                for k in range(4):
                    ins = modulate(4 + k, 1, hT[:, 4 + k, DEC_SEQ:TOK], bank[:, k * P:(k + 1) * P])
                ins.then_inc(ring_v.empty, 1)
                conv_list = [(ct, j) for pair in range(CC // 2) for j in range(CONV_K) for ct in (2 * pair, 2 * pair + 1)]
                conv_at = [0]

                def conv(n):
                    for ct, j in conv_list[conv_at[0]:conv_at[0] + n]:
                        m = conv_at[0]
                        w = vecs[:, P + j * CC + ct:P + j * CC + ct + 1]
                        if j == 0:
                            ring_v.wait_empty(dve, (l, "a_ctx", ct))
                            ins = nc.vector.tensor_scalar(acc[:, ct, :], zpad[:, ct, 0:CONV_OUT], w, vec_col(l, V_CB + ct), ALU.mult, ALU.add)
                        else:
                            dve.wait_ge(conv_step, l * len(conv_list) + m - 1)
                            ins = nc.vector.scalar_tensor_tensor(acc[:, ct, :], zpad[:, ct, j:j + CONV_OUT], w, acc[:, ct, :], ALU.mult, ALU.add)
                        ins.then_inc(conv_step, 1)
                        conv_at[0] += 1

                dve.wait_ge(zero_ready, 3 * (l + 1))
                for ct in range(CC):
                    for name, gate, a, b, at in (("a_lat", "gate_lat", 0, DEC_SEQ, PAD), ("a_ctx", "gate_ctx", DEC_SEQ, TOK, 2 * PAD)):
                        bank = ring_v.take(dve, (l, name, ct))
                        ring_a.wait_empty(dve, (l, gate, ct))
                        tt(zpad[:, ct, a + at:b + at], bank[:, 0:b - a], sig[:, ct % 2, a:b], ALU.mult).then_inc(ring_v.empty, 1)
                    if l == 0:
                        ada_columns(ADA_FIRST + 2 * ct, ADA_FIRST + 2 * ct + 2)
                    conv(CONV_EARLY[ct])
                if l == 0:
                    ring_v.wait_empty(dve, ("adaT", ADA_CHUNKS - 1))
                norm_gains(1, mod2_ready)

                for t in range(TILES):
                    bank = ring_v.take(dve, (l, "qkv1", t))
                    nc.vector.tensor_copy(proj[:, t, 512:QKV], bank[:, 0:QKV - 512]).then_inc(ring_v.empty, 1)
                    conv(8)
                dve.wait_ge(qkv_stat, 2 * (l + 1))
                step(nc.vector.reciprocal(stat[:, 32:32 + TILES], stat[:, 32:32 + TILES]))
                step(nc.vector.reciprocal(stat[:, 40:40 + TILES], stat[:, 40:40 + TILES]))
                dve.wait_ge(kvg_loaded, 16 * (l + 1))
                for t in range(TILES):
                    nc.vector.tensor_scalar(proj[:, t, 0:Q_LORA], proj[:, t, 0:Q_LORA], stat[:, 32 + t:33 + t], None, ALU.mult)
                    nc.vector.scalar_tensor_tensor(proj[:, t, Q_LORA:Q_LORA + KV_LORA], proj[:, t, Q_LORA:Q_LORA + KV_LORA],
                                                   stat[:, 40 + t:41 + t], kvg, ALU.mult, ALU.mult).then_inc(qkv_normed, 1)
                step(nc.vector.memset(kr[:, :, 0:NOPE], 0.0))
                kin = proj[:, 0:LAT, Q_LORA + KV_LORA:QKV]
                kcos = con[:, C_KC:C_KC + LAT * ROPE].rearrange("p (t n) -> p t n", t=LAT)
                ksin = con[:, C_KS:C_KS + LAT * ROPE].rearrange("p (t n) -> p t n", t=LAT)
                half = lambda ap, s: ap.rearrange("p t (a s r) -> p t a s r", a=2, s=2)[:, :, :, s, :]
                k1, k2 = kr[:, 0:LAT, NOPE:NOPE + ROPE], kr[:, 0:LAT, NOPE + ROPE:P]
                step(tt(k1, kin, kcos, ALU.mult))
                step(tt(half(k2, 0), half(kin, 1), half(ksin, 0), ALU.mult))
                step(tt(half(k2, 1), half(kin, 0), half(ksin, 1), ALU.mult))
                step(tt(k1, k1, k2, ALU.add))
                step(nc.vector.tensor_copy(k2, k1))
                dve.wait_ge(cache_loaded, 32 * (l + 1))
                for s in range(2):
                    a = NOPE + s * ROPE
                    step(nc.vector.tensor_copy(kr[:, 4, a:a + ROPE], cache_sb[:, KV_LORA:KV_LORA + ROPE]))
                    ins = nc.vector.tensor_copy(kr[:, 5, a:a + ROPE], proj[:, LAT, Q_LORA + KV_LORA:QKV])
                    if s == 0:
                        step(ins)
                ins.then_inc(krope_ready, 1)
                for k in range(KC):
                    bank = ring_v.take(dve, (l, "ckvT", k))
                    nc.vector.tensor_copy(ckvT[:, k, 0:DEC_SEQ], bank).then_inc(ring_v.empty, 1)
                for k in range(KC):
                    bank = ring_v.take(dve, (l, "ckvT_rest", k))
                    nc.vector.tensor_copy(ckvT[:, k, DEC_SEQ:KEYS], bank[:, 0:256]).then_inc(ring_v.empty, 1)
                bank = ring_v.take(dve, (l, "krT", 0))
                nc.vector.tensor_copy(kT[NOPE:P, 0, 0:512], bank[NOPE:P, :]).then_inc(ring_v.empty, 1)
                bank = ring_v.take(dve, (l, "krT", 1))
                nc.vector.tensor_copy(kT[NOPE:P, 0, 512:KEYS], bank[NOPE:P, 0:256]).then_inc(ring_v.empty, 1)
                tab = con[:, C_TAB:C_TAB + TOK]
                for h in range(HEADS):
                    bank = ring_v.take(dve, (l, "q", h))
                    tt(qT[:, h, 0:DEC_SEQ], bank, tab[:, 0:DEC_SEQ], ALU.mult).then_inc(ring_v.empty, 1)
                    conv(2)
                for j in range(2):
                    bank = ring_v.take(dve, (l, "q_ctx", j))
                    tt(qT[:, 4 * j:4 * j + 4, DEC_SEQ:TOK], bank.rearrange("p (h n) -> p h n", h=4),
                       tab[:, DEC_SEQ:TOK].unsqueeze(1).broadcast_to([P, 4, P]), ALU.mult).then_inc(ring_v.empty, 1)
                def maximum(i):
                    n = LAT_KEYS if i % TILES < LAT else SEQ
                    dve.wait_ge(scores, UNITS * l + i + 1)
                    step(nc.vector.reduce_max(att_stat[:, i:i + 1], flat[:, 1024 * (i % 2):1024 * (i % 2) + n], AXIS_X))
                    nc.vector.tensor_scalar(att_stat[:, UNITS + i:UNITS + i + 1], att_stat[:, i:i + 1], -SCALE, None, ALU.mult).then_inc(att_max, 1)

                def output(i):
                    h, t = divmod(i, TILES)
                    dve.wait_ge(att_out, UNITS * l + i + 1)
                    step(nc.vector.reciprocal(att_stat[:, 3 * UNITS + i:3 * UNITS + i + 1], att_stat[:, 2 * UNITS + i:2 * UNITS + i + 1]))
                    if l + 1 < DEPTH and 1 <= i <= ADA_NEXT_CHUNKS:
                        k = 2 * (i - 1)
                        tt(ada_cols[l + 1][:, 2 * k:2 * k + 4].rearrange("p (k v) -> p k v", v=2),
                           ps[:, 6, VH:VH + 4].rearrange("p (k v) -> p k v", v=2),
                           vec_cols[l + 1][:, V_BADA + k:V_BADA + k + 2].unsqueeze(2).broadcast_to([P, 2, 2]), ALU.add)
                    nc.vector.tensor_scalar(o_tok[:, t, h * VH:(h + 1) * VH], ps[:, 6, 0:VH],
                                            att_stat[:, 3 * UNITS + i:3 * UNITS + i + 1], None, ALU.mult).then_inc(att_out_empty, 1)

                dve.wait_ge(ckv_out, 32 * (l + 1))
                for i in range(UNITS):
                    maximum(i)
                    if i >= 2:
                        output(i - 2)
                    conv(1)
                output(UNITS - 2)
                output(UNITS - 1)
                conv(len(conv_list))
                dve.wait_ge(conv_step, (l + 1) * len(conv_list))
                halves = ((0, 512), (512, CONV_OUT))
                for j, (a, b) in enumerate(halves):
                    bank = ring_v.take(dve, (l, "ln", 0, j))
                    for k in range(CC):
                        ins = nc.vector.scalar_tensor_tensor(acc[:, k, a:b], bank[:, 0:b - a], -1.0 / CONV_C, acc[:, k, a:b], ALU.mult, ALU.add)
                        if j == 0:
                            if k == CC - 1:
                                ins.then_inc(ring_v.empty, 1)
                        elif k < CC - 1:
                            ins.then_inc(ln_centred, 1)
                        else:
                            step(ins)
                dve.sem_inc(ln_centred, 1)
                dve.sem_inc(ring_v.empty, 1)
                for j, (a, b) in enumerate(halves):
                    dve.wait_ge(ln_sqrt, 2 * l + j + 1)
                    step(nc.vector.reciprocal(ln_rstd[:, a:b], ln_rstd[:, a:b]))
                    dve.sem_inc(ring_v.empty, 1)
                for k in range(CC):
                    tt(acc[:, k, :], acc[:, k, :], ln_rstd, ALU.mult).then_inc(ln_done, 1)
                dve.wait_ge(conv_silu, 2 * CC * (l + 1))
                for i in range(6):
                    for j in range(2):
                        bank = ring_v.take(dve, (l, "bc", i, j))
                        nc.vector.tensor_copy(bc[:, i, j * 512:(j + 1) * 512], bank).then_inc(ring_v.empty, 1)
                ring_v.wait_empty(dve, (l, "bc", 5, 1))
                for t in range(TILES):
                    v = 0 if t < LAT else 1
                    for j in range(2):
                        cols = slice(j * 512, (j + 1) * 512)
                        bank = ring_v.take(dve, (l, "wo", t, j))
                        tt(res_tmp[:, cols], bank, g1_bc(v)[:, cols], ALU.mult).then_inc(ring_v.empty, 1)
                        ring_v.wait_empty(dve, (l, "wo", t, j))
                        tt(x[:, t, cols], x[:, t, cols], res_tmp[:, cols], ALU.add).then_inc(x_updated, 1)
                    dve.wait_ge(h2_stat, TILES * l + t + 1)
                    step(nc.vector.reciprocal(stat[:, 56 + t:57 + t], stat[:, 56 + t:57 + t]))
                    if t >= 2:
                        dve.wait_ge(h2_stored[t % 2], 16 * stores_of(l, t, t % 2))
                        ring_a.wait_full(dve, (l, "h2T", t - 2, 1))
                    step(nc.vector.scalar_tensor_tensor(h2s[:, t % 2], x[:, t, :], stat[:, 56 + t:57 + t], a2_bc(v), ALU.mult, ALU.mult))
                    tt(h2s[:, t % 2], h2s[:, t % 2], sh2_bc(v), ALU.add).then_inc(h2_ready, 1)

                cur = [80]

                def temp(n):
                    a = cur[0]
                    cur[0] += n
                    return r_tmp[:, a:a + n]

                t16 = lambda ap: ap.rearrange("p (t e) -> p t e", t=TILES)
                over16 = lambda ap, n=EXPERTS: ap.unsqueeze(2).broadcast_to([P, TILES, n])
                aff = t16(r_tmp[:, 0:80])
                w16 = con[:, C_W16:C_W16 + EXPERTS].unsqueeze(1).broadcast_to([P, TILES, EXPERTS])
                w4 = con[:, C_W4:C_W4 + GROUPS].unsqueeze(1).broadcast_to([P, TILES, GROUPS])
                ring_a.wait_empty(dve, (l, "logits"))
                sel = temp(80)
                step(tt(t16(sel), aff, rb[:, :].unsqueeze(1).broadcast_to([P, TILES, EXPERTS]), ALU.add))
                TG = TILES * GROUPS
                s4 = sel.rearrange("p (g m) -> p g m", m=PER_GROUP)
                sums = temp(TG * 6).rearrange("p (g m) -> p g m", m=6)
                for n, m, at in ((3, 3, 0), (2, 2, 3), (1, 1, 5)):
                    step(tt(sums[:, :, at:at + n], s4[:, :, 0:n], s4[:, :, m:m + 1].broadcast_to([P, TG, n]), ALU.add))
                score = temp(TG)
                step(nc.vector.reduce_max(score, sums, AXIS_X))

                def first_max(values, weights, out, width):
                    top = temp(TILES)
                    v3 = values.rearrange("p (t e) -> p t e", t=TILES)
                    o3 = out.rearrange("p (t e) -> p t e", t=TILES)
                    step(nc.vector.reduce_max(top, v3, AXIS_X))
                    step(tt(o3, v3, over16(top, width), ALU.is_equal))
                    step(tt(o3, o3, weights, ALU.mult))
                    step(nc.vector.reduce_max(top, o3, AXIS_X))
                    step(tt(o3, o3, over16(top, width), ALU.is_equal))

                in_group = temp(TG)
                first_max(score, w4, in_group, GROUPS)
                outside = temp(TG)
                step(nc.vector.tensor_scalar(outside, in_group, 1.0, BIG, ALU.subtract, ALU.mult))
                step(tt(s4, s4, in_group.unsqueeze(2).broadcast_to([P, TG, PER_GROUP]), ALU.mult))
                step(tt(s4, s4, outside.unsqueeze(2).broadcast_to([P, TG, PER_GROUP]), ALU.add))
                hot = [temp(80), temp(80)]
                first_max(sel, w16, hot[0], EXPERTS)
                step(nc.vector.scalar_tensor_tensor(sel, hot[0], -2 * BIG, sel, ALU.mult, ALU.add))
                first_max(sel, w16, hot[1], EXPERTS)
                both = temp(80)
                tt(both, hot[0], hot[1], ALU.add).then_inc(masks_ready, 1)
                dve.wait_ge(masks_ready, l + 1)
                top_aff, total, prod = temp(2 * TILES), temp(TILES), temp(80)
                for r in range(2):
                    step(tt(t16(prod), aff, t16(hot[r]), ALU.mult))
                    step(nc.vector.reduce_sum(top_aff[:, r * TILES:(r + 1) * TILES], t16(prod), AXIS_X))
                step(tt(total, top_aff[:, 0:TILES], top_aff[:, TILES:2 * TILES], ALU.add))
                step(nc.vector.reciprocal(total, total))
                src4 = slot_src[:, :].rearrange("p (t r j) -> p t r j", r=2, j=3)
                for r in range(2):
                    step(nc.vector.tensor_scalar(src4[:, :, r, 2], con[:, C_TOKID:C_TOKID + TILES], float(r * TOK), None, ALU.add))
                    step(tt(src4[:, :, r, 1].bitcast(FP32), top_aff[:, r * TILES:(r + 1) * TILES], total, ALU.mult))
                    step(nc.vector.tensor_copy(src4[:, :, r, 0], con[:, C_TOKID:C_TOKID + TILES]))
                for v in range(2):
                    for j in range(2):
                        bank = ring_v.take(dve, (l, "g2", v, j))
                        nc.vector.tensor_copy(g2_bc(v)[:, j * 512:(j + 1) * 512], bank).then_inc(ring_v.empty, 1)
                bank = ring_v.take(dve, (l, "slots"))
                counts = bank[:, 80:96]
                row = lambda i: nbf[:, 24 * i + 8:24 * i + 24]
                row_shift = lambda i, s: nbf[:, 24 * i + 8 - s:24 * i + 24 - s]
                step(nc.vector.tensor_scalar(row(0), counts, float(P) + 0.5, 1.0, ALU.is_gt, ALU.add))
                for m in range(2, TOK // P):
                    step(nc.vector.scalar_tensor_tensor(row(0), counts, float(m * P) + 0.5, row(0), ALU.is_gt, ALU.add))
                step(tt(row(1), row(0), row_shift(0, 1), ALU.add))
                step(tt(row(2), row(1), row_shift(1, 2), ALU.add))
                step(tt(row(1), row(2), row_shift(2, 4), ALU.add))
                step(tt(row(2), row(1), row_shift(1, 8), ALU.add))
                step(tt(row(3), row(2), row(0), ALU.subtract))
                place = temp(80)
                step(nc.vector.tensor_scalar(row(1), row(3), float(P), None, ALU.mult))
                step(tt(t16(place), t16(bank[:, 0:80]), row(1).unsqueeze(1).broadcast_to([P, TILES, EXPERTS]), ALU.add))
                found = temp(TILES)
                idx3 = idx[:, :].rearrange("p (t r) -> p t r", r=2)
                for r in range(2):
                    step(tt(t16(prod), t16(place), t16(hot[r]), ALU.mult))
                    step(nc.vector.reduce_sum(found, t16(prod), AXIS_X))
                    step(nc.vector.tensor_copy(idx3[:, :, r], found))
                part_of = temp(2 * TILES).bitcast(INT32)
                step(nc.vector.tensor_scalar(part_of, idx[:, :], P - 1, None, ALU.bitwise_and))
                step(nc.vector.tensor_scalar(idx[:, :], idx[:, :], 7, None, ALU.logical_shift_right))
                ins = nc.vector.scalar_tensor_tensor(idx[:, :], part_of, float(TABLE_BLOCKS), idx[:, :], ALU.mult, ALU.add)
                ins.then_inc(slots_ready, 1)
                step(nc.vector.tensor_copy(blocks[l][0:1, 0:EXPERTS], row(0)[0:1]))
                step(nc.vector.tensor_scalar(blocks[l][0:1, EXPERTS:2 * EXPERTS], row(3)[0:1], block_total[0:1, 0:1], None, ALU.add))
                step(nc.vector.tensor_copy(blocks[l][0:1, 2 * EXPERTS:2 * EXPERTS + 1], row(2)[0:1, EXPERTS - 1:EXPERTS]))
                step(tt(block_total[0:1, 0:1], block_total[0:1, 0:1], row(2)[0:1, EXPERTS - 1:EXPERTS], ALU.add))
                dve.sem_inc(plan_ready, 1)
                dve.sem_inc(ring_v.empty, 1)

                start = dve.value_load(blocks[l][0:1, EXPERTS:EXPERTS + 1], min_val=0, max_val=100)
                count = dve.value_load(blocks[l][0:1, 2 * EXPERTS:2 * EXPERTS + 1], min_val=1, max_val=MAX_BLOCKS)

                tab3 = slot_tab[:, :].rearrange("p (b j) -> p b j", j=3)

                def give_tokens(i):
                    nc.vector.tensor_copy(token_col[:, :], tab3[:, bass.ds(i, 1), 0]).then_inc(tokens_given, 1)

                def turn(n):
                    dve.wait_ge(xT_full, n + 1)
                    nc.vector.tensor_copy(xgT[:, 4:8, :], ps[:, 1].rearrange("p (k n) -> p k n", k=4)).then_inc(xT_dve, 1)

                dve.wait_ge(tab_loaded, 16 * (l + 1))
                give_tokens(0)
                turn(start + l)
                give_tokens(1)
                with dve.Fori(0, count) as i:
                    g = start + i
                    dve.wait_ge(silu_ready, g + 1)
                    nc.vector.scalar_tensor_tensor(hid, ps[:, 2, FF:2 * FF], tab3[:, bass.ds(i, 1), 1].bitcast(FP32), silu_g, ALU.mult, ALU.mult).then_inc(hid_ready, 1)
                    dve.wait_ge(hidT_full, g + 1)
                    nc.vector.tensor_copy(hidT, ps[:, 3, 0:256].rearrange("p (k n) -> p k n", k=2)).then_inc(hidT_ready, 1)
                    turn(g + (l + 1))
                    give_tokens(i + 2)
                    dve.wait_ge(y_stored, 16 * g + 16)
                    nc.vector.tensor_copy(row_out[:, :], tab3[:, bass.ds(i, 1), 2])
                    dve.wait_ge(y_full, g + 1)
                    nc.vector.tensor_copy(y_sb[:, 512:1024], ps[:, 5]).then_inc(y_dve, 1)
                for t in range(TILES):
                    v = 0 if t < LAT else 1
                    a, b2 = comb[2 * t], comb[2 * t + 1]
                    dve.wait_ge(comb_loaded[t], 32 * (l + 1))
                    step(tt(a, a, b2, ALU.add))
                    step(tt(a, a, g2_bc(v), ALU.mult))
                    tt(x[:, t, :], x[:, t, :], a, ALU.add).then_inc(comb_added, 1)
            dve.wait_ge(rms_stat, DEPTH + 1)
            step(nc.vector.reciprocal(stat[:, 8:8 + TILES], stat[:, 8:8 + TILES]))
            dve.wait_ge(final_loaded, 16)
            for t in range(TILES):
                nc.vector.scalar_tensor_tensor(xn[:, t, :], x[:, t, :], stat[:, 8 + t:9 + t], final_bc, ALU.mult, ALU.mult).then_inc(final_ready, 1)

        @block.tensor
        def _(pe):
            def product(out, lhs, rhs, n):
                for k in range(n):
                    ins = nc.tensor.matmul(out, lhs(k), rhs(k), start=(k == 0), stop=(k == n - 1))
                return ins

            pe.wait_ge(const_loaded, 16)
            pe.wait_ge(cond_loaded, 32)
            bank = ring_v.open(pe, "cond")
            nc.tensor.transpose(bank[:, 0:2 * DK], cond_rows[0:2 * DK, :], ident[0:2 * DK, 0:2 * DK]).then_inc(ring_v.full, 1)
            pe.wait_ge(rows_loaded, 128 * DEPTH)
            for l in range(DEPTH):
                bank = ring_v.open(pe, (l, "vec"))
                nc.tensor.transpose(bank[:, 0:VEC_ROWS], vec_rows[l][0:VEC_ROWS, 0:P], ident[0:VEC_ROWS, 0:VEC_ROWS])
                nc.tensor.transpose(bank[:, P:P + CONV_K * CC], vec_rows[l][0:CONV_K * CC, P:2 * P],
                                    ident[0:CONV_K * CC, 0:CONV_K * CC]).then_inc(ring_v.full, 1)
            pe.wait_ge(cond_ready, 1)

            def conditioning(out, w):
                for k in range(DK):
                    j = 32 * (k % 4)
                    ins = nc.tensor.matmul(out[j:j + 32], cond[:, 32 * k:32 * k + 32], w[:, k, :], start=(k < 4), stop=(k >= 4))
                return ins

            sel = con[:, C_SEL:C_SEL + 2]

            for l in range(DEPTH):
                if l >= 1:
                    end = pe.value_load(blocks[l - 1][0:1, 2 * EXPERTS - 1:2 * EXPERTS], min_val=0, max_val=100)
                    n_last = pe.value_load(blocks[l - 1][0:1, EXPERTS - 1:EXPERTS], min_val=1, max_val=5)
                    for s in (y_act, y_dve):
                        pe.wait_ge(s, end + n_last + 1)
                    for s in (xT_act, xT_dve):
                        pe.wait_ge(s, end + n_last + l)
                    pe.sem_inc(pe_passed, 1)

                def ada_turn(ch):
                    ring_a.wait_empty(pe, ("ada", ch))
                    bank = ring_v.open(pe, ("adaT", ch))
                    for j in range(4):
                        at = (ch % 2) * ADA_W + j * P
                        ins = nc.tensor.matmul(bank[:, 2 * j:2 * j + 2], ada_row[:, at:at + P], sel, start=True, stop=True)
                    ins.then_inc(ring_v.full, 1)

                def ada(a, b):
                    for ch in range(a, b):
                        pe.wait_ge(ada_loaded[ch % 2], 16 * (ch // 2 + 1))
                        bank = ring_a.open(pe, ("ada", ch))
                        conditioning(bank, ada_w[ch % 2]).then_inc(ring_a.full, 1)
                        if ch > a:
                            ada_turn(ch - 1)
                    ada_turn(b - 1)

                if l == 0:
                    ada(0, ADA_FIRST)
                pe.wait_ge(xn_ready, TILES * (l + 1))
                for k in range(DK):
                    ring = ring_v if k % 2 else ring_a
                    bank = ring.open(pe, (l, "xnT", k))
                    for t in range(LAT):
                        ins = nc.tensor.transpose(bank[:, t * P:(t + 1) * P], xn[:, t, k * P:(k + 1) * P], ident)
                    ins.then_inc(ring.full, 1)
                for j, ring in enumerate((ring_a, ring_v)):
                    bank = ring.open(pe, (l, "xpT", j))
                    for k in range(4):
                        ins = nc.tensor.transpose(bank[:, k * P:(k + 1) * P], xn[:, LAT, (4 * j + k) * P:(4 * j + k + 1) * P], ident)
                    ins.then_inc(ring.full, 1)
                ring_a.wait_empty(pe, (l, "xpT", 0))
                ring_v.wait_empty(pe, (l, "xpT", 1))
                pe.wait_ge(win_conv_loaded, 16 * (l + 1))
                for ct in range(CC):
                    for ring, name, col in ((ring_a, "gate", QKV + CONV_C + ct * P), (ring_v, "a", QKV + ct * P)):
                        for part, a, b in (("_lat", 0, DEC_SEQ), ("_ctx", DEC_SEQ, TOK)):
                            bank = ring.open(pe, (l, name + part, ct))
                            product(bank[:, 0:b - a], lambda k: win[:, k, col:col + P], lambda k: hT[:, k, a:b], DK).then_inc(ring.full, 1)
                    if l == 0:
                        ada(ADA_FIRST + 2 * ct, ADA_FIRST + 2 * ct + 2)
                pe.wait_ge(win_qkv_loaded, 16 * (l + 1))
                for t in range(TILES):
                    for ring, name, a, b in ((ring_a, "qkv0", 0, 512), (ring_v, "qkv1", 512, QKV)):
                        bank = ring.open(pe, (l, name, t))
                        product(bank[:, 0:b - a], lambda k: hT[:, k, t * P:(t + 1) * P], lambda k: win[:, k, a:b], DK).then_inc(ring.full, 1)
                pe.wait_ge(qkv_normed, TILES * (l + 1))
                for k in range(QC):
                    bank = ring_a.open(pe, (l, "qcT", k))
                    for t in range(LAT):
                        ins = nc.tensor.transpose(bank[:, t * P:(t + 1) * P], proj[:, t, k * P:(k + 1) * P], ident)
                    ins.then_inc(ring_a.full, 1)
                bank = ring_a.open(pe, (l, "qcT_ctx"))
                for k in range(QC):
                    ins = nc.tensor.transpose(bank[:, k * P:(k + 1) * P], proj[:, LAT, k * P:(k + 1) * P], ident)
                ins.then_inc(ring_a.full, 1)
                for k in range(KC):
                    bank = ring_v.open(pe, (l, "ckvT", k))
                    for t in range(LAT):
                        ins = nc.tensor.transpose(bank[:, t * P:(t + 1) * P], proj[:, t, Q_LORA + k * P:Q_LORA + (k + 1) * P], ident)
                    ins.then_inc(ring_v.full, 1)
                pe.wait_ge(cache_loaded, 32 * (l + 1))
                for k in range(KC):
                    bank = ring_v.open(pe, (l, "ckvT_rest", k))
                    nc.tensor.transpose(bank[:, 0:P], cache_sb[:, k * P:(k + 1) * P], ident)
                    nc.tensor.transpose(bank[:, P:2 * P], proj[:, LAT, Q_LORA + k * P:Q_LORA + (k + 1) * P], ident).then_inc(ring_v.full, 1)
                pe.wait_ge(krope_ready, l + 1)
                for j, tiles in enumerate(((0, 1, 2, 3), (4, 5))):
                    bank = ring_v.open(pe, (l, "krT", j))
                    for n, t in enumerate(tiles):
                        ins = nc.tensor.transpose(bank[:, n * P:(n + 1) * P], kr[:, t, :], ident)
                    ins.then_inc(ring_v.full, 1)
                pe.wait_ge(wuq_swapped, 2 * (l + 1))
                ring_a.wait_empty(pe, (l, "qcT_ctx"))
                for h in range(HEADS):
                    bank = ring_v.open(pe, (l, "q", h))
                    product(bank, lambda k: wuq[:, k, h, :], lambda k: qcT[:, k, 0:DEC_SEQ], QC).then_inc(ring_v.full, 1)
                for j in range(2):
                    bank = ring_v.open(pe, (l, "q_ctx", j))
                    for h in range(4):
                        ins = product(bank[:, h * P:(h + 1) * P], lambda k: wuq[:, k, 4 * j + h, :], lambda k: qcT[:, k, DEC_SEQ:TOK], QC)
                    ins.then_inc(ring_v.full, 1)
                pe.wait_ge(wukv_loaded, 16 * 2 * KC * (l + 1))
                ring_v.wait_empty(pe, (l, "ckvT_rest", KC - 1))
                for pr in range(HEADS // 2):
                    for name, a, b in (("k0", 0, 512), ("k1", 512, KEYS)):
                        bank = ring_a.open(pe, (l, name, pr))
                        product(bank[:, 0:b - a], lambda k: wk[:, k, pr * P:(pr + 1) * P], lambda k: ckvT[:, k, a:b], KC).then_inc(ring_a.full, 1)
                for t in range(6):
                    bank = ring_a.open(pe, (l, "v", t))
                    product(bank, lambda k: ckvT[:, k, t * P:(t + 1) * P], lambda k: wv[:, k, :], KC).then_inc(ring_a.full, 1)

                pe.wait_ge(k_spread, (HEADS - 1) * (l + 1))
                ring_a.wait_empty(pe, (l, "v", 5))
                ring_v.wait_empty(pe, (l, "q_ctx", 1))

                def score(i):
                    h, t = divmod(i, TILES)
                    b = 2 * (i % 2)
                    if i >= 2:
                        pe.wait_ge(att_exp, UNITS * l + i - 1)
                    q = qT[:, h, t * P:(t + 1) * P]
                    if t < LAT:
                        nc.tensor.matmul(ps[:, b], q, kT[:, h, 0:512], start=True, stop=True)
                        nc.tensor.matmul(ps[:, b + 1, 0:P], q, kT[:, h, 512:LAT_KEYS], start=True, stop=True).then_inc(scores, 1)
                    else:
                        nc.tensor.matmul(ps[:, b, 0:P], q, kT[:, h, LAT_KEYS:KEYS], start=True, stop=True).then_inc(scores, 1)

                score(0)
                score(1)
                for i in range(UNITS):
                    h, t = divmod(i, TILES)
                    u = UNITS * l + i
                    key_tiles = range(LAT + 1) if t < LAT else range(5, 6)
                    pe.wait_ge(att_exp, u + 1)
                    if i >= 1:
                        pe.wait_ge(probT_ready, u)
                    for n, kt in enumerate(key_tiles):
                        ins = nc.tensor.transpose(flat[:, 2048 + n * P:2048 + (n + 1) * P], prob[:, i % 2, n * P:(n + 1) * P], ident)
                    ins.then_inc(prob_turned, 1)
                    if i + 2 < UNITS:
                        score(i + 2)
                    if i >= 1:
                        pe.wait_ge(att_out_empty, u)
                    if l + 1 < DEPTH and 1 <= i <= ADA_NEXT_CHUNKS:
                        pe.wait_ge(ada_next_taken, ADA_NEXT_CHUNKS * l + i)
                        for j in range(2):
                            nc.tensor.matmul(ps[:, 6, VH + 2 * j:VH + 2 * j + 2], ada_next_row[:, j * P:(j + 1) * P], sel, start=True, stop=True)
                    pe.wait_ge(probT_ready, u + 1)
                    for n, kt in enumerate(key_tiles):
                        ins = nc.tensor.matmul(ps[:, 6, 0:VH], probT[:, i % 2, n * P:(n + 1) * P],
                                               v_sb[:, kt, h * VH:(h + 1) * VH], start=(n == 0), stop=(n == len(key_tiles) - 1))
                    ins.then_inc(att_out, 1)
                    if l + 1 < DEPTH and i < ADA_NEXT_CHUNKS:
                        pe.wait_ge(ada_next_loaded[i % 2], 16 * (ADA_NEXT_CHUNKS // 2 * l + i // 2 + 1))
                        conditioning(ps[:, 7, 0:ADA_NEXT_W], ada_next[i % 2]).then_inc(ada_next_full, 1)
                pe.wait_ge(att_out_empty, UNITS * (l + 1))
                pe.wait_ge(probT_ready, UNITS * (l + 1))
                for k in range(4):
                    bank = ring_a.open(pe, (l, "oT", k))
                    for t in range(LAT):
                        ins = nc.tensor.transpose(bank[:, t * P:(t + 1) * P], o_tok[:, t, k * P:(k + 1) * P], ident)
                    ins.then_inc(ring_a.full, 1)
                bank = ring_a.open(pe, (l, "oT_ctx"))
                for k in range(4):
                    ins = nc.tensor.transpose(bank[:, k * P:(k + 1) * P], o_tok[:, LAT, k * P:(k + 1) * P], ident)
                ins.then_inc(ring_a.full, 1)
                pe.wait_ge(conv_step, (l + 1) * CONV_K * CC)
                for s in range(2):
                    if s == 1:
                        pe.wait_ge(ln_squared, CC * (l + 1))
                    src = zsq if s else acc
                    for j, (a, b) in enumerate(((0, 512), (512, CONV_OUT))):
                        bank = ring_v.open(pe, (l, "ln", s, j))
                        product(bank[:, 0:b - a], lambda k: ones, lambda k: src[:, k, a:b], CC).then_inc(ring_v.full, 1)

                def spread(key, d):
                    pe.wait_ge(diag_ready, d + 1)
                    bank = ring_v.open(pe, key)
                    nc.tensor.matmul(bank, ones, diag[:, d % 2], start=True, stop=True).then_inc(ring_v.full, 1)

                for n in range(12):
                    spread((l, "bc", n // 2, n % 2), 16 * l + n)
                pe.wait_ge(wout_loaded, 16 * (l + 1))
                pe.wait_ge(conv_silu, 2 * CC * (l + 1))
                ring_a.wait_empty(pe, (l, "oT_ctx"))

                def h2_turn(t):
                    pe.wait_ge(h2_ready, TILES * l + t + 1)
                    for j in range(2):
                        bank = ring_a.open(pe, (l, "h2T", t, j))
                        for k in range(4):
                            ins = nc.tensor.transpose(bank[:, k * P:(k + 1) * P], h2s[:, t % 2, (4 * j + k) * P:(4 * j + k + 1) * P], ident)
                        ins.then_inc(ring_a.full, 1)

                for t in range(TILES):
                    for j in range(2):
                        bank = ring_v.open(pe, (l, "wo", t, j))
                        product(bank, lambda k: mixT[:, k, t * P:(t + 1) * P], lambda k: wout[:, k, j * 512:(j + 1) * 512], DK).then_inc(ring_v.full, 1)
                    if t >= 1:
                        h2_turn(t - 1)
                h2_turn(TILES - 1)
                ring_a.wait_empty(pe, (l, "h2T", TILES - 1, 1))
                bank = ring_a.open(pe, (l, "logits"))
                for t in range(TILES):
                    ins = product(bank[:, t * EXPERTS:(t + 1) * EXPERTS], lambda k: h2T[:, k, t * P:(t + 1) * P],
                                  lambda k: rw[:, k * EXPERTS:(k + 1) * EXPERTS], DK)
                ins.then_inc(ring_a.full, 1)
                for n in range(4):
                    spread((l, "g2", n // 2, n % 2), 16 * l + 12 + n)
                pe.wait_ge(masks_ready, l + 1)
                both = r_tmp[:, BOTH_AT:BOTH_AT + 80]
                bank = ring_v.open(pe, (l, "slots"))
                for t in range(TILES):
                    for s in range(t + 1):
                        nc.tensor.matmul(bank[:, t * EXPERTS:(t + 1) * EXPERTS], tri if s == t else ones,
                                         both[:, s * EXPERTS:(s + 1) * EXPERTS], start=(s == 0), stop=(s == t))
                for s in range(TILES):
                    ins = nc.tensor.matmul(bank[:, 80:96], ones, both[:, s * EXPERTS:(s + 1) * EXPERTS], start=(s == 0), stop=(s == TILES - 1))
                ins.then_inc(ring_v.full, 1)

                pe.wait_ge(plan_ready, l + 1)
                start = pe.value_load(blocks[l][0:1, EXPERTS:EXPERTS + 1], min_val=0, max_val=100)

                def turn(n):
                    pe.wait_ge(gathered, 16 * n + 16 * (l + 1))
                    for k in range(DK):
                        ins = nc.tensor.transpose(ps[:, k // 4, (k % 4) * P:(k % 4 + 1) * P], xg[:, k * P:(k + 1) * P], ident)
                    ins.then_inc(xT_full, 1)

                turn(start + l)
                with pe.Fori(0, EXPERTS // 2) as i:
                    for s in range(2):
                        first = pe.value_load(blocks[l][0:1, bass.ds(EXPERTS + 2 * i + s, 1)], min_val=0, max_val=100)
                        count = pe.value_load(blocks[l][0:1, bass.ds(2 * i + s, 1)], min_val=1, max_val=5)
                        pe.wait_ge(expert_loaded[s], (i + (EXPERTS // 2 * l + 1)) * 48)
                        pe.sem_inc(pe_passed, 1)
                        with pe.Fori(0, count) as b:
                            g = first + b
                            pe.wait_ge(xT_act, g + l + 1)
                            pe.wait_ge(xT_dve, g + l + 1)
                            product(ps[:, 2], lambda k: xgT[:, k, :], lambda k: wgu[s][:, k, :], DK).then_inc(gu_full, 1)
                            turn(g + l + 1)
                            pe.wait_ge(hid_ready, g + 1)
                            for k in range(2):
                                ins = nc.tensor.transpose(ps[:, 3, k * P:(k + 1) * P], hid[:, k * P:(k + 1) * P], ident)
                            ins.then_inc(hidT_full, 1)
                            pe.wait_ge(hidT_ready, g + 1)
                            pe.wait_ge(y_act, g + 1)
                            pe.wait_ge(y_dve, g + 1)
                            product(ps[:, 4], lambda k: hidT[:, k, :], lambda k: wdn[s][:, k, 0:512], 2)
                            product(ps[:, 5], lambda k: hidT[:, k, :], lambda k: wdn[s][:, k, 512:1024], 2).then_inc(y_full, 1)


BOTH_AT = 80 + 80 + 120 + 20 + 20 + 5 + 20 + 80 + 80 + 5 + 5
_INS = ['x_prompt', 'x_sample', 'cache_ckv', 'cache_krope', 'c', 'c_ctx', 'w_ada', 'b_ada', 'norm1_g', 'w_in',
        'q_norm_g', 'w_uq', 'kv_norm_g', 'w_ukv', 'conv_w', 'conv_b', 'conv_ln_g', 'conv_ln_b', 'w_out',
        'norm2_g', 'router_w', 'router_b', 'w_gate', 'w_up', 'w_down', 'final_g']
_OUTS = [("y_prompt", (1, SEQ, D)), ("y_sample", (1, DEC_SEQ, D)),
         ("new_ckv", (1, DEPTH, SEQ, KV_LORA)), ("new_krope", (1, DEPTH, SEQ, ROPE))]


def kernel(**inputs):
    import concourse.bacc as _bacc
    from concourse.bass_utils import run_bass_kernel_spmd as _run

    nc = _bacc.Bacc("TRN2", target_bir_lowering=False, num_devices=1)
    arrays, args = {}, []
    for name in _INS:
        a = np.ascontiguousarray(inputs[name])
        arrays[f"in_{name}"] = a
        args.append(nc.dram_tensor(f"in_{name}", a.shape, mybir.dt.from_np(a.dtype), kind="ExternalInput").ap())
    a = shape_constants()
    arrays["in_consts"] = a
    args.append(nc.dram_tensor("in_consts", a.shape, FP32, kind="ExternalInput").ap())
    for name, shape in _OUTS:
        args.append(nc.dram_tensor(f"out_{name}", shape, FP32, kind="ExternalOutput").ap())
    hybrid_step_kernel(nc, *args)
    r = _run(nc, [arrays], core_ids=[0])
    return tuple(r.results[0][f"out_{name}"] for name, _ in _OUTS)
```

```python
from contextlib import ExitStack

import numpy as np

import concourse.bass as bass
from concourse import mybir

FP32 = mybir.dt.float32
INT32 = mybir.dt.int32
ALU = mybir.AluOpType
ACT = mybir.ActivationFunctionType
AXIS_X = mybir.AxisListType.X

P = 128
D = 1024
DK = D // P
DEPTH = 2
SEQ, DEC_SEQ, PAST = 128, 512, 128
GRID_W = 64
TILES = (DEC_SEQ + SEQ) // P
LAT = DEC_SEQ // P
TOK = TILES * P
HEADS, NOPE, ROPE, VH = 8, 64, 32, 64
Q_LORA, KV_LORA, CONV_C, CONV_K = 384, 256, 512, 31
QC, KC, CC = Q_LORA // P, KV_LORA // P, CONV_C // P
PAD = CONV_K // 2
QKV = Q_LORA + KV_LORA + ROPE
D_IN = QKV + 2 * CONV_C
KEYS = TOK + PAST
LAT_KEYS = DEC_SEQ + PAST
EXPERTS, GROUPS, PER_GROUP, FF = 16, 4, 4, 256
PAIRS = ROPE // 4
EPS = 1e-6
SCALE = (NOPE + ROPE) ** -0.5
MAX_BLOCKS = 2 * TOK // P + EXPERTS - 1
NB = MAX_BLOCKS + 2
NO_ROW = 1 << 20
BIG = 1e30
ADA_CHUNKS = 6 * D // 512
CONV_EARLY = (0, 16, 16, 12)
ADA_FIRST = 4
ZPAD = 3 * PAD + TOK
CONV_OUT = TOK + PAD
UNITS = HEADS * TILES
VEC_ROWS = 48 + 8 + 8 + QC + 3 * CC
(V_BADA, V_G1, V_G2, V_QG, V_CB, V_LG, V_LB) = (0, 48, 56, 64, 64 + QC, 64 + QC + CC, 64 + QC + 2 * CC)

C_ID, C_TRI, C_ONE, C_TAB = 0, 128, 256, 384
C_KC = C_TAB + TOK
C_KS = C_KC + LAT * ROPE
C_W16 = C_KS + LAT * ROPE
C_W4 = C_W16 + EXPERTS
C_TOKID = C_W4 + GROUPS
C_SEL = C_TOKID + TILES
C_RAMP = C_SEL + 2
C_BLK = C_RAMP + P
N_CONST = C_BLK + NB
ADA_W = 512
ADA_NEXT_W = 256
ADA_NEXT_CHUNKS = 6 * D // ADA_NEXT_W


def shape_constants():
    c = np.zeros((P, N_CONST), np.float32)
    p = np.arange(P)
    c[:, C_ID:C_ID + P] = np.eye(P)
    c[:, C_TRI:C_TRI + P] = p[:, None] < p[None, :]
    c[:, C_ONE:C_ONE + P] = 1.0
    tok = np.arange(DEC_SEQ)
    freqs = (np.float32(10000.0) ** (-np.arange(PAIRS, dtype=np.float32) / PAIRS)).astype(np.float32)
    pos = np.stack([tok // GRID_W, tok % GRID_W], 1).astype(np.float32)
    ang = pos[:, :, None] * freqs
    cos, sin = np.cos(ang).astype(np.float32), np.sin(ang).astype(np.float32)
    cos_r = np.stack([cos, cos], 2).reshape(DEC_SEQ, ROPE)
    sin_r = np.stack([-sin, sin], 2).reshape(DEC_SEQ, ROPE)
    tab = c[:, C_TAB:C_TAB + TOK]
    tab[0:NOPE + ROPE] = 1.0
    tab[NOPE:NOPE + ROPE, 0:DEC_SEQ] = cos_r.T
    tab[NOPE + ROPE:P, 0:DEC_SEQ] = sin_r.T
    c[:, C_KC:C_KC + LAT * ROPE] = cos_r.reshape(LAT, P, ROPE).transpose(1, 0, 2).reshape(P, -1)
    c[:, C_KS:C_KS + LAT * ROPE] = sin_r.reshape(LAT, P, ROPE).transpose(1, 0, 2).reshape(P, -1)
    c[:, C_W16:C_W16 + EXPERTS] = EXPERTS - np.arange(EXPERTS)
    c[:, C_W4:C_W4 + GROUPS] = GROUPS - np.arange(GROUPS)
    c[:, C_SEL:C_SEL + 2] = p[:, None] % 32 == np.arange(2)
    c[:, C_TOKID:C_TOKID + TILES] = p[:, None] + P * np.arange(TILES)
    c[:, C_RAMP:C_RAMP + P] = p
    c[:, C_BLK:C_BLK + NB] = np.arange(NB)
    return c


class Ring:

    def __init__(self, banks, full, empty):
        self.banks, self.full, self.empty, self.number, self.order = banks, full, empty, {}, []

    def plan(self, *keys):
        for key in keys:
            self.number[key] = len(self.order)
            self.order.append(key)

    def bank(self, key):
        return self.banks[self.number[key] % len(self.banks)]

    def open(self, pe, key):
        before = self.number[key] - len(self.banks)
        if before >= 0:
            pe.wait_ge(self.empty, before + 1)
        return self.bank(key)

    def take(self, eng, key):
        eng.wait_ge(self.full, self.number[key] + 1)
        return self.bank(key)

    def wait_full(self, eng, key):
        eng.wait_ge(self.full, self.number[key] + 1)

    def wait_empty(self, eng, key):
        eng.wait_ge(self.empty, self.number[key] + 1)


def hybrid_step_kernel(nc, x_prompt, x_sample, cache_ckv, cache_krope, c, c_ctx, w_ada, b_ada, norm1_g, w_in,
                       q_norm_g, w_uq, kv_norm_g, w_ukv, conv_w, conv_b, conv_ln_g, conv_ln_b, w_out,
                       norm2_g, router_w, router_b, w_gate, w_up, w_down, final_g, consts,
                       y_prompt, y_sample, new_ckv, new_krope):
    ctx = ExitStack()
    with ctx:
        def sb(name, cols, dt=FP32, parts=P):
            return ctx.enter_context(nc.sbuf_tensor(name, [parts, cols], dt))

        def sem(name):
            return ctx.enter_context(nc.semaphore(name))

        h2_dram = nc.dram_tensor("h2_rows", [TOK, D], FP32, kind="Internal").ap()
        y_dram = nc.dram_tensor("expert_rows", [2 * TOK, D], FP32, kind="Internal").ap()

        con = sb("con", N_CONST)
        ident, tri, ones = con[:, C_ID:C_ID + P], con[:, C_TRI:C_TRI + P], con[:, C_ONE:C_ONE + P]
        vec_cols = [sb(f"vecs{l}", 2 * P) for l in range(DEPTH)]
        cond = sb("cond", 32 * DK)
        ada_cols = [sb(f"adat{l}", 96) for l in range(DEPTH)]
        mod = sb("mod", 32)
        rw = sb("rw", DK * EXPERTS)
        rb = sb("rb", EXPERTS)
        eps_t = sb("eps_t", 1)
        stat = sb("stat", 64)
        token_col, row_out = sb("token_col", 1, INT32), sb("row_out", 1, INT32)
        blocks = [sb(f"blocks{l}", 2 * EXPERTS + 1, INT32) for l in range(DEPTH)]
        nbf = sb("nbf", 5 * 24)
        block_total = sb("block_total", 1)

        x = sb("x", TILES * D)[:, :].rearrange("p (t d) -> p t d", t=TILES)
        W1 = sb("region_weights", DK * D_IN)
        H = sb("region_h", TILES * D)
        Q = sb("region_q", TILES * D)
        O = sb("region_o", 8576)
        BC = sb("region_bc", 6 * D)
        PR = sb("region_proj", TILES * QKV)
        CV = sb("region_conv", 3 * D)

        hT = H[:, 0:DK * TOK].rearrange("p (k t) -> p k t", k=DK)
        mixT = hT
        xn = Q[:, :].rearrange("p (t d) -> p t d", t=TILES)
        qT = Q[:, :].rearrange("p (h t) -> p h t", h=HEADS)
        h2T = Q[:, :].rearrange("p (k t) -> p k t", k=DK)
        win = W1[:, :].rearrange("p (k n) -> p k n", k=DK)
        kvg = Q[:, 0:KV_LORA]
        vec_rows = [PR[:, 1024 + 2 * P * l:1024 + 2 * P * (l + 1)] for l in range(DEPTH)]
        cond_rows = PR[:, 2048:2048 + P]
        cond_raw = PR[:, 2048 + P:2048 + P + 2 * DK]
        kT = W1[:, 0:HEADS * KEYS].rearrange("p (h t) -> p h t", h=HEADS)
        base = HEADS * KEYS
        v_sb = W1[:, base:base + 6 * 512].rearrange("p (t n) -> p t n", t=6)
        base += 6 * 512
        prob = W1[:, base:base + 2 * LAT_KEYS].rearrange("p (b n) -> p b n", b=2)
        base += 2 * LAT_KEYS
        probT = W1[:, base:base + 2 * LAT_KEYS].rearrange("p (b n) -> p b n", b=2)
        base += 2 * LAT_KEYS
        kr = W1[:, base:base + 6 * P].rearrange("p (t n) -> p t n", t=6)
        base += 6 * P
        cache_sb = W1[:, base:base + KV_LORA + ROPE]
        assert base + KV_LORA + ROPE <= DK * D_IN
        EW = DK * 512 + 2 * D
        wgu = [W1[:, s * EW:s * EW + DK * 512].rearrange("p (k n) -> p k n", k=DK) for s in range(2)]
        wdn = [W1[:, s * EW + DK * 512:(s + 1) * EW].rearrange("p (k n) -> p k n", k=2) for s in range(2)]
        ada_w = [a.rearrange("p (k n) -> p k n", k=DK) for a in (O[:, 0:4096], O[:, 4096:8192], H[:, 0:4096], BC[:, 0:4096])]
        wuq = O[:, 0:3072].rearrange("p (k h n) -> p k h n", k=QC, h=HEADS)
        wk = O[:, 3072:4096].rearrange("p (k n) -> p k n", k=KC)
        wv = O[:, 4096:5120].rearrange("p (k n) -> p k n", k=KC)
        qcT = O[:, 5120:5120 + QC * TOK].rearrange("p (k t) -> p k t", k=QC)
        ckvT = O[:, 7040:7040 + KC * KEYS].rearrange("p (k t) -> p k t", k=KC)
        wout = O[:, 0:8192].rearrange("p (k n) -> p k n", k=DK)
        proj = PR[:, :].rearrange("p (t n) -> p t n", t=TILES)
        o_tok = PR[:, 0:TILES * 512].rearrange("p (t n) -> p t n", t=TILES)
        y_sb, hid = PR[:, 0:1024], PR[:, 1024:1280]
        hidT = PR[:, 1280:1536].rearrange("p (k n) -> p k n", k=2)
        silu_g = PR[:, 1536:1792]
        zpad = CV[:, 0:CC * ZPAD].rearrange("p (k n) -> p k n", k=CC)
        diag = CV[:, 0:1024].rearrange("p (b n) -> p b n", b=2)
        h2s = CV[:, 0:2048].rearrange("p (b n) -> p b n", b=2)
        res_tmp = CV[:, 2048:3072]
        xg = CV[:, 0:1024]
        xgT = CV[:, 1024:2048].rearrange("p (k n) -> p k n", k=DK)
        acc = BC[:, 0:CC * CONV_OUT].rearrange("p (k n) -> p k n", k=CC)
        sig = BC[:, 2 * D + 1024:2 * D + 1024 + 2 * TOK].rearrange("p (b n) -> p b n", b=2)
        junk = BC[:, 5 * D:6 * D]
        att_stat = BC[:, 4 * D + 256:4 * D + 256 + 4 * UNITS]
        slot_tokens, slot_rows = (BC[:, 4 * D + n * NB:4 * D + (n + 1) * NB].bitcast(INT32) for n in range(2))
        slot_gates = BC[:, 4 * D + 2 * NB:4 * D + 3 * NB]
        junk2 = PR[:, 2048:3072]
        ada_row = PR[:, 0:1024]
        ada_next = [H[:, s * 2048:(s + 1) * 2048].rearrange("p (k n) -> p k n", k=DK) for s in range(2)]
        ada_next_row = H[:, 4096:4096 + ADA_NEXT_W]
        bc = BC[:, :].rearrange("p (i n) -> p i n", i=6)
        g1_bc, a2_bc, sh2_bc = (lambda v: bc[:, v]), (lambda v: bc[:, 2 + v]), (lambda v: bc[:, 4 + v])
        g2_bc = g1_bc
        zsq = Q[:, 0:CC * CONV_OUT].rearrange("p (k n) -> p k n", k=CC)
        ln_rstd = Q[:, CC * CONV_OUT:CC * CONV_OUT + CONV_OUT]
        comb = [H[:, n * D:(n + 1) * D] for n in range(4)] + [CV[:, n * D:(n + 1) * D] for n in range(3)] \
            + [PR[:, n * D:(n + 1) * D] for n in range(3)]
        r_tmp = H[:, 4096:5120]
        final_bc = bc[:, 2]
        TR = 2 * TILES
        hot_place = H[:, 0:TR * P].rearrange("p (j n) -> p j n", j=TR)
        hot_block = H[:, TR * P:TR * P + TR * NB].rearrange("p (j n) -> p j n", j=TR)
        table_rhs = H[:, TR * (P + NB):TR * (P + 3 * NB)].rearrange("p (j n) -> p j n", j=TR)

        ps = ctx.enter_context(nc.psum_tensor("ps", [P, 8, 512], FP32))
        flat = ps[:, :, :].rearrange("p b n -> p (b n)")

        ring_a = Ring([ps[:, b] for b in range(4)], sem("act_bank_full"), sem("act_bank_empty"))
        ring_v = Ring([ps[:, b] for b in range(4, 8)], sem("dve_bank_full"), sem("dve_bank_empty"))
        x_loaded, const_loaded, rows_loaded = [sem(f"x_loaded{j}") for j in range(3)], sem("const_loaded"), sem("rows_loaded")
        cond_loaded = sem("cond_loaded")
        kvg_loaded, final_loaded = sem("kvg_loaded"), sem("final_loaded")
        ada_loaded = [sem(f"ada_loaded{s}") for s in range(4)]
        win_conv_loaded, win_qkv_loaded = [sem(f"win_conv_loaded{ct}") for ct in range(CC)], sem("win_qkv_loaded")
        wuq_loaded, wukv_loaded, cache_loaded = sem("wuq_loaded"), sem("wukv_loaded"), sem("cache_loaded")
        wout_loaded = sem("wout_loaded")
        expert_loaded = [sem(f"expert_loaded{s}") for s in range(2)]
        act_step, dve_step, pool_step = sem("act_step"), sem("dve_step"), sem("pool_step")
        cond_ready, mod_ready, mod2_ready = sem("cond_ready"), sem("mod_ready"), sem("mod2_ready")
        ada_next_loaded = [sem(f"ada_next_loaded{s}") for s in range(2)]
        ada_next_full, ada_next_taken = sem("ada_next_full"), sem("ada_next_taken")
        rms_stat, xn_ready, zero_ready = sem("rms_stat"), sem("xn_ready"), sem("pad_zeroed")
        sig_ready, qkv_stat, qkv_normed = sem("sig_ready"), sem("qkv_stat"), sem("qkv_normed")
        krope_ready, wuq_swapped, k_spread = sem("krope_ready"), sem("wuq_swapped"), sem("k_spread")
        scores, att_max, att_exp = sem("scores"), sem("att_max"), sem("att_exp")
        prob_turned, probT_ready, att_out, att_out_empty = (
            sem("prob_turned"), sem("probT_ready"), sem("att_out"), sem("att_out_empty"))
        conv_step, ln_centred, ln_squared, ln_sqrt, ln_done, conv_silu = (
            sem("conv_step"), sem("ln_centred"), sem("ln_squared"), sem("ln_sqrt"), sem("ln_done"),
            sem("conv_silu"))
        diag_ready = sem("diag_ready")
        x_updated, h2_stat, h2_ready, h2_stored = sem("x_updated"), sem("h2_stat"), sem("h2_ready"), [sem("h2_stored0"), sem("h2_stored1")]
        masks_ready, table_rhs_ready, plan_ready = sem("masks_ready"), sem("table_rhs_ready"), sem("plan_ready")
        gathered, tokens_given = sem("gathered"), sem("tokens_given")
        xT_full, xT_act, xT_dve = sem("xT_full"), sem("xT_act"), sem("xT_dve")
        gu_full, silu_ready, hid_ready = sem("gu_full"), sem("silu_ready"), sem("hid_ready")
        hidT_full, hidT_ready = sem("hidT_full"), sem("hidT_ready")
        y_full, y_act, y_dve, y_stored = sem("y_full"), sem("y_act"), sem("y_dve"), sem("y_stored")
        comb_loaded, comb_added = [sem(f"comb_loaded{t}") for t in range(TILES)], sem("comb_added")
        pair_added, affinities_ready = sem("pair_added"), sem("affinities_ready")
        pool_passed, pe_passed, act_passed = sem("pool_passed"), sem("pe_passed"), sem("act_passed")
        outputs_done, final_ready = sem("outputs_done"), sem("final_ready")
        ckv_out = sem("ckv_out")

        def plan_ada(a, b):
            for ch in range(a, b):
                ring_a.plan(("ada", ch))
                ring_v.plan(("adaT", ch))

        for l in range(DEPTH):
            if l == 0:
                ring_v.plan("cond", *[(m, "vec") for m in range(DEPTH)])
                plan_ada(0, ADA_FIRST)
            for k in range(DK):
                (ring_v if k % 2 else ring_a).plan((l, "xnT", k))
            ring_a.plan((l, "xpT", 0))
            ring_v.plan((l, "xpT", 1))
            for ct in range(CC):
                ring_a.plan((l, "gate_lat", ct), (l, "gate_ctx", ct))
                ring_v.plan((l, "a_lat", ct), (l, "a_ctx", ct))
                if l == 0:
                    plan_ada(ADA_FIRST + 2 * ct, ADA_FIRST + 2 * ct + 2)
            for t in range(TILES):
                ring_a.plan((l, "qkv0", t))
                ring_v.plan((l, "qkv1", t))
            ring_a.plan(*[(l, "qcT", k) for k in range(QC)], (l, "qcT_ctx"))
            ring_v.plan(*[(l, "ckvT", k) for k in range(KC)], *[(l, "ckvT_rest", k) for k in range(KC)],
                        (l, "krT", 0), (l, "krT", 1))
            ring_v.plan(*[(l, "q", h) for h in range(HEADS)], (l, "q_ctx", 0), (l, "q_ctx", 1))
            for pr in range(HEADS // 2):
                ring_a.plan((l, "k0", pr), (l, "k1", pr))
            ring_a.plan(*[(l, "v", t) for t in range(6)])
            ring_a.plan(*[(l, "oT", k) for k in range(4)], (l, "oT_ctx"))
            ring_v.plan(*[(l, "ln", s, j) for s in range(2) for j in range(2)])
            ring_v.plan(*[(l, "bc", i, j) for i in range(6) for j in range(2)])
            for t in range(TILES):
                ring_v.plan((l, "wo", t, 0), (l, "wo", t, 1))
                ring_a.plan((l, "h2T", t, 0), (l, "h2T", t, 1))
                if t >= 1:
                    ring_a.plan((l, "logits", t - 1))
            ring_a.plan((l, "logits", TILES - 1))
            ring_a.plan((l, "g2", 0, 0), (l, "g2", 0, 1), (l, "g2", 1, 0), (l, "g2", 1, 1))
            ring_v.plan((l, "slots"), (l, "table"))

        def ada_buffer(ch):
            return ch if ch < ADA_FIRST else ch % 2

        def vec_col(l, v):
            return vec_cols[l][:, v:v + 1]

        def stores_of(l, t, parity):
            return l * ((TILES + 1 - parity) // 2) + (t + 1 - parity) // 2

        def wait_diag_used(eng, l, n):
            if n < 0:
                l, n = l - 1, n + 16
            if n < 12:
                ring_v.wait_full(eng, (l, "bc", n // 2, n % 2))
            else:
                ring_a.wait_full(eng, (l, "g2", (n - 12) // 2, n % 2))

        block = ctx.enter_context(nc.Block())

        @block.sync
        def _(sp):
            sp.dma_start(con[:, :], consts).then_inc(const_loaded, 16)
            sp.dma_start(cond_rows[0:DK, :], c[0, :].rearrange("(k q) -> k q", q=P)).then_inc(cond_loaded, 16)
            sp.dma_start(cond_rows[DK:2 * DK, :], c_ctx.rearrange("(k q) -> k q", q=P)).then_inc(cond_loaded, 16)
            for j in range(2):
                a, b = LAT // 2 * j, LAT // 2 * (j + 1)
                sp.dma_start(x[:, a:b, :], x_sample[0].rearrange("(t p) d -> p t d", p=P)[:, a:b, :]).then_inc(x_loaded[j], 16)
            sp.dma_start(x[:, LAT, :], x_prompt[0]).then_inc(x_loaded[2], 16)
            for l in range(DEPTH):
                at = 0
                for vec in (b_ada, norm1_g, norm2_g, q_norm_g, conv_b, conv_ln_g, conv_ln_b):
                    n = vec.shape[1] // P
                    sp.dma_start(vec_rows[l][at:at + n, 0:P], vec[l].rearrange("(k q) -> k q", q=P)).then_inc(rows_loaded, 16)
                    at += n
                sp.dma_start(vec_rows[l][0:CONV_K * CC, P:2 * P], conv_w[l].rearrange("j (k q) -> (j k) q", q=P)).then_inc(rows_loaded, 16)
            sp.dma_start(rw[:, :].rearrange("p (k n) -> p k n", k=DK), router_w.rearrange("(k p) n -> p k n", p=P)).then_inc(rows_loaded, 16)
            sp.dma_start(rb[:, :], router_b.rearrange("(a n) -> a n", a=1).broadcast_to([P, EXPERTS])).then_inc(rows_loaded, 16)
            wgu_dram = [w.rearrange("l e (k p) n -> l e p k n", p=P) for w in (w_gate, w_up)]
            wdn_dram = w_down.rearrange("l e (k p) n -> l e p k n", p=P)

            def load_expert(l, e, s):
                for j, w in enumerate(wgu_dram):
                    sp.dma_start(wgu[s][:, :, j * FF:(j + 1) * FF], w[l, e]).then_inc(expert_loaded[s], 16)
                sp.dma_start(wdn[s], wdn_dram[l, e]).then_inc(expert_loaded[s], 16)

            def load_ada(ch):
                if ch >= ADA_FIRST:
                    ring_a.wait_full(sp, ("ada", ch - (2 if ch >= ADA_FIRST + 2 else ADA_FIRST)))
                buf = ada_buffer(ch)
                sp.dma_start(ada_w[buf], w_ada[0].rearrange("(k p) n -> p k n", p=P)[:, :, ch * ADA_W:(ch + 1) * ADA_W]).then_inc(ada_loaded[buf], 16)

            def load_ada_next(l, ch):
                m = l * ADA_NEXT_CHUNKS + ch
                if ch >= 2:
                    sp.wait_ge(ada_next_full, m - 1)
                sp.dma_start(ada_next[ch % 2], w_ada[l + 1].rearrange("(k p) n -> p k n", p=P)[:, :, ch * ADA_NEXT_W:(ch + 1) * ADA_NEXT_W]).then_inc(ada_next_loaded[ch % 2], 16)

            def load_attention_weights(l):
                for k in range(QC):
                    sp.dma_start(wuq[:, k, :, 0:NOPE + ROPE], w_uq[l, k * P:(k + 1) * P, :].rearrange("p (h n) -> p h n", h=HEADS)).then_inc(wuq_loaded, 16)
                for k in range(KC):
                    src = w_ukv[l, k * P:(k + 1) * P, :].rearrange("p (h n) -> p h n", h=HEADS)
                    sp.dma_start(wk[:, k, :].rearrange("p (h n) -> p h n", h=HEADS), src[:, :, 0:NOPE]).then_inc(wukv_loaded, 16)
                    sp.dma_start(wv[:, k, :].rearrange("p (h n) -> p h n", h=HEADS), src[:, :, NOPE:NOPE + VH]).then_inc(wukv_loaded, 16)

            for l in range(DEPTH):
                if l == 0:
                    load_ada(0)
                    load_ada(1)
                    for ch in range(2, ADA_FIRST):
                        load_ada(ch)
                if l >= 1:
                    ring_v.wait_full(sp, (l - 1, "wo", TILES - 1, 1))
                    load_attention_weights(l)
                    last = sp.value_load(blocks[l - 1][0:1, 2 * EXPERTS - 1:2 * EXPERTS], min_val=0, max_val=100)
                    n_last = sp.value_load(blocks[l - 1][0:1, EXPERTS - 1:EXPERTS], min_val=1, max_val=5)
                    sp.wait_ge(y_full, last + n_last)
                    sp.wait_ge(comb_loaded[0], 32 * l)
                win_dram = w_in[l].rearrange("(k p) n -> p k n", p=P)
                for ct in range(CC):
                    for half in range(2):
                        a = QKV + half * CONV_C + ct * P
                        sp.dma_start(win[:, :, a:a + P], win_dram[:, :, a:a + P]).then_inc(win_conv_loaded[ct], 16)
                if l == 0:
                    load_ada(ADA_FIRST)
                    load_ada(ADA_FIRST + 1)
                sp.dma_start(win[:, :, 0:QKV], win_dram[:, :, 0:QKV]).then_inc(win_qkv_loaded, 16)
                if l == 0:
                    for ch in range(ADA_FIRST + 2, ADA_CHUNKS):
                        load_ada(ch)
                    ring_a.wait_full(sp, ("ada", ADA_CHUNKS - 1))
                    load_attention_weights(l)
                ring_v.wait_full(sp, (l, "a_ctx", CC - 1))
                sp.dma_start(kvg, kv_norm_g[l:l + 1, :].broadcast_to([P, KV_LORA])).then_inc(kvg_loaded, 16)
                ring_v.wait_full(sp, (l, "qkv1", TILES - 1))
                sp.dma_start(cache_sb[:, 0:KV_LORA], cache_ckv[0, l]).then_inc(cache_loaded, 16)
                sp.dma_start(cache_sb[:, KV_LORA:KV_LORA + ROPE], cache_krope[0, l]).then_inc(cache_loaded, 16)
                if l + 1 < DEPTH:
                    load_ada_next(l, 0)
                    load_ada_next(l, 1)
                ring_a.wait_full(sp, (l, "v", 5))
                ring_v.wait_full(sp, (l, "q_ctx", 1))
                sp.dma_start(wout, w_out[l].rearrange("(k p) n -> p k n", p=P)).then_inc(wout_loaded, 16)
                if l + 1 < DEPTH:
                    for ch in range(2, ADA_NEXT_CHUNKS):
                        load_ada_next(l, ch)
                sp.wait_ge(att_out, UNITS * (l + 1))
                for s in range(2):
                    load_expert(l, s, s)
                sp.wait_ge(plan_ready, l + 1)
                with sp.Fori(0, EXPERTS // 2 - 1) as i:
                    for s in range(2):
                        done = sp.value_load(blocks[l][0:1, bass.ds(EXPERTS + 2 * i + s, 1)], min_val=0, max_val=100)
                        n = sp.value_load(blocks[l][0:1, bass.ds(2 * i + s, 1)], min_val=1, max_val=5)
                        sp.wait_ge(y_full, done + n)
                        load_expert(l, 2 * i + s + 2, s)
            sp.wait_ge(ckv_out, 16 * 2 * DEPTH)
            sp.wait_ge(outputs_done, 16 * TILES)

        @block.gpsimd
        def _(pool):
            steps = [0]

            def step(ins):
                steps[0] += 1
                ins.then_inc(pool_step, 1)
                pool.wait_ge(pool_step, steps[0])

            for l in range(DEPTH):
                if l >= 1:
                    pool.wait_ge(comb_added, l * TILES)
                for a, b in ((0, PAD), (PAD + DEC_SEQ, 2 * PAD + DEC_SEQ), (2 * PAD + TOK, ZPAD)):
                    nc.gpsimd.memset(zpad[:, :, a:b], 0.0).then_inc(zero_ready, 1)
                pool.wait_ge(wuq_loaded, 16 * QC * (l + 1))
                for half in range(2):
                    dst = wuq[:, :, :, NOPE + ROPE:P].rearrange("p k h (a s r) -> p (k h) a s r", a=2, s=2)
                    src = wuq[:, :, :, NOPE:NOPE + ROPE].rearrange("p k h (a s r) -> p (k h) a s r", a=2, s=2)
                    nc.gpsimd.tensor_copy(dst[:, :, :, half, :], src[:, :, :, 1 - half, :]).then_inc(wuq_swapped, 1)
                ring_v.wait_empty(pool, (l, "krT", 1))
                pool.wait_ge(wuq_swapped, 2 * (l + 1))
                for h in range(1, HEADS):
                    nc.gpsimd.tensor_copy(kT[NOPE:P, h, :], kT[NOPE:P, 0, :]).then_inc(k_spread, 1)
                pool.wait_ge(k_spread, (HEADS - 1) * (l + 1))
                for k in range(CC):
                    pool.wait_ge(ln_centred, CC * l + k + 1)
                    nc.gpsimd.tensor_tensor(zsq[:, k, :], acc[:, k, :], acc[:, k, :], ALU.mult).then_inc(ln_squared, 1)
                pool.wait_ge(mod2_ready, l + 1)
                ring_v.wait_full(pool, (l, "ln", 1, 1))
                n = 0
                for i in range(8):
                    part = (2, 6, 3, 5)[i // 2]
                    for j in range(2):
                        d = 16 * l + n
                        if d >= 2:
                            wait_diag_used(pool, l, n - 2)
                        if i == 6 and j == 0:
                            for s in range(2):
                                pool.wait_ge(h2_stored[s], 16 * stores_of(l, TILES - s, s))
                            ring_a.wait_full(pool, (l, "h2T", TILES - 1, 1))
                        v = i % 2
                        if part == 6:
                            col = mod[:, 16:32].rearrange("p (k v) -> p k v", v=2)[:, 4 * j:4 * j + 4, v]
                        else:
                            col = ada_cols[l][:, :].rearrange("p (k v) -> p k v", v=2)[:, 8 * part + 4 * j:8 * part + 4 * j + 4, v]
                        nc.gpsimd.tensor_tensor(diag[:, n % 2].rearrange("p (a n) -> p a n", a=4),
                                                ident.unsqueeze(1).broadcast_to([P, 4, P]),
                                                col.unsqueeze(2).broadcast_to([P, 4, P]), ALU.mult).then_inc(diag_ready, 1)
                        n += 1
                ring_a.wait_full(pool, (l, "g2", 1, 1))
                pool.wait_ge(plan_ready, l + 1)
                start = pool.value_load(blocks[l][0:1, EXPERTS:EXPERTS + 1], min_val=0, max_val=100)
                count = pool.value_load(blocks[l][0:1, 2 * EXPERTS:2 * EXPERTS + 1], min_val=1, max_val=MAX_BLOCKS)

                def gather(n):
                    pool.wait_ge(tokens_given, n + 1)
                    pool.sem_inc(pool_passed, 1)
                    pool.indirect_dma_start(xg, None, h2_dram, bass.IndirectOffsetOnAxis(ap=token_col[:, 0:1], axis=0),
                                            bounds_check=TOK - 1, oob_is_err=False).then_inc(gathered, 16)

                gather(start + 2 * l)
                gather(start + (2 * l + 1))
                with pool.Fori(0, count) as i:
                    gather(start + i + (2 * l + 2))
                    pool.wait_ge(y_act, start + i + 2)
                    pool.wait_ge(y_dve, start + i + 2)
                    pool.sem_inc(pool_passed, 1)
                    pool.indirect_dma_start(y_dram, bass.IndirectOffsetOnAxis(ap=row_out[:, 0:1], axis=0), y_sb, None,
                                            bounds_check=2 * TOK - 1, oob_is_err=False).then_inc(y_stored, 16)
                for t in range(TILES):
                    pool.wait_ge(comb_loaded[t], 32 * (l + 1))
                    nc.gpsimd.tensor_tensor(comb[2 * t], comb[2 * t], comb[2 * t + 1], ALU.add).then_inc(pair_added, 1)

        @block.scalar
        def _(act):
            steps = [0]

            def step(ins):
                steps[0] += 1
                ins.then_inc(act_step, 1)
                act.wait_ge(act_step, steps[0])

            def row_stats(l):
                for t in range(TILES + 2):
                    if l == DEPTH and t >= 2:
                        act.wait_ge(final_ready, t - 1)
                        act.dma_start(y_sample[0, (t - 2) * P:(t - 1) * P, :] if t - 2 < LAT else y_prompt[0], xn[:, t - 2, :]).then_inc(outputs_done, 16)
                    if t >= TILES:
                        continue
                    if l >= 1:
                        act.wait_ge(comb_added, TILES * (l - 1) + t + 1)
                    else:
                        act.wait_ge(x_loaded[t * 2 // LAT], 16)
                    step(nc.scalar.activation(junk, x[:, t, :], ACT.Square, accum_out=stat[:, t:t + 1]))
                    nc.scalar.activation(stat[:, 8 + t:9 + t], stat[:, t:t + 1], ACT.Sqrt, scale=1.0 / D,
                                         bias=eps_t[:, 0:1]).then_inc(rms_stat, 1)

            ring_v.wait_empty(act, "cond")
            nc.scalar.activation(cond[:, :].rearrange("p (k v) -> p v k", v=32)[:, 0:2, :],
                                 cond_raw.rearrange("p (v k) -> p v k", v=2),
                                 ACT.Silu).then_inc(cond_ready, 1)
            act.sem_inc(y_act, 1)
            for l in range(DEPTH):
                def ada_rows(a, b):
                    for ch in range(a, b):
                        bank = ring_a.take(act, ("ada", ch))
                        if ch >= 2:
                            ring_v.wait_full(act, ("adaT", ch - 2))
                        nc.scalar.activation(ada_row[:, (ch % 2) * ADA_W:(ch % 2 + 1) * ADA_W], bank, ACT.Copy).then_inc(ring_a.empty, 1)

                row_stats(l)
                if l == 0:
                    ada_rows(0, ADA_FIRST)
                act.wait_ge(mod_ready, l + 1)

                def modulate(k, v, dst, src):
                    return nc.scalar.activation(dst, src, ACT.Identity, scale=mod[:, 2 * k + v:2 * k + v + 1],
                                                bias=ada_cols[l][:, 2 * k + v:2 * k + v + 1])

                for k in range(0, DK, 2):
                    bank = ring_a.take(act, (l, "xnT", k))
                    modulate(k, 0, hT[:, k, 0:DEC_SEQ], bank).then_inc(ring_a.empty, 1)
                bank = ring_a.take(act, (l, "xpT", 0))
                for k in range(4):
                    ins = modulate(k, 1, hT[:, k, DEC_SEQ:TOK], bank[:, k * P:(k + 1) * P])
                ins.then_inc(ring_a.empty, 1)
                for ct in range(CC):
                    if ct >= 2 or l >= 1:
                        ring_v.wait_empty(act, (l, "a_ctx", ct - 2) if ct >= 2 else (l - 1, "a_ctx", ct + 2))
                    for name, a, b in (("gate_lat", 0, DEC_SEQ), ("gate_ctx", DEC_SEQ, TOK)):
                        bank = ring_a.take(act, (l, name, ct))
                        nc.scalar.activation(sig[:, ct % 2, a:b], bank[:, 0:b - a], ACT.Sigmoid).then_inc(ring_a.empty, 1)
                    if l == 0:
                        ada_rows(ADA_FIRST + 2 * ct, ADA_FIRST + 2 * ct + 2)
                def latent_stats(t):
                    ring_a.wait_empty(act, (l, "qkv0", t))
                    ring_v.wait_empty(act, (l, "qkv1", t))
                    step(nc.scalar.activation(junk[:, 0:Q_LORA], proj[:, t, 0:Q_LORA], ACT.Square, accum_out=stat[:, 16 + t:17 + t]))
                    step(nc.scalar.activation(junk[:, 0:KV_LORA], proj[:, t, Q_LORA:Q_LORA + KV_LORA], ACT.Square, accum_out=stat[:, 24 + t:25 + t]))
                    for at, width in ((16, Q_LORA), (24, KV_LORA)):
                        nc.scalar.activation(stat[:, at + 16 + t:at + 17 + t], stat[:, at + t:at + t + 1], ACT.Sqrt, scale=1.0 / width,
                                             bias=eps_t[:, 0:1]).then_inc(qkv_stat, 1)

                for t in range(TILES):
                    bank = ring_a.take(act, (l, "qkv0", t))
                    nc.scalar.activation(proj[:, t, 0:512], bank, ACT.Copy).then_inc(ring_a.empty, 1)
                    if t >= 1:
                        latent_stats(t - 1)
                latent_stats(TILES - 1)
                act.wait_ge(qkv_normed, TILES * (l + 1))
                act.dma_start(new_ckv[0, l], proj[:, LAT, Q_LORA:Q_LORA + KV_LORA]).then_inc(ckv_out, 16)
                act.dma_start(new_krope[0, l], proj[:, LAT, Q_LORA + KV_LORA:QKV]).then_inc(ckv_out, 16)
                for k in range(QC):
                    bank = ring_a.take(act, (l, "qcT", k))
                    nc.scalar.activation(qcT[:, k, 0:DEC_SEQ], bank, ACT.Copy, scale=vec_col(l, V_QG + k)).then_inc(ring_a.empty, 1)
                bank = ring_a.take(act, (l, "qcT_ctx"))
                for k in range(QC):
                    ins = nc.scalar.activation(qcT[:, k, DEC_SEQ:TOK], bank[:, k * P:(k + 1) * P], ACT.Copy, scale=vec_col(l, V_QG + k))
                ins.then_inc(ring_a.empty, 1)
                for pr in range(HEADS // 2):
                    for name, a, b in (("k0", 0, 512), ("k1", 512, KEYS)):
                        bank = ring_a.take(act, (l, name, pr))
                        nc.scalar.activation(kT[0:NOPE, 2 * pr, a:b], bank[0:NOPE, 0:b - a], ACT.Copy)
                        nc.scalar.activation(kT[0:NOPE, 2 * pr + 1, a:b], bank[NOPE:P, 0:b - a], ACT.Copy).then_inc(ring_a.empty, 1)
                for t in range(6):
                    bank = ring_a.take(act, (l, "v", t))
                    nc.scalar.activation(v_sb[:, t, :], bank, ACT.Copy).then_inc(ring_a.empty, 1)

                def exponential(i):
                    n = LAT_KEYS if i % TILES < LAT else SEQ
                    u = UNITS * l + i
                    act.wait_ge(att_max, u + 1)
                    if i >= 2:
                        act.wait_ge(prob_turned, u - 1)
                    nc.scalar.activation(prob[:, i % 2, 0:n], flat[:, 1024 * (i % 2):1024 * (i % 2) + n], ACT.Exp,
                                         bias=att_stat[:, UNITS + i:UNITS + i + 1], scale=SCALE,
                                         accum_out=att_stat[:, 2 * UNITS + i:2 * UNITS + i + 1]).then_inc(att_exp, 1)

                def turned(i):
                    n = LAT_KEYS if i % TILES < LAT else SEQ
                    u = UNITS * l + i
                    act.wait_ge(prob_turned, u + 1)
                    if i >= 2:
                        act.wait_ge(att_out, u - 1)
                    nc.scalar.activation(probT[:, i % 2, 0:n], flat[:, 2048:2048 + n], ACT.Copy).then_inc(probT_ready, 1)

                exponential(0)
                for i in range(UNITS):
                    if l + 1 < DEPTH and 1 <= i <= ADA_NEXT_CHUNKS:
                        act.wait_ge(ada_next_full, ADA_NEXT_CHUNKS * l + i)
                        act.wait_ge(att_out, UNITS * l + i)
                        nc.scalar.activation(ada_next_row, ps[:, 7, 0:ADA_NEXT_W], ACT.Copy).then_inc(ada_next_taken, 1)
                    turned(i)
                    if i + 1 < UNITS:
                        exponential(i + 1)
                for k in range(4):
                    bank = ring_a.take(act, (l, "oT", k))
                    nc.scalar.activation(mixT[:, k, 0:DEC_SEQ], bank, ACT.Copy).then_inc(ring_a.empty, 1)
                bank = ring_a.take(act, (l, "oT_ctx"))
                nc.scalar.activation(mixT[:, 0:4, DEC_SEQ:TOK], bank.rearrange("p (k n) -> p k n", k=4), ACT.Copy).then_inc(ring_a.empty, 1)
                for j, (a, b) in enumerate(((0, 512), (512, CONV_OUT))):
                    ring_v.wait_full(act, (l, "ln", 1, j))
                    nc.scalar.activation(ln_rstd[:, a:b], ring_v.bank((l, "ln", 1, j))[:, 0:b - a], ACT.Sqrt,
                                         scale=1.0 / CONV_C, bias=eps_t[:, 0:1]).then_inc(ln_sqrt, 1)
                for k in range(CC):
                    act.wait_ge(ln_done, CC * l + k + 1)
                    for src, dst in (((0, 512), (0, 512)), ((512 + PAD, CONV_OUT), (512, TOK))):
                        nc.scalar.activation(mixT[:, 4 + k, dst[0]:dst[1]], acc[:, k, src[0]:src[1]], ACT.Silu,
                                             scale=vec_col(l, V_LG + k), bias=vec_col(l, V_LB + k)).then_inc(conv_silu, 1)

                def turned_h2(t):
                    for j in range(2):
                        bank = ring_a.take(act, (l, "h2T", t, j))
                        nc.scalar.activation(h2T[:, 4 * j:4 * j + 4, t * P:(t + 1) * P],
                                             bank.rearrange("p (k n) -> p k n", k=4), ACT.Copy).then_inc(ring_a.empty, 1)
                    if t >= 1:
                        logits_out(t - 1)

                def logits_out(t):
                    bank = ring_a.take(act, (l, "logits", t))
                    nc.scalar.activation(r_tmp[:, t * EXPERTS:(t + 1) * EXPERTS], bank[:, 0:EXPERTS], ACT.Copy).then_inc(ring_a.empty, 1)

                for t in range(TILES):
                    act.wait_ge(x_updated, 2 * (TILES * l + t + 1))
                    step(nc.scalar.activation(junk2, x[:, t, :], ACT.Square, accum_out=stat[:, 48 + t:49 + t]))
                    nc.scalar.activation(stat[:, 56 + t:57 + t], stat[:, 48 + t:49 + t], ACT.Sqrt, scale=1.0 / D,
                                         bias=eps_t[:, 0:1]).then_inc(h2_stat, 1)
                    act.wait_ge(h2_ready, TILES * l + t + 1)
                    act.dma_start(h2_dram[t * P:(t + 1) * P, :], h2s[:, t % 2]).then_inc(h2_stored[t % 2], 16)
                    if t >= 1:
                        turned_h2(t - 1)
                turned_h2(TILES - 1)
                logits_out(TILES - 1)
                ring_a.wait_empty(act, (l, "logits", TILES - 1))
                nc.scalar.activation(r_tmp[:, 0:TILES * EXPERTS], r_tmp[:, 0:TILES * EXPERTS], ACT.Sigmoid).then_inc(affinities_ready, 1)

                ring_v.wait_empty(act, (l, "wo", TILES - 1, 1))
                for v in range(2):
                    for j in range(2):
                        bank = ring_a.take(act, (l, "g2", v, j))
                        nc.scalar.activation(g2_bc(v)[:, j * 512:(j + 1) * 512], bank, ACT.Copy).then_inc(ring_a.empty, 1)

                if l == DEPTH - 1:
                    act.dma_start(final_bc, final_g.rearrange("(a n) -> a n", a=1).broadcast_to([P, D])).then_inc(final_loaded, 16)

                act.wait_ge(plan_ready, l + 1)
                start = act.value_load(blocks[l][0:1, EXPERTS:EXPERTS + 1], min_val=0, max_val=100)
                count = act.value_load(blocks[l][0:1, 2 * EXPERTS:2 * EXPERTS + 1], min_val=1, max_val=MAX_BLOCKS)

                def turn(n):
                    act.wait_ge(xT_full, n + 1)
                    nc.scalar.activation(xgT[:, 0:4, :], ps[:, 0].rearrange("p (k n) -> p k n", k=4), ACT.Copy).then_inc(xT_act, 1)

                turn(start + l)
                with act.Fori(0, count) as i:
                    g = start + i
                    act.wait_ge(gu_full, g + 1)
                    nc.scalar.activation(silu_g, ps[:, 2, 0:FF], ACT.Silu).then_inc(silu_ready, 1)
                    turn(g + l + 1)
                    act.wait_ge(y_full, g + 1)
                    act.wait_ge(y_stored, 16 * g)
                    nc.scalar.activation(y_sb[:, 0:512], ps[:, 4], ACT.Copy).then_inc(y_act, 1)
                act.wait_ge(y_stored, (start + count) * 16)
                act.sem_inc(act_passed, 1)
                for t in range(TILES):
                    for r in range(2):
                        act.dma_start(comb[2 * t + r], y_dram[r * TOK + t * P:r * TOK + (t + 1) * P, :]).then_inc(comb_loaded[t], 16)
            row_stats(DEPTH)

        @block.vector
        def _(dve):
            steps = [0]

            def step(ins):
                steps[0] += 1
                ins.then_inc(dve_step, 1)
                dve.wait_ge(dve_step, steps[0])

            def tt(out, a, b, op):
                return nc.vector.tensor_tensor(out, a, b, op)

            step(nc.vector.memset(eps_t[:, :], EPS))
            step(nc.vector.memset(block_total[:, :], 0.0))
            step(nc.vector.memset(nbf[:, :], 0.0))
            step(nc.vector.memset(cond[:, :], 0.0))
            bank = ring_v.take(dve, "cond")
            nc.vector.tensor_copy(cond_raw, bank[:, 0:2 * DK]).then_inc(ring_v.empty, 1)
            dve.sem_inc(y_dve, 1)
            for l in range(DEPTH):
                bank = ring_v.take(dve, (l, "vec"))
                step(nc.vector.tensor_copy(vec_cols[l][:, 0:VEC_ROWS], bank[:, 0:VEC_ROWS]))
                nc.vector.tensor_copy(vec_cols[l][:, P:P + CONV_K * CC], bank[:, P:P + CONV_K * CC]).then_inc(ring_v.empty, 1)
            ring_v.wait_empty(dve, (DEPTH - 1, "vec"))
            mod3 = mod[:, :].rearrange("p (k v) -> p k v", v=2)

            def normalise(l, t):
                dve.wait_ge(rms_stat, TILES * l + t + 1)
                step(nc.vector.reciprocal(stat[:, 8 + t:9 + t], stat[:, 8 + t:9 + t]))
                if l < DEPTH:
                    nc.vector.tensor_scalar(xn[:, t, :], x[:, t, :], stat[:, 8 + t:9 + t], None, ALU.mult).then_inc(xn_ready, 1)
                else:
                    dve.wait_ge(final_loaded, 16)
                    nc.vector.scalar_tensor_tensor(xn[:, t, :], x[:, t, :], stat[:, 8 + t:9 + t], final_bc, ALU.mult, ALU.mult).then_inc(final_ready, 1)

            for l in range(DEPTH):
                vecs = vec_cols[l]
                adat3 = ada_cols[l][:, :].rearrange("p (k v) -> p k v", v=2)

                def ada_columns(a, b):
                    for ch in range(a, b):
                        bank = ring_v.take(dve, ("adaT", ch))
                        tt(adat3[:, 4 * ch:4 * ch + 4, :], bank[:, 0:8].rearrange("p (k v) -> p k v", v=2),
                           vecs[:, V_BADA + 4 * ch:V_BADA + 4 * ch + 4].unsqueeze(2).broadcast_to([P, 4, 2]),
                           ALU.add).then_inc(ring_v.empty, 1)

                def norm_gains(i, done):
                    part, gains = ((1, V_G1), (4, V_G2))[i]
                    step(nc.vector.tensor_scalar(mod3[:, 8 * i:8 * i + 8, :], adat3[:, 8 * part:8 * part + 8, :], 1.0, None, ALU.add))
                    tt(mod3[:, 8 * i:8 * i + 8, :], mod3[:, 8 * i:8 * i + 8, :],
                       vecs[:, gains:gains + 8].unsqueeze(2).broadcast_to([P, 8, 2]), ALU.mult).then_inc(done, 1)

                if l == 0:
                    for t in range(TILES):
                        normalise(0, t)
                    ada_columns(0, ADA_FIRST)
                    ring_v.wait_empty(dve, ("adaT", ADA_FIRST - 1))
                norm_gains(0, mod_ready)
                dve.wait_ge(mod_ready, l + 1)

                def modulate(k, v, dst, src):
                    return nc.vector.tensor_scalar(dst, src, mod[:, 2 * k + v:2 * k + v + 1],
                                                   ada_cols[l][:, 2 * k + v:2 * k + v + 1], ALU.mult, ALU.add)

                for k in range(1, DK, 2):
                    bank = ring_v.take(dve, (l, "xnT", k))
                    modulate(k, 0, hT[:, k, 0:DEC_SEQ], bank).then_inc(ring_v.empty, 1)
                bank = ring_v.take(dve, (l, "xpT", 1))
                for k in range(4):
                    ins = modulate(4 + k, 1, hT[:, 4 + k, DEC_SEQ:TOK], bank[:, k * P:(k + 1) * P])
                ins.then_inc(ring_v.empty, 1)
                conv_list = [(ct, j) for pair in range(CC // 2) for j in range(CONV_K) for ct in (2 * pair, 2 * pair + 1)]
                conv_at = [0]

                def conv(n):
                    for ct, j in conv_list[conv_at[0]:conv_at[0] + n]:
                        m = conv_at[0]
                        w = vecs[:, P + j * CC + ct:P + j * CC + ct + 1]
                        if j == 0:
                            ring_v.wait_empty(dve, (l, "a_ctx", ct))
                            ins = nc.vector.tensor_scalar(acc[:, ct, :], zpad[:, ct, 0:CONV_OUT], w, vec_col(l, V_CB + ct), ALU.mult, ALU.add)
                        else:
                            dve.wait_ge(conv_step, l * len(conv_list) + m - 1)
                            ins = nc.vector.scalar_tensor_tensor(acc[:, ct, :], zpad[:, ct, j:j + CONV_OUT], w, acc[:, ct, :], ALU.mult, ALU.add)
                        ins.then_inc(conv_step, 1)
                        conv_at[0] += 1

                dve.wait_ge(zero_ready, 3 * (l + 1))
                for ct in range(CC):
                    for name, gate, a, b, at in (("a_lat", "gate_lat", 0, DEC_SEQ, PAD), ("a_ctx", "gate_ctx", DEC_SEQ, TOK, 2 * PAD)):
                        bank = ring_v.take(dve, (l, name, ct))
                        ring_a.wait_empty(dve, (l, gate, ct))
                        tt(zpad[:, ct, a + at:b + at], bank[:, 0:b - a], sig[:, ct % 2, a:b], ALU.mult).then_inc(ring_v.empty, 1)
                    if l == 0:
                        ada_columns(ADA_FIRST + 2 * ct, ADA_FIRST + 2 * ct + 2)
                    conv(CONV_EARLY[ct])
                if l == 0:
                    ring_v.wait_empty(dve, ("adaT", ADA_CHUNKS - 1))
                norm_gains(1, mod2_ready)

                def latent_norm(t):
                    dve.wait_ge(qkv_stat, 2 * (TILES * l + t + 1))
                    step(nc.vector.reciprocal(stat[:, 32 + t:33 + t], stat[:, 32 + t:33 + t]))
                    step(nc.vector.reciprocal(stat[:, 40 + t:41 + t], stat[:, 40 + t:41 + t]))
                    dve.wait_ge(kvg_loaded, 16 * (l + 1))
                    nc.vector.tensor_scalar(proj[:, t, 0:Q_LORA], proj[:, t, 0:Q_LORA], stat[:, 32 + t:33 + t], None, ALU.mult)
                    nc.vector.scalar_tensor_tensor(proj[:, t, Q_LORA:Q_LORA + KV_LORA], proj[:, t, Q_LORA:Q_LORA + KV_LORA],
                                                   stat[:, 40 + t:41 + t], kvg, ALU.mult, ALU.mult).then_inc(qkv_normed, 1)

                for t in range(TILES):
                    bank = ring_v.take(dve, (l, "qkv1", t))
                    nc.vector.tensor_copy(proj[:, t, 512:QKV], bank[:, 0:QKV - 512]).then_inc(ring_v.empty, 1)
                    if t < TILES - 1:
                        conv(10)
                    if t >= 1:
                        latent_norm(t - 1)
                latent_norm(TILES - 1)
                step(nc.vector.memset(kr[:, :, 0:NOPE], 0.0))
                kin = proj[:, 0:LAT, Q_LORA + KV_LORA:QKV]
                kcos = con[:, C_KC:C_KC + LAT * ROPE].rearrange("p (t n) -> p t n", t=LAT)
                ksin = con[:, C_KS:C_KS + LAT * ROPE].rearrange("p (t n) -> p t n", t=LAT)
                half = lambda ap, s: ap.rearrange("p t (a s r) -> p t a s r", a=2, s=2)[:, :, :, s, :]
                k1, k2 = kr[:, 0:LAT, NOPE:NOPE + ROPE], kr[:, 0:LAT, NOPE + ROPE:P]
                step(tt(k1, kin, kcos, ALU.mult))
                step(tt(half(k2, 0), half(kin, 1), half(ksin, 0), ALU.mult))
                step(tt(half(k2, 1), half(kin, 0), half(ksin, 1), ALU.mult))
                step(tt(k1, k1, k2, ALU.add))
                step(nc.vector.tensor_copy(k2, k1))
                dve.wait_ge(cache_loaded, 32 * (l + 1))
                for s in range(2):
                    a = NOPE + s * ROPE
                    step(nc.vector.tensor_copy(kr[:, 4, a:a + ROPE], cache_sb[:, KV_LORA:KV_LORA + ROPE]))
                    ins = nc.vector.tensor_copy(kr[:, 5, a:a + ROPE], proj[:, LAT, Q_LORA + KV_LORA:QKV])
                    if s == 0:
                        step(ins)
                ins.then_inc(krope_ready, 1)
                for k in range(KC):
                    bank = ring_v.take(dve, (l, "ckvT", k))
                    nc.vector.tensor_copy(ckvT[:, k, 0:DEC_SEQ], bank).then_inc(ring_v.empty, 1)
                for k in range(KC):
                    bank = ring_v.take(dve, (l, "ckvT_rest", k))
                    nc.vector.tensor_copy(ckvT[:, k, DEC_SEQ:KEYS], bank[:, 0:256]).then_inc(ring_v.empty, 1)
                bank = ring_v.take(dve, (l, "krT", 0))
                nc.vector.tensor_copy(kT[NOPE:P, 0, 0:512], bank[NOPE:P, :]).then_inc(ring_v.empty, 1)
                bank = ring_v.take(dve, (l, "krT", 1))
                nc.vector.tensor_copy(kT[NOPE:P, 0, 512:KEYS], bank[NOPE:P, 0:256]).then_inc(ring_v.empty, 1)
                tab = con[:, C_TAB:C_TAB + TOK]
                for h in range(HEADS):
                    bank = ring_v.take(dve, (l, "q", h))
                    tt(qT[:, h, 0:DEC_SEQ], bank, tab[:, 0:DEC_SEQ], ALU.mult).then_inc(ring_v.empty, 1)
                    conv(2)
                for j in range(2):
                    bank = ring_v.take(dve, (l, "q_ctx", j))
                    tt(qT[:, 4 * j:4 * j + 4, DEC_SEQ:TOK], bank.rearrange("p (h n) -> p h n", h=4),
                       tab[:, DEC_SEQ:TOK].unsqueeze(1).broadcast_to([P, 4, P]), ALU.mult).then_inc(ring_v.empty, 1)
                def maximum(i):
                    n = LAT_KEYS if i % TILES < LAT else SEQ
                    dve.wait_ge(scores, UNITS * l + i + 1)
                    step(nc.vector.reduce_max(att_stat[:, i:i + 1], flat[:, 1024 * (i % 2):1024 * (i % 2) + n], AXIS_X))
                    nc.vector.tensor_scalar(att_stat[:, UNITS + i:UNITS + i + 1], att_stat[:, i:i + 1], -SCALE, None, ALU.mult).then_inc(att_max, 1)

                def output(i):
                    h, t = divmod(i, TILES)
                    dve.wait_ge(att_out, UNITS * l + i + 1)
                    step(nc.vector.reciprocal(att_stat[:, 3 * UNITS + i:3 * UNITS + i + 1], att_stat[:, 2 * UNITS + i:2 * UNITS + i + 1]))
                    if l + 1 < DEPTH and 1 <= i <= ADA_NEXT_CHUNKS:
                        k = 2 * (i - 1)
                        tt(ada_cols[l + 1][:, 2 * k:2 * k + 4].rearrange("p (k v) -> p k v", v=2),
                           ps[:, 6, VH:VH + 4].rearrange("p (k v) -> p k v", v=2),
                           vec_cols[l + 1][:, V_BADA + k:V_BADA + k + 2].unsqueeze(2).broadcast_to([P, 2, 2]), ALU.add)
                    nc.vector.tensor_scalar(o_tok[:, t, h * VH:(h + 1) * VH], ps[:, 6, 0:VH],
                                            att_stat[:, 3 * UNITS + i:3 * UNITS + i + 1], None, ALU.mult).then_inc(att_out_empty, 1)

                dve.wait_ge(ckv_out, 32 * (l + 1))
                for i in range(UNITS):
                    maximum(i)
                    if i >= 2:
                        output(i - 2)
                    conv(1)
                output(UNITS - 2)
                output(UNITS - 1)
                conv(len(conv_list))
                dve.wait_ge(conv_step, (l + 1) * len(conv_list))
                halves = ((0, 512), (512, CONV_OUT))
                for j, (a, b) in enumerate(halves):
                    bank = ring_v.take(dve, (l, "ln", 0, j))
                    for k in range(CC):
                        ins = nc.vector.scalar_tensor_tensor(acc[:, k, a:b], bank[:, 0:b - a], -1.0 / CONV_C, acc[:, k, a:b], ALU.mult, ALU.add)
                        if j == 0:
                            if k == CC - 1:
                                ins.then_inc(ring_v.empty, 1)
                        elif k < CC - 1:
                            ins.then_inc(ln_centred, 1)
                        else:
                            step(ins)
                dve.sem_inc(ln_centred, 1)
                dve.sem_inc(ring_v.empty, 1)
                for j, (a, b) in enumerate(halves):
                    dve.wait_ge(ln_sqrt, 2 * l + j + 1)
                    step(nc.vector.reciprocal(ln_rstd[:, a:b], ln_rstd[:, a:b]))
                    dve.sem_inc(ring_v.empty, 1)
                for k in range(CC):
                    tt(acc[:, k, :], acc[:, k, :], ln_rstd, ALU.mult).then_inc(ln_done, 1)
                dve.wait_ge(conv_silu, 2 * CC * (l + 1))
                for i in range(6):
                    for j in range(2):
                        bank = ring_v.take(dve, (l, "bc", i, j))
                        nc.vector.tensor_copy(bc[:, i, j * 512:(j + 1) * 512], bank).then_inc(ring_v.empty, 1)
                ring_v.wait_empty(dve, (l, "bc", 5, 1))
                for t in range(TILES):
                    v = 0 if t < LAT else 1
                    for j in range(2):
                        cols = slice(j * 512, (j + 1) * 512)
                        bank = ring_v.take(dve, (l, "wo", t, j))
                        tt(res_tmp[:, cols], bank, g1_bc(v)[:, cols], ALU.mult).then_inc(ring_v.empty, 1)
                        ring_v.wait_empty(dve, (l, "wo", t, j))
                        tt(x[:, t, cols], x[:, t, cols], res_tmp[:, cols], ALU.add).then_inc(x_updated, 1)
                    dve.wait_ge(h2_stat, TILES * l + t + 1)
                    step(nc.vector.reciprocal(stat[:, 56 + t:57 + t], stat[:, 56 + t:57 + t]))
                    if t >= 2:
                        dve.wait_ge(h2_stored[t % 2], 16 * stores_of(l, t, t % 2))
                        ring_a.wait_full(dve, (l, "h2T", t - 2, 1))
                    step(nc.vector.scalar_tensor_tensor(h2s[:, t % 2], x[:, t, :], stat[:, 56 + t:57 + t], a2_bc(v), ALU.mult, ALU.mult))
                    tt(h2s[:, t % 2], h2s[:, t % 2], sh2_bc(v), ALU.add).then_inc(h2_ready, 1)

                cur = [80]

                def temp(n):
                    a = cur[0]
                    cur[0] += n
                    return r_tmp[:, a:a + n]

                t16 = lambda ap: ap.rearrange("p (t e) -> p t e", t=TILES)
                over16 = lambda ap, n=EXPERTS: ap.unsqueeze(2).broadcast_to([P, TILES, n])
                aff = t16(r_tmp[:, 0:80])
                w16 = con[:, C_W16:C_W16 + EXPERTS].unsqueeze(1).broadcast_to([P, TILES, EXPERTS])
                w4 = con[:, C_W4:C_W4 + GROUPS].unsqueeze(1).broadcast_to([P, TILES, GROUPS])
                dve.wait_ge(affinities_ready, l + 1)
                sel = temp(80)
                step(tt(t16(sel), aff, rb[:, :].unsqueeze(1).broadcast_to([P, TILES, EXPERTS]), ALU.add))
                TG = TILES * GROUPS
                s4 = sel.rearrange("p (g m) -> p g m", m=PER_GROUP)
                sums = temp(TG * 6).rearrange("p (g m) -> p g m", m=6)
                for n, m, at in ((3, 3, 0), (2, 2, 3), (1, 1, 5)):
                    step(tt(sums[:, :, at:at + n], s4[:, :, 0:n], s4[:, :, m:m + 1].broadcast_to([P, TG, n]), ALU.add))
                score = temp(TG)
                step(nc.vector.reduce_max(score, sums, AXIS_X))

                def first_max(values, weights, out, width):
                    top = temp(TILES)
                    v3 = values.rearrange("p (t e) -> p t e", t=TILES)
                    o3 = out.rearrange("p (t e) -> p t e", t=TILES)
                    step(nc.vector.reduce_max(top, v3, AXIS_X))
                    step(tt(o3, v3, over16(top, width), ALU.is_equal))
                    step(tt(o3, o3, weights, ALU.mult))
                    step(nc.vector.reduce_max(top, o3, AXIS_X))
                    step(tt(o3, o3, over16(top, width), ALU.is_equal))

                in_group = temp(TG)
                first_max(score, w4, in_group, GROUPS)
                outside = temp(TG)
                step(nc.vector.tensor_scalar(outside, in_group, 1.0, BIG, ALU.subtract, ALU.mult))
                step(tt(s4, s4, in_group.unsqueeze(2).broadcast_to([P, TG, PER_GROUP]), ALU.mult))
                step(tt(s4, s4, outside.unsqueeze(2).broadcast_to([P, TG, PER_GROUP]), ALU.add))
                hot = [temp(80), temp(80)]
                first_max(sel, w16, hot[0], EXPERTS)
                step(nc.vector.scalar_tensor_tensor(sel, hot[0], -2 * BIG, sel, ALU.mult, ALU.add))
                first_max(sel, w16, hot[1], EXPERTS)
                both, sums_before = temp(80), temp(96)
                assert BOTH_AT == cur[0] - 176
                step(nc.vector.memset(sums_before[:, 0:EXPERTS], 0.0))
                step(tt(both, hot[0], hot[1], ALU.add))
                for t in range(TILES):
                    a = t * EXPERTS
                    step(tt(sums_before[:, a + EXPERTS:a + 2 * EXPERTS], sums_before[:, a:a + EXPERTS], both[:, a:a + EXPERTS], ALU.add))
                dve.sem_inc(masks_ready, 1)
                top_aff, total, prod = temp(2 * TILES), temp(TILES), temp(80)
                for r in range(2):
                    step(tt(t16(prod), aff, t16(hot[r]), ALU.mult))
                    step(nc.vector.reduce_sum(top_aff[:, r * TILES:(r + 1) * TILES], t16(prod), AXIS_X))
                step(tt(total, top_aff[:, 0:TILES], top_aff[:, TILES:2 * TILES], ALU.add))
                step(nc.vector.reciprocal(total, total))
                gate_of = temp(TR)
                for r in range(2):
                    step(tt(gate_of[:, r * TILES:(r + 1) * TILES], top_aff[:, r * TILES:(r + 1) * TILES], total, ALU.mult))
                row_of = temp(TR)
                for r in range(2):
                    step(nc.vector.tensor_scalar(row_of[:, r * TILES:(r + 1) * TILES], con[:, C_TOKID:C_TOKID + TILES], float(r * TOK + 1), None, ALU.add))
                bank = ring_v.take(dve, (l, "slots"))
                row = lambda i: nbf[:, 24 * i + 8:24 * i + 24]
                row_shift = lambda i, s: nbf[:, 24 * i + 8 - s:24 * i + 24 - s]
                count_int = temp(EXPERTS).bitcast(INT32)
                step(nc.vector.tensor_scalar(count_int, bank[:, 80:96], float(P - 1), None, ALU.add))
                step(nc.vector.tensor_scalar(count_int, count_int, 7, None, ALU.logical_shift_right))
                step(nc.vector.tensor_scalar(row(0), count_int, 1.0, None, ALU.max))
                step(tt(row(1), row(0), row_shift(0, 1), ALU.add))
                step(tt(row(2), row(1), row_shift(1, 2), ALU.add))
                step(tt(row(1), row(2), row_shift(2, 4), ALU.add))
                step(tt(row(2), row(1), row_shift(1, 8), ALU.add))
                step(tt(row(3), row(2), row(0), ALU.subtract))
                place = temp(80)
                step(nc.vector.tensor_scalar(row(1), row(3), float(P), None, ALU.mult))
                step(tt(t16(place), t16(bank[:, 0:80]), row(1).unsqueeze(1).broadcast_to([P, TILES, EXPERTS]), ALU.add))
                dve.sem_inc(ring_v.empty, 1)
                found, part = temp(TR), temp(2 * TR)
                part_int = temp(2 * TR).bitcast(INT32)
                for r in range(2):
                    step(tt(t16(prod), t16(place), t16(hot[r]), ALU.mult))
                    step(nc.vector.reduce_sum(found[:, r * TILES:(r + 1) * TILES], t16(prod), AXIS_X))
                step(nc.vector.tensor_copy(part_int[:, 0:TR], found))
                step(nc.vector.tensor_scalar(part_int[:, TR:2 * TR], part_int[:, 0:TR], 7, None, ALU.logical_shift_right))
                step(nc.vector.tensor_scalar(part_int[:, 0:TR], part_int[:, 0:TR], P - 1, None, ALU.bitwise_and))
                step(nc.vector.tensor_copy(part, part_int))
                step(tt(hot_block, con[:, C_BLK:C_BLK + NB].unsqueeze(1).broadcast_to([P, TR, NB]), part[:, TR:2 * TR].unsqueeze(2).broadcast_to([P, TR, NB]), ALU.is_equal))
                for n, value in enumerate((row_of, gate_of)):
                    step(tt(table_rhs[:, :, n * NB:(n + 1) * NB], hot_block, value.unsqueeze(2).broadcast_to([P, TR, NB]), ALU.mult))
                ramp = con[:, C_RAMP:C_RAMP + P]
                step(tt(hot_place, ramp.unsqueeze(1).broadcast_to([P, TR, P]), part[:, 0:TR].unsqueeze(2).broadcast_to([P, TR, P]), ALU.is_equal))
                dve.sem_inc(table_rhs_ready, 1)
                step(nc.vector.tensor_copy(blocks[l][0:1, 0:EXPERTS], row(0)[0:1]))
                step(nc.vector.tensor_scalar(blocks[l][0:1, EXPERTS:2 * EXPERTS], row(3)[0:1], block_total[0:1, 0:1], None, ALU.add))
                step(nc.vector.tensor_copy(blocks[l][0:1, 2 * EXPERTS:2 * EXPERTS + 1], row(2)[0:1, EXPERTS - 1:EXPERTS]))
                step(tt(block_total[0:1, 0:1], block_total[0:1, 0:1], row(2)[0:1, EXPERTS - 1:EXPERTS], ALU.add))
                bank = ring_v.take(dve, (l, "table"))
                free, row_f, wrap = (hot_block[:, n, :] for n in range(3))
                step(nc.vector.tensor_scalar(free, bank[:, 0:NB], 0.5, float(NO_ROW), ALU.is_lt, ALU.mult))
                step(nc.vector.scalar_tensor_tensor(row_f, bank[:, 0:NB], -1.0, free, ALU.add, ALU.add))
                step(nc.vector.tensor_scalar(wrap, row_f, TOK - 0.5, float(-TOK), ALU.is_gt, ALU.mult))
                step(tt(slot_tokens, row_f, wrap, ALU.add))
                step(nc.vector.tensor_copy(slot_rows, row_f))
                step(nc.vector.tensor_copy(slot_gates, bank[:, NB:2 * NB]))
                dve.sem_inc(ring_v.empty, 1)
                dve.sem_inc(plan_ready, 1)

                start = dve.value_load(blocks[l][0:1, EXPERTS:EXPERTS + 1], min_val=0, max_val=100)
                count = dve.value_load(blocks[l][0:1, 2 * EXPERTS:2 * EXPERTS + 1], min_val=1, max_val=MAX_BLOCKS)

                def give_tokens(i):
                    nc.vector.tensor_copy(token_col[:, :], slot_tokens[:, bass.ds(i, 1)]).then_inc(tokens_given, 1)

                def turn(n):
                    dve.wait_ge(xT_full, n + 1)
                    nc.vector.tensor_copy(xgT[:, 4:8, :], ps[:, 1].rearrange("p (k n) -> p k n", k=4)).then_inc(xT_dve, 1)

                give_tokens(0)
                turn(start + l)
                give_tokens(1)
                with dve.Fori(0, count) as i:
                    g = start + i
                    dve.wait_ge(silu_ready, g + 1)
                    nc.vector.scalar_tensor_tensor(hid, ps[:, 2, FF:2 * FF], slot_gates[:, bass.ds(i, 1)], silu_g, ALU.mult, ALU.mult).then_inc(hid_ready, 1)
                    dve.wait_ge(hidT_full, g + 1)
                    nc.vector.tensor_copy(hidT, ps[:, 3, 0:256].rearrange("p (k n) -> p k n", k=2)).then_inc(hidT_ready, 1)
                    turn(g + (l + 1))
                    give_tokens(i + 2)
                    dve.wait_ge(y_stored, 16 * g)
                    nc.vector.tensor_copy(row_out[:, :], slot_rows[:, bass.ds(i, 1)])
                    dve.wait_ge(y_full, g + 1)
                    nc.vector.tensor_copy(y_sb[:, 512:1024], ps[:, 5]).then_inc(y_dve, 1)
                for t in range(TILES):
                    v = 0 if t < LAT else 1
                    a = comb[2 * t]
                    dve.wait_ge(pair_added, TILES * l + t + 1)
                    step(tt(a, a, g2_bc(v), ALU.mult))
                    tt(x[:, t, :], x[:, t, :], a, ALU.add).then_inc(comb_added, 1)
                    if t >= 1:
                        normalise(l + 1, t - 1)
                normalise(l + 1, TILES - 1)

        @block.tensor
        def _(pe):
            def product(out, lhs, rhs, n):
                for k in range(n):
                    ins = nc.tensor.matmul(out, lhs(k), rhs(k), start=(k == 0), stop=(k == n - 1))
                return ins

            pe.wait_ge(const_loaded, 16)
            pe.wait_ge(cond_loaded, 32)
            bank = ring_v.open(pe, "cond")
            nc.tensor.transpose(bank[:, 0:2 * DK], cond_rows[0:2 * DK, :], ident[0:2 * DK, 0:2 * DK]).then_inc(ring_v.full, 1)
            pe.wait_ge(rows_loaded, 128 * DEPTH + 32)
            for l in range(DEPTH):
                bank = ring_v.open(pe, (l, "vec"))
                nc.tensor.transpose(bank[:, 0:VEC_ROWS], vec_rows[l][0:VEC_ROWS, 0:P], ident[0:VEC_ROWS, 0:VEC_ROWS])
                nc.tensor.transpose(bank[:, P:P + CONV_K * CC], vec_rows[l][0:CONV_K * CC, P:2 * P],
                                    ident[0:CONV_K * CC, 0:CONV_K * CC]).then_inc(ring_v.full, 1)
            pe.wait_ge(cond_ready, 1)

            def conditioning(out, w):
                for k in range(DK):
                    j = 32 * (k % 4)
                    ins = nc.tensor.matmul(out[j:j + 32], cond[:, 32 * k:32 * k + 32], w[:, k, :], start=(k < 4), stop=(k >= 4))
                return ins

            sel = con[:, C_SEL:C_SEL + 2]

            for l in range(DEPTH):
                if l >= 1:
                    end = pe.value_load(blocks[l - 1][0:1, 2 * EXPERTS - 1:2 * EXPERTS], min_val=0, max_val=100)
                    n_last = pe.value_load(blocks[l - 1][0:1, EXPERTS - 1:EXPERTS], min_val=1, max_val=5)
                    for s in (y_act, y_dve):
                        pe.wait_ge(s, end + n_last + 1)
                    for s in (xT_act, xT_dve):
                        pe.wait_ge(s, end + n_last + l)
                    pe.sem_inc(pe_passed, 1)

                def ada_turn(ch):
                    ring_a.wait_empty(pe, ("ada", ch))
                    bank = ring_v.open(pe, ("adaT", ch))
                    for j in range(4):
                        at = (ch % 2) * ADA_W + j * P
                        ins = nc.tensor.matmul(bank[:, 2 * j:2 * j + 2], ada_row[:, at:at + P], sel, start=True, stop=True)
                    ins.then_inc(ring_v.full, 1)

                def ada(a, b):
                    for ch in range(a, b):
                        pe.wait_ge(ada_loaded[ada_buffer(ch)], 16 if ch < ADA_FIRST else 16 * ((ch - ADA_FIRST) // 2 + 2))
                        bank = ring_a.open(pe, ("ada", ch))
                        conditioning(bank, ada_w[ada_buffer(ch)]).then_inc(ring_a.full, 1)
                        if ch > a:
                            ada_turn(ch - 1)
                    ada_turn(b - 1)

                if l == 0:
                    ada(0, ADA_FIRST)
                pe.wait_ge(xn_ready, TILES * (l + 1))
                for k in range(DK):
                    ring = ring_v if k % 2 else ring_a
                    bank = ring.open(pe, (l, "xnT", k))
                    for t in range(LAT):
                        ins = nc.tensor.transpose(bank[:, t * P:(t + 1) * P], xn[:, t, k * P:(k + 1) * P], ident)
                    ins.then_inc(ring.full, 1)
                for j, ring in enumerate((ring_a, ring_v)):
                    bank = ring.open(pe, (l, "xpT", j))
                    for k in range(4):
                        ins = nc.tensor.transpose(bank[:, k * P:(k + 1) * P], xn[:, LAT, (4 * j + k) * P:(4 * j + k + 1) * P], ident)
                    ins.then_inc(ring.full, 1)
                ring_a.wait_empty(pe, (l, "xpT", 0))
                ring_v.wait_empty(pe, (l, "xpT", 1))
                for ct in range(CC):
                    pe.wait_ge(win_conv_loaded[ct], 32 * (l + 1))
                    for ring, name, col in ((ring_a, "gate", QKV + CONV_C + ct * P), (ring_v, "a", QKV + ct * P)):
                        for part, a, b in (("_lat", 0, DEC_SEQ), ("_ctx", DEC_SEQ, TOK)):
                            bank = ring.open(pe, (l, name + part, ct))
                            product(bank[:, 0:b - a], lambda k: win[:, k, col:col + P], lambda k: hT[:, k, a:b], DK).then_inc(ring.full, 1)
                    if l == 0:
                        ada(ADA_FIRST + 2 * ct, ADA_FIRST + 2 * ct + 2)
                pe.wait_ge(win_qkv_loaded, 16 * (l + 1))
                for t in range(TILES):
                    for ring, name, a, b in ((ring_a, "qkv0", 0, 512), (ring_v, "qkv1", 512, QKV)):
                        bank = ring.open(pe, (l, name, t))
                        product(bank[:, 0:b - a], lambda k: hT[:, k, t * P:(t + 1) * P], lambda k: win[:, k, a:b], DK).then_inc(ring.full, 1)
                pe.wait_ge(qkv_normed, TILES * (l + 1))
                for k in range(QC):
                    bank = ring_a.open(pe, (l, "qcT", k))
                    for t in range(LAT):
                        ins = nc.tensor.transpose(bank[:, t * P:(t + 1) * P], proj[:, t, k * P:(k + 1) * P], ident)
                    ins.then_inc(ring_a.full, 1)
                bank = ring_a.open(pe, (l, "qcT_ctx"))
                for k in range(QC):
                    ins = nc.tensor.transpose(bank[:, k * P:(k + 1) * P], proj[:, LAT, k * P:(k + 1) * P], ident)
                ins.then_inc(ring_a.full, 1)
                for k in range(KC):
                    bank = ring_v.open(pe, (l, "ckvT", k))
                    for t in range(LAT):
                        ins = nc.tensor.transpose(bank[:, t * P:(t + 1) * P], proj[:, t, Q_LORA + k * P:Q_LORA + (k + 1) * P], ident)
                    ins.then_inc(ring_v.full, 1)
                pe.wait_ge(cache_loaded, 32 * (l + 1))
                for k in range(KC):
                    bank = ring_v.open(pe, (l, "ckvT_rest", k))
                    nc.tensor.transpose(bank[:, 0:P], cache_sb[:, k * P:(k + 1) * P], ident)
                    nc.tensor.transpose(bank[:, P:2 * P], proj[:, LAT, Q_LORA + k * P:Q_LORA + (k + 1) * P], ident).then_inc(ring_v.full, 1)
                pe.wait_ge(krope_ready, l + 1)
                for j, tiles in enumerate(((0, 1, 2, 3), (4, 5))):
                    bank = ring_v.open(pe, (l, "krT", j))
                    for n, t in enumerate(tiles):
                        ins = nc.tensor.transpose(bank[:, n * P:(n + 1) * P], kr[:, t, :], ident)
                    ins.then_inc(ring_v.full, 1)
                pe.wait_ge(wuq_swapped, 2 * (l + 1))
                ring_a.wait_empty(pe, (l, "qcT_ctx"))
                for h in range(HEADS):
                    bank = ring_v.open(pe, (l, "q", h))
                    product(bank, lambda k: wuq[:, k, h, :], lambda k: qcT[:, k, 0:DEC_SEQ], QC).then_inc(ring_v.full, 1)
                for j in range(2):
                    bank = ring_v.open(pe, (l, "q_ctx", j))
                    for h in range(4):
                        ins = product(bank[:, h * P:(h + 1) * P], lambda k: wuq[:, k, 4 * j + h, :], lambda k: qcT[:, k, DEC_SEQ:TOK], QC)
                    ins.then_inc(ring_v.full, 1)
                pe.wait_ge(wukv_loaded, 16 * 2 * KC * (l + 1))
                ring_v.wait_empty(pe, (l, "ckvT_rest", KC - 1))
                for pr in range(HEADS // 2):
                    for name, a, b in (("k0", 0, 512), ("k1", 512, KEYS)):
                        bank = ring_a.open(pe, (l, name, pr))
                        product(bank[:, 0:b - a], lambda k: wk[:, k, pr * P:(pr + 1) * P], lambda k: ckvT[:, k, a:b], KC).then_inc(ring_a.full, 1)
                for t in range(6):
                    bank = ring_a.open(pe, (l, "v", t))
                    product(bank, lambda k: ckvT[:, k, t * P:(t + 1) * P], lambda k: wv[:, k, :], KC).then_inc(ring_a.full, 1)

                pe.wait_ge(k_spread, (HEADS - 1) * (l + 1))
                ring_a.wait_empty(pe, (l, "v", 5))
                ring_v.wait_empty(pe, (l, "q_ctx", 1))

                def score(i):
                    h, t = divmod(i, TILES)
                    b = 2 * (i % 2)
                    if i >= 2:
                        pe.wait_ge(att_exp, UNITS * l + i - 1)
                    q = qT[:, h, t * P:(t + 1) * P]
                    if t < LAT:
                        nc.tensor.matmul(ps[:, b], q, kT[:, h, 0:512], start=True, stop=True)
                        nc.tensor.matmul(ps[:, b + 1, 0:P], q, kT[:, h, 512:LAT_KEYS], start=True, stop=True).then_inc(scores, 1)
                    else:
                        nc.tensor.matmul(ps[:, b, 0:P], q, kT[:, h, LAT_KEYS:KEYS], start=True, stop=True).then_inc(scores, 1)

                score(0)
                score(1)
                for i in range(UNITS):
                    h, t = divmod(i, TILES)
                    u = UNITS * l + i
                    key_tiles = range(LAT + 1) if t < LAT else range(5, 6)
                    pe.wait_ge(att_exp, u + 1)
                    if i >= 1:
                        pe.wait_ge(probT_ready, u)
                    for n, kt in enumerate(key_tiles):
                        ins = nc.tensor.transpose(flat[:, 2048 + n * P:2048 + (n + 1) * P], prob[:, i % 2, n * P:(n + 1) * P], ident)
                    ins.then_inc(prob_turned, 1)
                    if i + 2 < UNITS:
                        score(i + 2)
                    if i >= 1:
                        pe.wait_ge(att_out_empty, u)
                    if l + 1 < DEPTH and 1 <= i <= ADA_NEXT_CHUNKS:
                        pe.wait_ge(ada_next_taken, ADA_NEXT_CHUNKS * l + i)
                        for j in range(2):
                            nc.tensor.matmul(ps[:, 6, VH + 2 * j:VH + 2 * j + 2], ada_next_row[:, j * P:(j + 1) * P], sel, start=True, stop=True)
                    if l + 1 < DEPTH and i < ADA_NEXT_CHUNKS:
                        pe.wait_ge(ada_next_loaded[i % 2], 16 * (ADA_NEXT_CHUNKS // 2 * l + i // 2 + 1))
                        conditioning(ps[:, 7, 0:ADA_NEXT_W], ada_next[i % 2]).then_inc(ada_next_full, 1)
                    pe.wait_ge(probT_ready, u + 1)
                    for n, kt in enumerate(key_tiles):
                        ins = nc.tensor.matmul(ps[:, 6, 0:VH], probT[:, i % 2, n * P:(n + 1) * P],
                                               v_sb[:, kt, h * VH:(h + 1) * VH], start=(n == 0), stop=(n == len(key_tiles) - 1))
                    ins.then_inc(att_out, 1)
                pe.wait_ge(att_out_empty, UNITS * (l + 1))
                pe.wait_ge(probT_ready, UNITS * (l + 1))
                for k in range(4):
                    bank = ring_a.open(pe, (l, "oT", k))
                    for t in range(LAT):
                        ins = nc.tensor.transpose(bank[:, t * P:(t + 1) * P], o_tok[:, t, k * P:(k + 1) * P], ident)
                    ins.then_inc(ring_a.full, 1)
                bank = ring_a.open(pe, (l, "oT_ctx"))
                for k in range(4):
                    ins = nc.tensor.transpose(bank[:, k * P:(k + 1) * P], o_tok[:, LAT, k * P:(k + 1) * P], ident)
                ins.then_inc(ring_a.full, 1)
                pe.wait_ge(conv_step, (l + 1) * CONV_K * CC)
                for s in range(2):
                    if s == 1:
                        pe.wait_ge(ln_squared, CC * (l + 1))
                    src = zsq if s else acc
                    for j, (a, b) in enumerate(((0, 512), (512, CONV_OUT))):
                        bank = ring_v.open(pe, (l, "ln", s, j))
                        product(bank[:, 0:b - a], lambda k: ones, lambda k: src[:, k, a:b], CC).then_inc(ring_v.full, 1)

                def spread(ring, key, d):
                    pe.wait_ge(diag_ready, d + 1)
                    bank = ring.open(pe, key)
                    nc.tensor.matmul(bank, ones, diag[:, d % 2], start=True, stop=True).then_inc(ring.full, 1)

                for n in range(12):
                    spread(ring_v, (l, "bc", n // 2, n % 2), 16 * l + n)
                pe.wait_ge(wout_loaded, 16 * (l + 1))
                pe.wait_ge(conv_silu, 2 * CC * (l + 1))
                ring_a.wait_empty(pe, (l, "oT_ctx"))

                def h2_turn(t):
                    pe.wait_ge(h2_ready, TILES * l + t + 1)
                    for j in range(2):
                        bank = ring_a.open(pe, (l, "h2T", t, j))
                        for k in range(4):
                            ins = nc.tensor.transpose(bank[:, k * P:(k + 1) * P], h2s[:, t % 2, (4 * j + k) * P:(4 * j + k + 1) * P], ident)
                        ins.then_inc(ring_a.full, 1)

                def logits(t):
                    ring_a.wait_empty(pe, (l, "h2T", t, 1))
                    bank = ring_a.open(pe, (l, "logits", t))
                    product(bank[:, 0:EXPERTS], lambda k: h2T[:, k, t * P:(t + 1) * P],
                            lambda k: rw[:, k * EXPERTS:(k + 1) * EXPERTS], DK).then_inc(ring_a.full, 1)

                for t in range(TILES):
                    for j in range(2):
                        bank = ring_v.open(pe, (l, "wo", t, j))
                        product(bank, lambda k: mixT[:, k, t * P:(t + 1) * P], lambda k: wout[:, k, j * 512:(j + 1) * 512], DK).then_inc(ring_v.full, 1)
                    if t >= 1:
                        h2_turn(t - 1)
                    if t >= 2:
                        logits(t - 2)
                h2_turn(TILES - 1)
                logits(TILES - 2)
                logits(TILES - 1)
                for n in range(4):
                    spread(ring_a, (l, "g2", n // 2, n % 2), 16 * l + 12 + n)
                pe.wait_ge(masks_ready, l + 1)
                both, sums_before = r_tmp[:, BOTH_AT:BOTH_AT + 80], r_tmp[:, BOTH_AT + 80:BOTH_AT + 176]
                bank = ring_v.open(pe, (l, "slots"))
                nc.tensor.matmul(bank[:, 0:80], tri, both, start=True, stop=False)
                nc.tensor.matmul(bank[:, 0:80], ones, sums_before[:, 0:80], start=False, stop=True)
                nc.tensor.matmul(bank[:, 80:96], ones, sums_before[:, 80:96], start=True, stop=True).then_inc(ring_v.full, 1)
                pe.wait_ge(table_rhs_ready, l + 1)
                bank = ring_v.open(pe, (l, "table"))
                product(bank[:, 0:2 * NB], lambda j: hot_place[:, j, :], lambda j: table_rhs[:, j, :], TR).then_inc(ring_v.full, 1)

                ring_a.wait_empty(pe, (l, "g2", 1, 1))
                pe.wait_ge(plan_ready, l + 1)
                start = pe.value_load(blocks[l][0:1, EXPERTS:EXPERTS + 1], min_val=0, max_val=100)

                def turn(n):
                    pe.wait_ge(gathered, 16 * n + 16 * (l + 1))
                    for k in range(DK):
                        ins = nc.tensor.transpose(ps[:, k // 4, (k % 4) * P:(k % 4 + 1) * P], xg[:, k * P:(k + 1) * P], ident)
                    ins.then_inc(xT_full, 1)

                turn(start + l)
                with pe.Fori(0, EXPERTS // 2) as i:
                    for s in range(2):
                        first = pe.value_load(blocks[l][0:1, bass.ds(EXPERTS + 2 * i + s, 1)], min_val=0, max_val=100)
                        count = pe.value_load(blocks[l][0:1, bass.ds(2 * i + s, 1)], min_val=1, max_val=5)
                        pe.wait_ge(expert_loaded[s], (i + (EXPERTS // 2 * l + 1)) * 48)
                        pe.sem_inc(pe_passed, 1)
                        with pe.Fori(0, count) as b:
                            g = first + b
                            pe.wait_ge(xT_act, g + l + 1)
                            pe.wait_ge(xT_dve, g + l + 1)
                            product(ps[:, 2], lambda k: xgT[:, k, :], lambda k: wgu[s][:, k, :], DK).then_inc(gu_full, 1)
                            turn(g + l + 1)
                            pe.wait_ge(hid_ready, g + 1)
                            for k in range(2):
                                ins = nc.tensor.transpose(ps[:, 3, k * P:(k + 1) * P], hid[:, k * P:(k + 1) * P], ident)
                            ins.then_inc(hidT_full, 1)
                            pe.wait_ge(hidT_ready, g + 1)
                            pe.wait_ge(y_act, g + 1)
                            pe.wait_ge(y_dve, g + 1)
                            product(ps[:, 4], lambda k: hidT[:, k, :], lambda k: wdn[s][:, k, 0:512], 2)
                            product(ps[:, 5], lambda k: hidT[:, k, :], lambda k: wdn[s][:, k, 512:1024], 2).then_inc(y_full, 1)


BOTH_AT = 80 + 80 + 120 + 20 + 20 + 5 + 20 + 80 + 80 + 5 + 5
_INS = ['x_prompt', 'x_sample', 'cache_ckv', 'cache_krope', 'c', 'c_ctx', 'w_ada', 'b_ada', 'norm1_g', 'w_in',
        'q_norm_g', 'w_uq', 'kv_norm_g', 'w_ukv', 'conv_w', 'conv_b', 'conv_ln_g', 'conv_ln_b', 'w_out',
        'norm2_g', 'router_w', 'router_b', 'w_gate', 'w_up', 'w_down', 'final_g']
_OUTS = [("y_prompt", (1, SEQ, D)), ("y_sample", (1, DEC_SEQ, D)),
         ("new_ckv", (1, DEPTH, SEQ, KV_LORA)), ("new_krope", (1, DEPTH, SEQ, ROPE))]


def kernel(**inputs):
    import concourse.bacc as _bacc
    from concourse.bass_utils import run_bass_kernel_spmd as _run

    nc = _bacc.Bacc("TRN2", target_bir_lowering=False, num_devices=1)
    arrays, args = {}, []
    for name in _INS:
        a = np.ascontiguousarray(inputs[name])
        arrays[f"in_{name}"] = a
        args.append(nc.dram_tensor(f"in_{name}", a.shape, mybir.dt.from_np(a.dtype), kind="ExternalInput").ap())
    a = shape_constants()
    arrays["in_consts"] = a
    args.append(nc.dram_tensor("in_consts", a.shape, FP32, kind="ExternalInput").ap())
    for name, shape in _OUTS:
        args.append(nc.dram_tensor(f"out_{name}", shape, FP32, kind="ExternalOutput").ap())
    hybrid_step_kernel(nc, *args)
    r = _run(nc, [arrays], core_ids=[0])
    return tuple(r.results[0][f"out_{name}"] for name, _ in _OUTS)
```
